# Optimizing a Trainium2 kernel written in Bass

```python
import jax, jax.numpy as jnp
from jax import lax
import numpy as np

D_MODEL = 1024
BATCH = 1
SEQ = 1024
DEPTH = 1

MEM_LEN = 256
EPS = 1e-6
GM_GROUPS = 8
GM_GROUP_DIM = D_MODEL // GM_GROUPS
GM_WIDTH = GM_GROUPS * GM_GROUP_DIM
GM_CHUNK = 128
SSD_INNER = 2 * D_MODEL
SSD_HEAD_DIM = 64
SSD_HEADS = SSD_INNER // SSD_HEAD_DIM
SSD_GROUPS = 4
SSD_HPG = SSD_HEADS // SSD_GROUPS
SSD_STATE = 128
SSD_CONV = 4
SSD_CHUNK = 128
SSD_XBC = SSD_INNER + 2 * SSD_GROUPS * SSD_STATE
X_HEADS = 4
X_HEAD_DIM = D_MODEL // X_HEADS
FFN_DIM = 2816
FFN_CONV = 3
N_BRANCH = 2
IN_SIZES = (GM_WIDTH, GM_WIDTH, SSD_INNER, SSD_XBC, SSD_HEADS, D_MODEL, D_MODEL)
IN_COLS = sum(IN_SIZES)

kernel_name = "hybrid_gmlp_ssd_memxattn_convffn"

def rmsnorm(x, g):
    xf = x.astype(jnp.float32)
    y = xf * lax.rsqrt(jnp.mean(xf * xf, axis=-1, keepdims=True) + EPS)
    return (y * g.astype(jnp.float32)).astype(x.dtype)

def causal_dwconv(x, w, b):
    k_width = w.shape[0]
    s = x.shape[1]
    xp = jnp.pad(x, ((0, 0), (k_width - 1, 0), (0, 0)))
    y = b
    for k in range(k_width):
        y = y + xp[:, k:k + s, :] * w[k]
    return y

def gmlp_branch(u, v, v_gain, w_s, b_s):
    bsz, s, _ = v.shape
    n_chunks = s // GM_CHUNK
    u = jax.nn.gelu(u)
    v = rmsnorm(jax.nn.gelu(v), v_gain)
    vc = v.reshape(bsz, n_chunks, GM_CHUNK, GM_GROUPS, GM_GROUP_DIM)
    mask = jnp.tril(jnp.ones((GM_CHUNK, GM_CHUNK), dtype=w_s.dtype))
    ws = w_s * mask
    mixed = jnp.einsum('gts,bcsgd->bctgd', ws, vc) + b_s.T[None, None, :, :, None]
    return u * mixed.reshape(bsz, s, GM_WIDTH)

def ssd_branch(z, xbc, dt_raw, conv_w, conv_b, dt_bias, a_log, d_skip, norm_g):
    bsz, s, _ = z.shape
    nc, L = s // SSD_CHUNK, SSD_CHUNK
    G, R, P, N = SSD_GROUPS, SSD_HPG, SSD_HEAD_DIM, SSD_STATE
    xbc = jax.nn.silu(causal_dwconv(xbc, conv_w, conv_b))
    xs, bm, cm = jnp.split(xbc, [SSD_INNER, SSD_INNER + G * N], axis=-1)
    dt = jax.nn.softplus(dt_raw.astype(jnp.float32) + dt_bias.astype(jnp.float32))
    a = -jnp.exp(a_log.astype(jnp.float32))
    x = xs.reshape(bsz, nc, L, G, R, P)
    bc = bm.reshape(bsz, nc, L, G, N)
    cc = cm.reshape(bsz, nc, L, G, N)
    dt_c = dt.reshape(bsz, nc, L, G, R)
    xd = x * dt_c[..., None]
    a_cs = jnp.cumsum(jnp.moveaxis((dt * a).reshape(bsz, nc, L, G, R), 2, -1), axis=-1)
    causal = jnp.tril(jnp.ones((L, L), dtype=bool))
    seg = a_cs[..., :, None] - a_cs[..., None, :]
    lmat = jnp.exp(jnp.where(causal, seg, -jnp.inf))
    cb = jnp.einsum('bclgn,bcsgn->bcgls', cc, bc)
    scores = cb[:, :, :, None] * lmat
    y_diag = jnp.einsum('bcgrls,bcsgrp->bclgrp', scores, xd)
    decay = jnp.exp(a_cs[..., -1:] - a_cs)
    states = jnp.einsum('bcsgn,bcgrs,bcsgrp->bcgrpn', bc, decay, xd)
    chunk_decay = jnp.exp(a_cs[..., -1])

    def step(h, inp):
        st, dec = inp
        return h * dec[..., None, None] + st, h

    h0 = jnp.zeros_like(states[:, 0])
    _, prev = lax.scan(step, h0, (jnp.moveaxis(states, 1, 0), jnp.moveaxis(chunk_decay, 1, 0)))
    prev = jnp.moveaxis(prev, 0, 1)
    y_off = jnp.einsum('bclgn,bcgrpn->bclgrp', cc, prev) * jnp.exp(jnp.moveaxis(a_cs, -1, 2))[..., None]
    y = y_diag + y_off + x * d_skip.reshape(G, R)[:, :, None]
    y = y.reshape(bsz, s, SSD_INNER) * jax.nn.silu(z)
    yg = y.reshape(bsz, s, G, SSD_INNER // G)
    yf = yg.astype(jnp.float32)
    yf = yf * lax.rsqrt(jnp.mean(yf * yf, axis=-1, keepdims=True) + EPS)
    return (yf.reshape(bsz, s, SSD_INNER) * norm_g.astype(jnp.float32)).astype(y.dtype)

def mem_cross_attn(h, mem_n, w_q, w_kv, w_o):
    bsz, s, _ = h.shape
    m = mem_n.shape[1]
    q = (h @ w_q).reshape(bsz, s, X_HEADS, X_HEAD_DIM)
    k, v = jnp.split(mem_n @ w_kv, 2, axis=-1)
    k = k.reshape(bsz, m, X_HEADS, X_HEAD_DIM)
    v = v.reshape(bsz, m, X_HEADS, X_HEAD_DIM)
    sc = jnp.einsum('bshd,bmhd->bhsm', q, k).astype(jnp.float32) * (X_HEAD_DIM ** -0.5)
    p = jax.nn.softmax(sc, axis=-1).astype(v.dtype)
    o = jnp.einsum('bhsm,bmhd->bshd', p, v).reshape(bsz, s, D_MODEL)
    return o @ w_o

def conv_ffn(h, w_up, conv_w, conv_b, w_down):
    up = causal_dwconv(h @ w_up, conv_w, conv_b)
    a, b = jnp.split(up, 2, axis=-1)
    return (jax.nn.gelu(a) * b) @ w_down

def setup_inputs(seed: int = 0) -> dict:
    key = jax.random.key(seed)
    ks = iter(jax.random.split(key, 40))

    def nrm(shape, scale):
        return jax.random.normal(next(ks), shape, jnp.float32) * scale

    def gain(width):
        return 1.0 + nrm((DEPTH, width), 0.02)

    dt0 = jnp.exp(jax.random.uniform(next(ks), (DEPTH, SSD_HEADS), jnp.float32,
                                     np.log(1e-3), np.log(1e-1)))
    dt_bias = dt0 + jnp.log(-jnp.expm1(-dt0))
    a_log = jnp.log(jax.random.uniform(next(ks), (DEPTH, SSD_HEADS), jnp.float32, 1.0, 16.0))
    return {
        "x": nrm((BATCH, SEQ, D_MODEL), 1.0),
        "mem": nrm((BATCH, MEM_LEN, D_MODEL), 1.0),
        "norm_pre_mix": gain(D_MODEL),
        "norm_post_mix": gain(D_MODEL),
        "norm_pre_mem": gain(D_MODEL),
        "norm_mem_kv": gain(D_MODEL),
        "norm_post_mem": gain(D_MODEL),
        "norm_pre_ffn": gain(D_MODEL),
        "norm_post_ffn": gain(D_MODEL),
        "w_in": nrm((DEPTH, D_MODEL, IN_COLS), D_MODEL ** -0.5),
        "gm_v_norm": gain(GM_WIDTH),
        "gm_w_s": nrm((DEPTH, GM_GROUPS, GM_CHUNK, GM_CHUNK), GM_CHUNK ** -0.5),
        "gm_b_s": 1.0 + nrm((DEPTH, GM_GROUPS, GM_CHUNK), 0.02),
        "ssd_conv_w": nrm((DEPTH, SSD_CONV, SSD_XBC), SSD_CONV ** -0.5),
        "ssd_conv_b": nrm((DEPTH, SSD_XBC), 0.02),
        "ssd_dt_bias": dt_bias,
        "ssd_a_log": a_log,
        "ssd_d": 1.0 + nrm((DEPTH, SSD_HEADS), 0.02),
        "ssd_norm": gain(SSD_INNER),
        "w_branch_a": nrm((DEPTH, GM_WIDTH, D_MODEL), GM_WIDTH ** -0.5),
        "w_branch_b": nrm((DEPTH, SSD_INNER, D_MODEL), SSD_INNER ** -0.5),
        "w_out": nrm((DEPTH, D_MODEL, D_MODEL), D_MODEL ** -0.5),
        "xa_w_q": nrm((DEPTH, D_MODEL, D_MODEL), D_MODEL ** -0.5),
        "xa_w_kv": nrm((DEPTH, D_MODEL, 2 * D_MODEL), D_MODEL ** -0.5),
        "xa_w_o": nrm((DEPTH, D_MODEL, D_MODEL), D_MODEL ** -0.5),
        "ffn_w_up": nrm((DEPTH, D_MODEL, 2 * FFN_DIM), D_MODEL ** -0.5),
        "ffn_conv_w": nrm((DEPTH, FFN_CONV, 2 * FFN_DIM), FFN_CONV ** -0.5),
        "ffn_conv_b": nrm((DEPTH, 2 * FFN_DIM), 0.02),
        "ffn_w_down": nrm((DEPTH, FFN_DIM, D_MODEL), FFN_DIM ** -0.5),
    }

def reference(x, mem, norm_pre_mix, norm_post_mix, norm_pre_mem, norm_mem_kv, norm_post_mem,
              norm_pre_ffn, norm_post_ffn, w_in, gm_v_norm, gm_w_s, gm_b_s, ssd_conv_w, ssd_conv_b,
              ssd_dt_bias, ssd_a_log, ssd_d, ssd_norm, w_branch_a, w_branch_b, w_out,
              xa_w_q, xa_w_kv, xa_w_o, ffn_w_up, ffn_conv_w, ffn_conv_b, ffn_w_down):
    split_points = [int(i) for i in np.cumsum(IN_SIZES)[:-1]]
    for l in range(DEPTH):
        h = rmsnorm(x, norm_pre_mix[l])
        proj = h @ w_in[l]
        u, v, z, xbc, dt_raw, g_a, g_b = jnp.split(proj, split_points, axis=-1)
        y_a = gmlp_branch(u, v, gm_v_norm[l], gm_w_s[l], gm_b_s[l]) @ w_branch_a[l]
        y_b = ssd_branch(z, xbc, dt_raw, ssd_conv_w[l], ssd_conv_b[l], ssd_dt_bias[l],
                         ssd_a_log[l], ssd_d[l], ssd_norm[l]) @ w_branch_b[l]
        mixed = jax.nn.sigmoid(g_a) * y_a + jax.nn.sigmoid(g_b) * y_b
        x = x + rmsnorm(mixed @ w_out[l], norm_post_mix[l])
        h = rmsnorm(x, norm_pre_mem[l])
        mem_n = rmsnorm(mem, norm_mem_kv[l])
        x = x + rmsnorm(mem_cross_attn(h, mem_n, xa_w_q[l], xa_w_kv[l], xa_w_o[l]), norm_post_mem[l])
        h = rmsnorm(x, norm_pre_ffn[l])
        x = x + rmsnorm(conv_ffn(h, ffn_w_up[l], ffn_conv_w[l], ffn_conv_b[l], ffn_w_down[l]),
                        norm_post_ffn[l])
    return x


_drawn_inputs = setup_inputs


def setup_inputs(seed=0):
    import zlib

    import numpy as np

    out = dict(_drawn_inputs(seed))
    spreads = {}
    factors = {'norm_post_mix': 3.418,
     'norm_pre_mem': 4.312,
     'norm_mem_kv': 3.034,
     'norm_post_mem': 14.077,
     'norm_pre_ffn': 11.217,
     'norm_post_ffn': 24.036,
     'gm_v_norm': 8.0,
     'gm_b_s': 7.257,
     'ssd_conv_b': 3.044,
     'ssd_d': 8.0,
     'ssd_norm': 4.544,
     'ffn_conv_b': 11.099}
    for name, (base, spread) in spreads.items():
        noise = np.random.default_rng([zlib.crc32(name.encode()), seed]).standard_normal(out[name].shape)
        drawn = base * np.exp(spread * noise) if base else spread * noise
        out[name] = __import__('jax').numpy.asarray(drawn.astype(out[name].dtype))
    for name, factor in factors.items():
        out[name] = (out[name] * factor).astype(out[name].dtype)
    return out
```

```python
import concourse.bass as bass
from concourse import mybir
from contextlib import ExitStack


F32 = mybir.dt.float32
F32R = mybir.dt.float32r
ALU = mybir.AluOpType
ACT = mybir.ActivationFunctionType
AX = mybir.AxisListType

P = 128
SEQ = 1024
DM = 1024
KT = DM // P
NT = SEQ // P
HALF = 512
MEM = 256
EPS = 1e-6

GROUPS = 4
HPG = 8
HD = 64
XG = HPG * HD // P
CONV = 4
XBC_TILES = 24
U_OFF, V_OFF, Z_OFF, XBC_OFF = 0, 1024, 2048, 4096
DT_OFF, GA_OFF, GB_OFF = 7168, 7200, 8224
HEADS = 32

FFN_TILES = 22
FFN_CONV = 3
FFN_STEPS = FFN_TILES // 2

XH = 4
XHD = 256

SSD_TILES = 16
W_SSD = 0
W_V = W_SSD + GROUPS * SSD_TILES
W_BRANCH = W_V + 8
W_OUT = W_BRANCH + 24
W_K = W_OUT + 8
W_VM = W_K + 8
W_Q = W_VM + 8
W_O = W_Q + 8
W_FFN = W_O + 8
FFN_W = 6

NORM_TILES = [8, 2, 8, 8]
NORM_T0 = [0, 8, 10, 18]
NORM_H0 = [0, 2, 3, 5]
NORM_G0 = [0, 16, 24, 40]
PRE_X, PRE_MEM_TOK, PRE_MEM, PRE_FFN = range(4)


def trunk(nc, a, out):
    ctx = ExitStack()

    def dram(name, shape):
        return nc.dram_tensor(name, shape, F32, kind="Internal").ap()

    gates_dram = dram("gates_scratch", (24, P, SEQ))
    ssd_dram = dram("ssd_scratch", (16, P, SEQ))

    with ctx:
        def sb(name, shape, dt=F32, c=ctx):
            return c.enter_context(nc.sbuf_tensor(name, shape, dt))

        def sem(name):
            return ctx.enter_context(nc.semaphore(name))

        act_hi = sb("act_hi", [P, KT, SEQ], F32R)
        act_lo = sb("act_lo", [P, KT, SEQ], F32R)
        w_raw = sb("w_raw", [P, 2, 1024])
        w_hi = sb("w_hi", [P, 2, 1024], F32R)
        w_lo = sb("w_lo", [P, 2, 1024], F32R)
        ident = sb("ident", [P, P])
        tri = sb("tri", [P, P])
        after = sb("after", [P, P])
        consts = sb("consts", [P, 4, P])
        stat = sb("stat", [P, 8])
        stat_v = sb("stat_v", [P, 8])
        stat_r = sb("stat_r", [P, 8])
        stat_s = sb("stat_s", [P, 8])
        ffn_conv_c = None

        ssd = ExitStack()
        ws_t = None
        keep = ExitStack()
        ws_t = sb("ws_t", [P, 8, P], c=keep)
        base = ExitStack()
        after_r = sb("after_r", [P, P], F32R, base)
        ones = sb("ones", [P, P], c=base)
        dt = sb("dt", [P, NT, HEADS], c=base)
        dA = sb("dA", [P, NT, HEADS], c=base)
        dA_hi = sb("dA_hi", [P, NT, HEADS], F32R, base)
        dA_lo = sb("dA_lo", [P, NT, HEADS], c=base)
        d_skip = sb("d_skip", [P, HEADS], c=base)

        setup = ExitStack()
        x_tok = sb("x_tok", [P, NT, DM], c=setup)
        rows = sb("rows", [P, 4, P], c=setup)
        ws_rows = sb("ws_rows", [P, 8, P], c=setup)
        junk = sb("junk", [P, DM], c=setup)
        dtw = sb("dtw", [P, KT, HEADS], c=setup)
        dtw_hi = sb("dtw_hi", [P, KT, HEADS], F32R, setup)
        dtw_lo = sb("dtw_lo", [P, KT, HEADS], F32R, setup)
        dt_bias = sb("dt_bias", [P, HEADS], c=setup)
        a_log = sb("a_log", [P, HEADS], c=setup)
        dt_x = sb("dt_x", [P, NT, HEADS], c=setup)
        dt_abs = sb("dt_abs", [P, NT, HEADS], c=setup)
        dt_e = sb("dt_e", [P, NT, HEADS], c=setup)
        dt_d = sb("dt_d", [P, NT, HEADS], c=setup)
        dt_r = sb("dt_r", [P, NT, HEADS], c=setup)
        dt_s = sb("dt_s", [P, NT, HEADS], c=setup)
        dt_q = sb("dt_q", [P, NT, HEADS], c=setup)
        dt_p = sb("dt_p", [P, NT, HEADS], c=setup)
        neg_a = sb("neg_a", [P, HEADS], c=setup)
        setup.close()

        xs = sb("xs", [P, NT, HALF], c=ssd)
        zs = sb("zs", [P, NT, HALF], c=ssd)
        b_t = sb("b_t", [P, SEQ], c=ssd)
        c_t = sb("c_t", [P, SEQ], c=ssd)
        b_tok = sb("b_tok", [P, NT, P], c=ssd)
        xbc_raw = sb("xbc_raw", [P, 2, CONV - 1 + SEQ], c=ssd)
        conv = sb("conv", [P, SEQ], c=ssd)
        gate_out = sb("gate_out", [P, 2, HALF], c=ssd)
        tri_hi = sb("tri_hi", [P, 2, HALF], F32R, ssd)
        tri_lo = sb("tri_lo", [P, 2, HALF], F32R, ssd)
        scores = sb("scores", [P, 2, HALF], c=ssd)
        cb_m = sb("cb_m", [P, P], c=ssd)
        xd = sb("xd", [P, 2, HALF], c=ssd)
        xdd = sb("xdd", [P, HALF], c=ssd)
        state = sb("state", [P, HALF], c=ssd)
        y_sum = sb("y_sum", [P, HALF], c=ssd)
        sq_junk = sb("sq_junk", [P, HALF], c=ssd)
        y_t = sb("y_t", [P, 2, XG, P], c=ssd)
        g_conv = sb("g_conv", [P, CONV + 1, XG + 2], c=ssd)
        g_dt = sb("g_dt", [P, NT, HPG], c=ssd)
        g_hi = sb("g_hi", [P, NT, HPG], c=ssd)
        g_lo = sb("g_lo", [P, NT, HPG], c=ssd)
        g_dA = sb("g_dA", [P, NT, HPG], c=ssd)
        decays = sb("decays", [P, 3, NT, HPG], c=ssd)
        g_in, g_out, g_chunk = (decays[:, i, :, :] for i in range(3))
        g_skip = sb("g_skip", [P, HPG], c=ssd)
        g_gain = sb("g_gain", [P, XG], c=ssd)
        ssd.close()
        base.close()

        mixp = ExitStack()
        r2 = sb("r2", [P, NT, DM], c=mixp)
        r1 = sb("r1", [P, NT, DM], c=mixp)
        bs_bc = sb("bs_bc", [P, 8, P], c=mixp)
        g_tmp = sb("g_tmp", [P, 2, HALF], c=mixp)
        y_in = sb("y_in", [P, 2, SEQ], c=mixp)
        junk2 = sb("junk2", [P, DM], c=mixp)
        mixp.close()
        keep.close()

        later = ExitStack()
        pad = sb("ws_t_place", [P, 8, P], c=later)
        r2_ = sb("r2_place", [P, NT, DM], c=later)
        r1_ = sb("r1_place", [P, NT, DM], c=later)
        kv = ExitStack()
        k_t = sb("k_t", [P, 8, MEM], c=kv)
        v_tok = sb("v_tok", [P, 2, DM], c=kv)
        memp = ExitStack()
        mem_tok = sb("mem_tok", [P, 2, DM], c=memp)
        mem_hi = sb("mem_hi", [P, KT, MEM], F32R, memp)
        mem_lo = sb("mem_lo", [P, KT, MEM], F32R, memp)
        post_gain = sb("post_gain", [P, DM], c=memp)
        junk3 = sb("junk3", [P, DM], c=memp)
        memp.close()
        att = ExitStack()
        q_t = sb("q_t", [P, 2, SEQ], c=att)
        prob = sb("prob", [P, NT, MEM], c=att)
        prob_t = sb("prob_t", [P, 2, SEQ], c=att)
        a_max = sb("a_max", [P, 8], c=att)
        a_nm = sb("a_nm", [P, 8], c=att)
        a_sum = sb("a_sum", [P, 8], c=att)
        a_rec = sb("a_rec", [P, 8], c=att)
        att.close()
        post2 = ExitStack()
        post_gain2 = sb("post_gain2", [P, DM], c=post2)
        junk4 = sb("junk4", [P, DM], c=post2)
        post2.close()
        kv.close()
        ffn = ExitStack()
        up_raw = sb("up_raw", [P, 2, FFN_CONV - 1 + SEQ], c=ffn)
        up_a = sb("up_a", [P, SEQ], c=ffn)
        up_b = sb("up_b", [P, SEQ], c=ffn)
        f_hi = sb("f_hi", [P, 2, SEQ], F32R, ffn)
        f_lo = sb("f_lo", [P, 2, SEQ], F32R, ffn)
        ffn.close()
        post3 = ExitStack()
        post_gain3 = sb("post_gain3", [P, DM], c=post3)
        junk5 = sb("junk5", [P, DM], c=post3)
        post3.close()
        later.close()

        bank = [ctx.enter_context(nc.psum_tensor(f"bank{i}", [P, HALF], F32)) for i in range(8)]

        w_in = [sem(f"w_in{i}") for i in range(2)]
        w_hi_done = sem("w_hi_done")
        w_split = sem("w_split")
        w_begun = sem("w_begun")
        sp_held = sem("sp_held")
        held = sem("held")
        masks = sem("masks")
        rows_in, x_in, ws_in, dt_in = sem("rows_in"), sem("x_in"), sem("ws_in"), sem("dt_in")
        c_tr, c_ev = sem("c_tr"), sem("c_ev")
        n_sq, n_var, n_rt, n_xs = sem("n_sq"), sem("n_var"), sem("n_rt"), sem("n_xs")
        n_tr, n_hi, n_lo = sem("n_tr"), sem("n_hi"), sem("n_lo")
        dt_w, dt_mm, dt_dve, dt_act, dt_cum, dt_exp = [sem(f"dt_{n}") for n in ("w", "mm", "dve", "act", "cum", "exp")]
        z_mm, z_ev, t_mm, t_ev, cv, sl, xt, xe = [sem(n) for n in ("z_mm", "z_ev", "t_mm", "t_ev", "cv", "sl", "xt", "xe")]
        g_mm, g_ev = sem("g_mm"), sem("g_ev")
        g_st = [sem(f"g_st{i}") for i in range(2)]
        y_st = [sem(f"y_st{i}") for i in range(2)]
        gc = sem("group_consts")
        xd_s, sk, rh, seg, ex, cb, sc, xdd_s = [sem(n) for n in ("xd_done", "skip_done", "rh", "seg", "ex", "cb", "sc", "xdd_done")]
        yd, yo, st, pv, yy, sq, ysv, ysr, ys, yt, ye = [sem(n) for n in ("yd", "yo", "st", "pv", "yy", "sq", "ysv", "ysr", "ys", "yt", "ye")]
        v_mm, v_ev, v_sq, v_var, v_rt, v_sc = [sem(n) for n in ("v_mm", "v_ev", "v_sq", "v_var", "v_rt", "v_sc")]
        slot_in = [sem(f"slot_in{i}") for i in range(8)]
        m_mm, m_ev, m_hi, m_lo = [sem(n) for n in ("m_mm", "m_ev", "m_hi", "m_lo")]
        bs_in = sem("bs_in")
        b_mm, b_ev, b_hi, b_lo = [sem(n) for n in ("b_mm", "b_ev", "b_hi", "b_lo")]
        y_ld = [sem(f"y_ld{i}") for i in range(2)]
        s_hi, s_lo = sem("s_hi"), sem("s_lo")
        o_mm, o_ev, o_sq, o_var, o_rt, o_y, o_x = [sem(n) for n in ("o_mm", "o_ev", "o_sq", "o_var", "o_rt", "o_y", "o_x")]
        gain_in, xr_in, mem_in = sem("gain_in"), sem("xr_in"), sem("mem_in")
        k_mm, k_ev = sem("k_mm"), sem("k_ev")
        q_mm, q_ev, s_mm, a_mx, a_ex, a_pn, a_tr, a_te, p_mm, p_ev = [sem(n) for n in ("q_mm", "q_ev", "s_mm", "a_mx", "a_ex", "a_pn", "a_tr", "a_te", "p_mm", "p_ev")]
        f_mm, f_ev, f_cv, f_gl, f_h, f_l, d_mm, d_ad = [sem(n) for n in ("f_mm", "f_ev", "f_cv", "f_gl", "f_h", "f_l", "d_mm", "d_ad")]
        out_st = sem("out_st")

        LEAD = 1
        Y_LEAD = LEAD + NT

        def nth(g, per, k):
            return g * per + (k + LEAD)

        def yth(g, k):
            return g * NT + (k + Y_LEAD)

        LAST = GROUPS - 1
        GC = 9

        def bc(ap, shape):
            return ap.unsqueeze(2).to_broadcast(shape)

        def wcols(slot, k):
            return w_hi[:, slot, k * P:(k + 1) * P], w_lo[:, slot, k * P:(k + 1) * P]

        def channels_half(slot, half, bk, first_inc, hi=act_hi, lo=act_lo, n=HALF, before=None):
            for kt in range(KT):
                if before:
                    before(kt)
                wh, wl = wcols(slot, kt)
                ah, al = (t[:, kt, half * n:(half + 1) * n] for t in (hi, lo))
                for i, (w, x) in enumerate(((wh, ah), (wh, al), (wl, ah))):
                    m = nc.tensor.matmul(bank[bk][:, 0:n], w, x, start=kt == 0 and i == 0,
                                         stop=kt == KT - 1 and i == 2)
                    if first_inc and kt == 0 and i == 0:
                        m.then_inc(w_begun, 1)
            return m

        def tokens_tile(slot, part, done, tiles=NT, hi=act_hi, lo=act_lo, free=None, bk0=0, ready=None):
            for kk in range(2):
                kt = 2 * part + kk
                wh, wl = (w[:, slot, kk * HALF:(kk + 1) * HALF] for w in (w_hi, w_lo))
                if ready:
                    ready(kt)
                for t in range(tiles):
                    if kt == 0 and free:
                        free(t)
                    ah, al = (x[:, kt, t * P:(t + 1) * P] for x in (hi, lo))
                    for i, (x, w) in enumerate(((ah, wh), (ah, wl), (al, wh))):
                        m = nc.tensor.matmul(bank[bk0 + t][:, :], x, w, start=kt == 0 and i == 0,
                                             stop=kt == KT - 1 and i == 2)
                        if kk == 0 and t == 0 and i == 0:
                            m.then_inc(w_begun, 1)
                    if kt == KT - 1:
                        m.then_inc(done, 1)

        block = ctx.enter_context(nc.Block())

        @block.sync
        def _(sp):
            x_v = a["x"][0].rearrange("(t p) d -> p t d", p=P)
            for h in range(2):
                sp.dma_start(x_tok[:, 4 * h:4 * h + 4, :], x_v[:, 4 * h:4 * h + 4, :]).then_inc(x_in, 16)
            sp.dma_start(dtw[:, :, :], a["w_in"][0, :, DT_OFF:DT_OFF + HEADS].rearrange("(k p) c -> p k c", p=P)).then_inc(dt_in, 16)

            def load(i, slot, src, dst=None):
                if not (isinstance(i, int) and i < 2):
                    sp.wait_ge(w_split, i - 1)
                if not isinstance(i, int):
                    sp.sem_inc(sp_held, 1)
                sp.dma_start(w_raw[:, slot, :] if dst is None else dst, src).then_inc(w_in[slot], 16)

            def channel_tile(w, col):
                return w[:, bass.ds(col, P)].rearrange("(k p) c -> p k c", p=P)

            def token_tile(w, part, col):
                return w[2 * part * P:2 * (part + 1) * P, bass.ds(col, HALF)].rearrange("(k p) c -> p k c", p=P)

            def raw(slot, k):
                return w_raw[:, slot, :].rearrange("p (k c) -> p k c", k=k)

            win = a["w_in"][0]

            def ssd_cols(g):
                cols = [XBC_OFF + g * HALF + P * j for j in range(XG)]
                cols += [XBC_OFF + 2048 + g * P, XBC_OFF + 2560 + g * P]
                return cols + [off + g * 2 * P + P * j for off in (GA_OFF, GB_OFF, U_OFF) for j in range(2)]

            def ssd_loads(g, start=0):
                for j in range(start, SSD_TILES):
                    i = g * SSD_TILES + j
                    if j < 4:
                        load(i, j % 2, token_tile(win, j, Z_OFF + g * HALF), raw(j % 2, 2))
                    else:
                        load(i, j % 2, channel_tile(win, ssd_cols(g)[j - 4]), raw(j % 2, KT))

            ssd_loads(0)
            with sp.Fori(1, GROUPS) as g:
                ssd_loads(g)

            def token_loads(i0, w, col0=0):
                for n in range(2):
                    for part in range(4):
                        load(i0 + 4 * n + part, part % 2, token_tile(w, part, col0 + n * HALF), raw(part % 2, 2))

            def channel_loads(i0, w):
                for j in range(8):
                    load(i0 + j, j % 2, channel_tile(w, j * P), raw(j % 2, KT))

            token_loads(W_V, win, V_OFF)
            channel_loads(W_BRANCH, a["w_branch_a"][0])
            channel_loads(W_BRANCH + 8, a["w_branch_b"][0, 0:DM, :])
            channel_loads(W_BRANCH + 16, a["w_branch_b"][0, DM:2 * DM, :])
            token_loads(W_OUT, a["w_out"][0])
            channel_loads(W_K, a["xa_w_kv"][0, :, 0:DM])
            token_loads(W_VM, a["xa_w_kv"][0], DM)
            channel_loads(W_Q, a["xa_w_q"][0])
            token_loads(W_O, a["xa_w_o"][0])

            up, down = a["ffn_w_up"][0], a["ffn_w_down"][0]

            def up_loads(i, step, pair):
                col = step * 2 * P + pair * P
                load(i, 0, channel_tile(up, col), raw(0, KT))
                load(i + 1, 1, channel_tile(up, col + FFN_TILES * P), raw(1, KT))

            def down_loads(i, step):
                rows_v = down[bass.ds(step * 2 * P, 2 * P), :].rearrange("(k p) c -> p k c", p=P)
                for n in range(2):
                    load(i + n, n, rows_v[:, :, n * HALF:(n + 1) * HALF], raw(n, 2))

            up_loads(W_FFN, 0, 0)
            up_loads(W_FFN + 2, 0, 1)
            with sp.Fori(1, FFN_STEPS) as s:
                i = s * FFN_W + (W_FFN - 2)
                up_loads(i, s, 0)
                down_loads(i + 2, s - 1)
                up_loads(i + 4, s, 1)
            down_loads(W_FFN + 4 + (FFN_STEPS - 1) * FFN_W, FFN_STEPS - 1)

            out_v = out[0].rearrange("(t p) d -> p t d", p=P)
            for t in range(NT):
                sp.wait_ge(o_x, 16 + t + 1)
                sp.dma_start(out_v[:, t, :], r1[:, t, :]).then_inc(out_st, 16)
            sp.wait_ge(out_st, 16 * NT)

        @block.gpsimd
        def _(pool):
            nc.gpsimd.memset(ident[:, :], 0.0).then_inc(masks, 1)
            nc.gpsimd.memset(tri[:, :], 1.0).then_inc(masks, 1)
            nc.gpsimd.memset(after[:, :], 1.0).then_inc(masks, 1)
            nc.gpsimd.memset(ones[:, :], 1.0).then_inc(masks, 1)
            pool.wait_ge(masks, 4)
            nc.gpsimd.affine_select(out=ident[:, :], in_=ident[:, :], compare_op=ALU.not_equal, fill=1.0,
                                    base=0, pattern=[[-1, P]], channel_multiplier=1).then_inc(masks, 1)
            nc.gpsimd.affine_select(out=tri[:, :], in_=tri[:, :], compare_op=ALU.is_ge, fill=0.0,
                                    base=0, pattern=[[1, P]], channel_multiplier=-1).then_inc(masks, 1)
            nc.gpsimd.affine_select(out=after[:, :], in_=after[:, :], compare_op=ALU.is_gt, fill=0.0,
                                    base=0, pattern=[[-1, P]], channel_multiplier=1).then_inc(masks, 1)

            pool.sem_inc(rh, LEAD)

            def split(i, slot, loads):
                pool.wait_ge(w_begun, i + LEAD)
                pool.wait_ge(w_in[slot], loads * 16)
                if not isinstance(i, int):
                    pool.sem_inc(held, 1)
                nc.gpsimd.tensor_scalar(w_hi[:, slot, :], w_raw[:, slot, :], 1.0, 1.0, ALU.mult, ALU.mult).then_inc(w_hi_done, 1)
                pool.wait_ge(w_hi_done, i + 1)
                nc.gpsimd.tensor_tensor(w_lo[:, slot, :], w_raw[:, slot, :], w_hi[:, slot, :].bitcast(F32),
                                        ALU.subtract).then_inc(w_split, 1)

            def triangle(g, c):
                for h in range(2):
                    if c:
                        pool.wait_ge(seg, g * 16 + (2 * (c - 1) + h + 1))
                    else:
                        pool.wait_ge(gc, nth(g, GC, GC))
                    for dst, src in ((tri_hi, g_hi), (tri_lo, g_lo)):
                        nc.gpsimd.tensor_tensor(dst[:, h, :].rearrange("p (r l) -> p r l", l=P),
                                                bc(src[:, c, 4 * h:4 * h + 4], [P, 4, P]),
                                                tri[:, :].unsqueeze(1).to_broadcast([P, 4, P]), ALU.mult).then_inc(rh, 1)

            with pool.Fori(0, GROUPS) as g:
                def ssd_split(j):
                    split(g * SSD_TILES + j, j % 2, g * (SSD_TILES // 2) + (j // 2 + 1))
                for j in range(11):
                    ssd_split(j)
                triangle(g, 0)
                ssd_split(11)
                triangle(g, 1)
                ssd_split(12)
                triangle(g, 2)
                triangle(g, 3)
                ssd_split(13)
                triangle(g, 4)
                triangle(g, 5)
                ssd_split(14)
                triangle(g, 6)
                triangle(g, 7)
                ssd_split(15)

            def splits(i0, i1):
                with pool.Fori(i0 // 2, i1 // 2) as j:
                    for s in range(2):
                        split(j * 2 + s, s, j + 1)
            splits(W_V, W_FFN + FFN_STEPS * FFN_W)

        @block.tensor
        def _(pe):
            pe.sem_inc(yd, LEAD)
            pe.sem_inc(w_begun, LEAD)
            pe.wait_ge(masks, 7)
            pe.wait_ge(rows_in, 16 * ROW_LOADS)
            for r, n in enumerate(ROW_COUNTS):
                m = nc.tensor.transpose(bank[0][:, r * P:r * P + n], rows[0:n, r, :], ident[0:n, 0:n])
            m.then_inc(c_tr, 1)
            pe.wait_ge(ws_in, 16)
            for h in range(2):
                for i in range(4):
                    m = nc.tensor.transpose(bank[1 + h][:, i * P:(i + 1) * P], ws_rows[:, 4 * h + i, :], ident[:, :])
                m.then_inc(c_tr, 1)

            def norm_transposes(u, src, free=None):
                tiles = NORM_TILES[u]
                per = min(4, tiles)
                for h in range(tiles // per):
                    pe.wait_ge(n_xs, NORM_T0[u] + per * (h + 1))
                    for kt in range(KT):
                        q = h * KT + kt
                        if q >= 8:
                            pe.wait_ge(n_lo, NORM_G0[u] + q - 7)
                        elif free:
                            free(q)
                        for i in range(per):
                            m = nc.tensor.transpose(bank[q % 8][:, i * P:(i + 1) * P],
                                                    src[:, h * per + i, kt * P:(kt + 1) * P], ident[:, :])
                        m.then_inc(n_tr, 1)

            pe.wait_ge(c_ev, 6)
            norm_transposes(PRE_X, x_tok)

            pe.wait_ge(n_lo, NORM_G0[1])
            pe.wait_ge(dt_w, 2)
            for t in range(NT):
                for kt in range(KT):
                    ah, al = (x[:, kt, t * P:(t + 1) * P] for x in (act_hi, act_lo))
                    for i, (x, w) in enumerate(((ah, dtw_hi), (ah, dtw_lo), (al, dtw_hi))):
                        m = nc.tensor.matmul(bank[0][:, t * HEADS:(t + 1) * HEADS], x, w[:, kt, :],
                                             start=kt == 0 and i == 0, stop=kt == KT - 1 and i == 2)
            m.then_inc(dt_mm, 1)

            def seg_and_cb(g, c):
                for h in range(2):
                    pe.wait_ge(rh, nth(g, 32, 4 * c + 2 * h + 2))
                    pe.wait_ge(ex, nth(g, 16, 2 * c + h - 1 if c else 0))
                    for i, t in enumerate((tri_hi, tri_lo)):
                        m = nc.tensor.matmul(bank[4 + h][:, :], after_r[:, :], t[:, h, :], start=i == 0, stop=i == 1)
                    m.then_inc(seg, 1)
                pe.wait_ge(sc, nth(g, 24, 3 * c - 2 if c else 0))
                nc.tensor.matmul(bank[3][:, 0:P], b_t[:, c * P:(c + 1) * P], c_t[:, c * P:(c + 1) * P],
                                 start=True, stop=True).then_inc(cb, 1)

            def chunk_products(g, c):
                pe.wait_ge(sc, nth(g, 24, 3 * c + 3))
                pe.wait_ge(xd_s, nth(g, 8, c + 1))
                pe.wait_ge(yy, nth(g, 32, 4 * c - 2 if c else 0))
                for r in range(HPG):
                    m = nc.tensor.matmul(bank[6][:, r * HD:(r + 1) * HD],
                                         scores[:, r // 4, (r % 4) * P:(r % 4 + 1) * P],
                                         xd[:, c % 2, r * HD:(r + 1) * HD], start=True, stop=True)
                m.then_inc(yd, 1)
                pe.wait_ge(pv, nth(g, 17, 2 * c + 1))
                nc.tensor.matmul(bank[7][:, :], c_t[:, c * P:(c + 1) * P], state[:, :],
                                 start=True, stop=True).then_inc(yo, 1)
                pe.wait_ge(xdd_s, nth(g, 8, c + 1))
                nc.tensor.matmul(bank[2][:, :], b_tok[:, c, :], xdd[:, :], start=True, stop=True).then_inc(st, 1)

            def gate_half(g, q):
                j = 10 + q // 2
                if q % 2 == 0:
                    pe.wait_ge(w_split, g * SSD_TILES + (j + 1))
                if q < 2:
                    pe.wait_ge(t_ev, nth(g, 12, 9 + q))
                else:
                    pe.wait_ge(g_ev, nth(g, 12, q - 1))
                channels_half(j % 2, q % 2, q % 2, q % 2 == 0).then_inc(g_mm, 1)

            def to_tokens(g, idx):
                pe.wait_ge(sl, nth(g, 6, idx + 1))
                for h in range(2):
                    q = 2 * idx + h
                    pe.wait_ge(xe, nth(g, 10, max(0, q - 3)))
                    for i in range(4):
                        c = 4 * h + i
                        src = b_t if idx == XG else conv
                        m = nc.tensor.transpose(bank[4 + q % 4][:, i * P:(i + 1) * P], src[:, c * P:(c + 1) * P], ident[:, :])
                    m.then_inc(xt, 1)

            def ssd_group(g):
                def z_free(t):
                    pe.wait_ge(ye, yth(g, t + 1) - NT)
                for part in range(4):
                    pe.wait_ge(w_split, g * SSD_TILES + (part + 1))
                    tokens_tile(part % 2, part, z_mm, free=z_free)
                for idx in range(6):
                    pe.wait_ge(w_split, g * SSD_TILES + (4 + idx + 1))
                    for h in range(2):
                        b = 2 * (idx % 2) + h
                        if idx < 2:
                            pe.wait_ge(z_ev, nth(g, 8, b + 1))
                        else:
                            pe.wait_ge(t_ev, nth(g, 12, 2 * (idx - 2) + h + 1))
                        channels_half(idx % 2, h, b, h == 0).then_inc(t_mm, 1)
                    if idx == 0:
                        pe.wait_ge(z_ev, nth(g, 8, 8))
                        pe.wait_ge(gc, nth(g, GC, GC))
                        for i, mask in enumerate((tri, after, ones)):
                            m = nc.tensor.matmul(bank[7][:, i * NT * HPG:(i + 1) * NT * HPG], mask[:, :],
                                                 g_dA[:, :, :].rearrange("p c h -> p (c h)"), start=True, stop=True)
                        m.then_inc(dt_cum, 1)
                    if idx == 2:
                        pe.wait_ge(dt_exp, g + 1)
                    if idx >= 1:
                        to_tokens(g, idx - 1)
                for q in range(2):
                    gate_half(g, q)
                pe.wait_ge(xe, nth(g, 10, 10))
                pe.wait_ge(t_ev, nth(g, 12, 12))
                pe.wait_ge(sl, nth(g, 6, 6))
                seg_and_cb(g, 0)
                for c in range(NT):
                    gate_half(g, c + 2)
                    chunk_products(g, c)
                    if c + 1 < NT:
                        seg_and_cb(g, c + 1)
                for q in range(NT + 2, 12):
                    gate_half(g, q)
                for c in range(NT):
                    pe.wait_ge(ys, nth(g, 8, c + 1))
                    if c < 2:
                        pe.wait_ge(g_ev, nth(g, 12, 11 + c))
                    for i in range(XG):
                        m = nc.tensor.transpose(bank[c][:, i * P:(i + 1) * P], xs[:, c, i * P:(i + 1) * P], ident[:, :])
                    m.then_inc(yt, 1)

            pe.wait_ge(dt_dve, 1)
            with pe.Fori(0, GROUPS) as g:
                ssd_group(g)

            for n in range(2):
                def v_free(t, n=n):
                    if n:
                        pe.wait_ge(v_ev, t + 1)
                    else:
                        pe.wait_ge(ye, yth(LAST, t + 1))
                for part in range(4):
                    pe.wait_ge(w_split, W_V + 4 * n + part + 1)
                    tokens_tile(part % 2, part, v_mm, free=v_free)
            pe.wait_ge(v_sc, 8)
            for q in range(16):
                if q >= 8:
                    pe.wait_ge(m_ev, 2 * (q - 8) + 1)
                for i in range(4):
                    c = 4 * (q % 2) + i
                    m = nc.tensor.matmul(bank[q % 8][:, i * P:(i + 1) * P],
                                         r1[:, c, (q // 2) * P:(q // 2 + 1) * P], ws_t[:, q // 2, :],
                                         start=True, stop=True)
                m.then_inc(m_mm, 1)

            for part in range(3):
                for j in range(8):
                    pe.wait_ge(w_split, W_BRANCH + 8 * part + j + 1)
                    for h in range(2):
                        r = 16 * part + 2 * j + h
                        b = r % 8
                        if part == 0:
                            pe.wait_ge(m_ev, 2 * (8 + b) + 1)
                            if j >= 4:
                                pe.wait_ge(b_ev, r - 7)
                        elif r < 24:
                            pe.wait_ge(b_ev, r - 7)
                        else:
                            pe.wait_ge(b_ev, 16 + 2 * (r - 8 - 16) + 1)

                        def ready(kt, part=part, j=j, h=h):
                            if j == 0 and part == 0:
                                pe.wait_ge(m_lo, 2 * kt + h + 1)
                            elif j == 0 and h == 0:
                                pe.wait_ge(b_lo, 8 * (part - 1) + kt + 1)
                        channels_half(j % 2, h, b, h == 0, before=ready).then_inc(b_mm, 1)

            def out_product(u, i0, free0, between=None):
                for n in range(2):
                    def free(t, n=n):
                        if n and not between:
                            pe.wait_ge(o_ev, 16 * u + t + 1)
                        elif n:
                            pe.wait_ge(n_lo, NORM_G0[PRE_MEM_TOK] + t + 1)
                        else:
                            free0(t)

                    def ready(kt, n=n):
                        if n == 0:
                            pe.wait_ge(s_lo, 8 * u + kt + 1)
                    for part in range(4):
                        pe.wait_ge(w_split, i0 + 4 * n + part + 1)
                        tokens_tile(part % 2, part, o_mm, free=free, ready=ready)
                    if n == 0 and between:
                        between()

            def mem_free(q):
                pe.wait_ge(o_ev, q + 1)
            out_product(0, W_OUT, lambda t: pe.wait_ge(b_ev, 16 + 64),
                        lambda: norm_transposes(PRE_MEM_TOK, mem_tok, mem_free))

            for j in range(8):
                pe.wait_ge(w_split, W_K + j + 1)
                pe.wait_ge(o_ev, 8 + j + 1)
                channels_half(j % 2, 0, j, True, mem_hi, mem_lo, MEM).then_inc(k_mm, 1)
            for n in range(2):
                for part in range(4):
                    pe.wait_ge(w_split, W_VM + 4 * n + part + 1)
                    tokens_tile(part % 2, part, k_mm, 2, mem_hi, mem_lo,
                                free=lambda t, n=n: pe.wait_ge(k_ev, 2 * n + t + 1), bk0=2 * n)
            pe.wait_ge(k_ev, 12)
            norm_transposes(PRE_MEM, r2)

            def queries(h):
                for d in range(2):
                    pe.wait_ge(w_split, W_Q + 2 * h + d + 1)
                    for half in range(2):
                        r = 4 * h + 2 * d + half
                        if h:
                            pe.wait_ge(q_ev, r - 3)

                        channels_half(d, half, 2 * d + half, half == 0).then_inc(q_mm, 1)

            pe.wait_ge(n_lo, NORM_G0[PRE_FFN])
            queries(0)
            for h in range(XH):
                pe.wait_ge(q_ev, 4 * h + 4)
                for t in range(NT):
                    b = 4 + t // 2
                    if h and t % 2 == 0:
                        pe.wait_ge(p_ev, 4 * (h - 1) + t // 2 + 1)
                    for d in range(2):
                        m = nc.tensor.matmul(bank[b][:, (t % 2) * MEM:(t % 2 + 1) * MEM], q_t[:, d, t * P:(t + 1) * P],
                                             k_t[:, 2 * h + d, :], start=d == 0, stop=d == 1)
                    if t % 2:
                        m.then_inc(s_mm, 1)
                if h + 1 < XH:
                    queries(h + 1)
                pe.wait_ge(a_pn, 9 * h + 9)
                for q in range(4):
                    for i in range(4):
                        t = 4 * (q % 2) + i
                        m = nc.tensor.transpose(bank[4 + q][:, i * P:(i + 1) * P],
                                                prob[:, t, (q // 2) * P:(q // 2 + 1) * P], ident[:, :])
                    m.then_inc(a_tr, 1)
                pe.wait_ge(a_te, 4 * h + 4)
                for q in range(4):
                    d, half = q // 2, q % 2
                    for mt in range(2):
                        m = nc.tensor.matmul(bank[4 + q][:, :], v_tok[:, mt, h * XHD + d * P:h * XHD + (d + 1) * P],
                                             prob_t[:, mt, half * HALF:(half + 1) * HALF], start=mt == 0, stop=mt == 1)
                    m.then_inc(p_mm, 1)
            out_product(1, W_O, lambda t: pe.wait_ge(p_ev, 16) if t >= 4 else pe.wait_ge(q_ev, 16))
            norm_transposes(PRE_FFN, r2, lambda q: pe.wait_ge(o_ev, 32))
            pe.wait_ge(n_lo, NORM_G0[PRE_FFN] + 16)

            def up_products(i, u, first=False):
                for w in range(2):
                    pe.wait_ge(w_split, i + (w + 1))
                    for half in range(2):
                        b = 2 * w + half
                        if not first:
                            pe.wait_ge(f_ev, u * 4 + (b - 3))
                        channels_half(w, half, b, half == 0).then_inc(f_mm, 1)

            def down_products(i, step):
                pe.wait_ge(f_l, step * 2 + 2)
                for n in range(2):
                    pe.wait_ge(w_split, i + (n + 1))
                    for t in range(NT):
                        r = 8 * n + t
                        pe.wait_ge(d_ad, step * 16 + (r + 1))
                        for k in range(2):
                            fh, fl = (x[:, k, t * P:(t + 1) * P] for x in (f_hi, f_lo))
                            wh, wl = (w[:, n, k * HALF:(k + 1) * HALF] for w in (w_hi, w_lo))
                            for j, (x, w) in enumerate(((fh, wh), (fh, wl), (fl, wh))):
                                m = nc.tensor.matmul(bank[4 + r % 4][:, :], x, w, start=k == 0 and j == 0,
                                                     stop=k == 1 and j == 2)
                                if t == 0 and k == 0 and j == 0:
                                    m.then_inc(w_begun, 1)
                        m.then_inc(d_mm, 1)

            up_products(W_FFN, 0, True)
            up_products(W_FFN + 2, 1)
            with pe.Fori(1, FFN_STEPS) as s:
                i = s * FFN_W + (W_FFN - 2)
                up_products(i, s * 2)
                down_products(i + 2, s - 1)
                up_products(i + 4, s * 2 + 1)
            down_products(W_FFN + 4 + (FFN_STEPS - 1) * FFN_W, FFN_STEPS - 1)

        @block.scalar
        def _(act):
            A = nc.scalar.activation
            for s in (z_ev, t_ev, sl, g_ev, ex, sq):
                act.sem_inc(s, LEAD)
            for s in (*g_st, *y_st):
                act.sem_inc(s, 16)

            def row_load(dst, src):
                act.dma_start(dst, src).then_inc(rows_in, 16)
            row_load(rows[0:96, 0, :], a["ssd_conv_w"][0].rearrange("k (j p) -> (k j) p", p=P))
            row_load(rows[96:120, 0, :], a["ssd_conv_b"][0].rearrange("(j p) -> j p", p=P))
            row_load(rows[0:88, 1, :], a["ffn_conv_w"][0, 0:2].rearrange("k (j p) -> (k j) p", p=P))
            row_load(rows[0:44, 2, :], a["ffn_conv_w"][0, 2].rearrange("(j p) -> j p", p=P))
            row_load(rows[44:88, 2, :], a["ffn_conv_b"][0].rearrange("(j p) -> j p", p=P))
            for i, n in enumerate(GAIN_ROWS):
                row_load(rows[8 * i:8 * i + 8, 3, :], a[n][0].rearrange("(j p) -> j p", p=P))
            row_load(rows[40:56, 3, :], a["ssd_norm"][0].rearrange("(j p) -> j p", p=P))
            act.dma_start(ws_rows[:, :, :], a["gm_w_s"][0].rearrange("g t s -> t g s")).then_inc(ws_in, 16)
            for dst, n in ((dt_bias, "ssd_dt_bias"), (a_log, "ssd_a_log"), (d_skip, "ssd_d")):
                act.dma_start(dst[:, :], a[n][0].partition_broadcast(P)).then_inc(dt_in, 16)

            def squares(u, h, src, jk, wait=None):
                per = min(4, NORM_TILES[u])
                for t in range(per * h, per * (h + 1)):
                    if wait:
                        wait(t)
                    if NORM_T0[u] + t:
                        act.wait_ge(n_sq, NORM_T0[u] + t)
                    A(jk[:, :], src[:, t, :], ACT.Square, accum_out=stat[:, t:t + 1]).then_inc(n_sq, 1)

            def root(u, h):
                per = min(4, NORM_TILES[u])
                act.wait_ge(n_var, 2 * (NORM_H0[u] + h) + 2)
                A(stat_s[:, per * h:per * (h + 1)], stat_r[:, per * h:per * (h + 1)], ACT.Sqrt).then_inc(n_rt, 1)

            def highs(u, gain0, hi):
                per = min(4, NORM_TILES[u])
                for q in range(NORM_TILES[u] // per * KT):
                    h, kt = q // KT, q % KT
                    act.wait_ge(n_tr, NORM_G0[u] + q + 1)
                    A(hi[:, kt, h * per * P:(h + 1) * per * P], bank[q % 8][:, 0:per * P], ACT.Copy,
                      scale=consts[:, 3, gain0 + kt:gain0 + kt + 1]).then_inc(n_hi, 1)

            for h in range(2):
                squares(PRE_X, h, x_tok, junk, lambda t: act.wait_ge(x_in, 32))
            for h in range(2):
                root(PRE_X, h)
            act.wait_ge(c_ev, 4)
            highs(PRE_X, 0, act_hi)

            act.wait_ge(dt_dve, 1)
            A(dt_abs[:, :, :], dt_x[:, :, :], ACT.Abs).then_inc(dt_act, 1)
            act.wait_ge(dt_act, 1)
            A(dt_e[:, :, :], dt_abs[:, :, :], ACT.Exp, scale=-1.0).then_inc(dt_act, 1)
            A(neg_a[:, :], a_log[:, :], ACT.Exp).then_inc(dt_act, 1)

            def gate_evac(g, q):
                act.wait_ge(g_st[q % 2], g * 96 + (16 * (q // 2) + 16))
                act.wait_ge(g_mm, nth(g, 12, q + 1) - LEAD)
                A(gate_out[:, q % 2, :], bank[q % 2][:, :], ACT.Sigmoid if q < 8 else ACT.Gelu_apprx_tanh).then_inc(g_ev, 1)
                act.wait_ge(g_ev, nth(g, 12, q + 1))
                tile = g * 2 + ((q // 4) * 8 + q // 2 % 2)
                act.dma_start(gates_dram[bass.ds(tile, 1), :, (q % 2) * HALF:(q % 2 + 1) * HALF].rearrange("j p t -> p (j t)"),
                              gate_out[:, q % 2, :]).then_inc(g_st[q % 2], 16)

            def ssd_group(g):
                for t in range(NT):
                    act.wait_ge(z_mm, g * 8 + (t + 1))
                    A(zs[:, t, :], bank[t][:, :], ACT.Silu).then_inc(z_ev, 1)

                def silu(idx):
                    act.wait_ge(cv, nth(g, 24, 4 * idx + 4))
                    dst = conv if idx < XG else b_t if idx == XG else c_t
                    A(dst[:, :], conv[:, :], ACT.Silu).then_inc(sl, 1)
                for idx in range(6):
                    for h in range(2):
                        if h and idx:
                            silu(idx - 1)
                        act.wait_ge(t_mm, g * 12 + (2 * idx + h + 1))
                        if h == 0:
                            act.wait_ge(cv, nth(g, 24, max(0, 4 * (idx - 1))))
                        A(xbc_raw[:, idx % 2, CONV - 1 + h * HALF:CONV - 1 + (h + 1) * HALF],
                          bank[2 * (idx % 2) + h][:, :], ACT.Copy).then_inc(t_ev, 1)
                    if idx == 0:
                        act.wait_ge(dt_cum, g + 1)
                        A(decays[:, :, :, :].rearrange("p i c h -> p (i c h)"), bank[7][:, 0:3 * NT * HPG],
                          ACT.Exp).then_inc(dt_exp, 1)
                silu(5)
                for q in range(2):
                    gate_evac(g, q)

                def square(c):
                    act.wait_ge(yy, nth(g, 32, 4 * c + 4))
                    act.wait_ge(sq, nth(g, 8, c))
                    A(sq_junk[:, :], xs[:, c, :], ACT.Square, accum_out=stat[:, c:c + 1]).then_inc(sq, 1)
                for c in range(NT):
                    for h in range(2):
                        act.wait_ge(seg, g * 16 + (2 * c + h + 1))
                        act.wait_ge(yd, nth(g, 8, c))
                        A(scores[:, h, :], bank[4 + h][:, :], ACT.Exp).then_inc(ex, 1)
                    gate_evac(g, c + 2)
                    if c:
                        square(c - 1)
                square(NT - 1)
                act.wait_ge(ysv, g * 2 + 2)
                A(stat_s[:, :], stat_r[:, :], ACT.Sqrt).then_inc(ysr, 1)
                for q in range(NT + 2, 12):
                    gate_evac(g, q)
                for c in range(NT):
                    act.wait_ge(ye, yth(g, c + 1))
                    act.dma_start(ssd_dram[bass.ds(g * XG, XG), :, c * P:(c + 1) * P].rearrange("j p t -> p j t"),
                                  y_t[:, c % 2, :, :]).then_inc(y_st[c % 2], 16)

            act.wait_ge(n_lo, NORM_G0[1])
            act.wait_ge(dt_dve, 16)
            with act.Fori(0, GROUPS) as g:
                ssd_group(g)

            for s in (*g_st,):
                act.wait_ge(s, 16 + 96 * GROUPS)
            for s in (*y_st,):
                act.wait_ge(s, 16 + 64 * GROUPS)
            for j in range(8):
                act.dma_start(r2[:, j, :], gates_dram[16 + j]).then_inc(slot_in[j], 16)
            act.dma_start(bs_bc[:, :, :], a["gm_b_s"][0].partition_broadcast(P)).then_inc(bs_in, 16)
            for n in range(2):
                for t in range(NT):
                    act.wait_ge(v_mm, 8 * n + t + 1)
                    A(r1[:, t, n * HALF:(n + 1) * HALF], bank[t][:, :], ACT.Gelu_apprx_tanh).then_inc(v_ev, 1)
            for t in range(NT):
                act.wait_ge(v_ev, 8 + t + 1)
                if t:
                    act.wait_ge(v_sq, t)
                A(junk2[:, :], r1[:, t, :], ACT.Square, accum_out=stat[:, t:t + 1]).then_inc(v_sq, 1)
            act.wait_ge(v_var, 2)
            A(stat_s[:, :], stat_r[:, :], ACT.Sqrt).then_inc(v_rt, 1)
            for q in range(16):
                act.wait_ge(m_ev, 2 * q + 2)
                A(act_hi[:, q // 2, (q % 2) * HALF:(q % 2 + 1) * HALF], g_tmp[:, q % 2, :], ACT.Copy).then_inc(m_hi, 1)
                if q % 2:
                    j = q // 2
                    act.dma_start(r2[:, j, :], gates_dram[j]).then_inc(slot_in[j], 16)
            for j in range(8):
                act.wait_ge(b_ev, 2 * j + 2)
                act.dma_start(r2[:, j, :], gates_dram[8 + j]).then_inc(slot_in[j], 16)

            def y_load(k):
                if k >= 2:
                    act.wait_ge(b_lo, k - 1)
                act.dma_start(y_in[:, k % 2, :], ssd_dram[k]).then_inc(y_ld[k % 2], 16)
            for k in range(2):
                y_load(k)
            for k in range(16):
                if k % 8 == 0:
                    act.wait_ge(b_mm, 16 * (k // 8 + 1))
                act.wait_ge(y_ld[k % 2], 16 * (k // 2 + 1))
                A(act_hi[:, k % 8, :], y_in[:, k % 2, :], ACT.Copy).then_inc(b_hi, 1)
                if k + 2 < 16:
                    y_load(k + 2)

            def split_highs(u, src, wait):
                wait()
                for kt in range(KT):
                    A(act_hi[:, kt, :], src[:, kt, :], ACT.Copy).then_inc(s_hi, 1)

            split_highs(0, r1, lambda: act.wait_ge(b_ev, 80))

            act.dma_start(mem_tok[:, :, :], a["mem"][0].rearrange("(t p) d -> p t d", p=P)).then_inc(mem_in, 16)
            act.dma_start(post_gain[:, :], a["norm_post_mix"][0].partition_broadcast(P)).then_inc(gain_in, 16)
            act.wait_ge(s_lo, 8)
            act.dma_start(r1[:, :, :], a["x"][0].rearrange("(t p) d -> p t d", p=P)).then_inc(xr_in, 16)
            squares(PRE_MEM_TOK, 0, mem_tok, junk3, lambda t: act.wait_ge(mem_in, 16))
            root(PRE_MEM_TOK, 0)
            highs(PRE_MEM_TOK, 24, mem_hi)

            def post_stats(u, jk):
                for h in range(2):
                    for t in range(4 * h, 4 * h + 4):
                        if u < 2:
                            act.wait_ge(o_ev, 16 * u + 8 + t + 1)
                        if 8 * u + t:
                            act.wait_ge(o_sq, 8 * u + t)
                        A(jk[:, :], r2[:, t, :], ACT.Square, accum_out=stat[:, t:t + 1]).then_inc(o_sq, 1)
                for h in range(2):
                    act.wait_ge(o_var, 4 * u + 2 * h + 2)
                    A(stat_s[:, 4 * h:4 * h + 4], stat_r[:, 4 * h:4 * h + 4], ACT.Sqrt).then_inc(o_rt, 1)
            post_stats(0, junk3)
            for j in range(8):
                act.wait_ge(k_mm, j + 1)
                A(k_t[:, j, :], bank[j][:, 0:MEM], ACT.Copy).then_inc(k_ev, 1)
            for n in range(2):
                for t in range(2):
                    act.wait_ge(k_mm, 8 + 2 * n + t + 1)
                    A(v_tok[:, t, n * HALF:(n + 1) * HALF], bank[2 * n + t][:, :], ACT.Copy).then_inc(k_ev, 1)
            for h in range(2):
                squares(PRE_MEM, h, r1, junk3, lambda t: act.wait_ge(o_x, t + 1))
            for h in range(2):
                root(PRE_MEM, h)
            highs(PRE_MEM, 8, act_hi)

            def query_evac(h):
                for r in range(4):
                    act.wait_ge(q_mm, 4 * h + r + 1)
                    A(q_t[:, r // 2, (r % 2) * HALF:(r % 2 + 1) * HALF], bank[r][:, :], ACT.Copy).then_inc(q_ev, 1)
            act.wait_ge(n_lo, NORM_G0[PRE_FFN])
            query_evac(0)
            for h in range(XH):
                for t in range(NT):
                    act.wait_ge(a_mx, 5 * h + 5)
                    if h:
                        act.wait_ge(a_tr, 4 * h)
                    A(prob[:, t, :], bank[4 + t // 2][:, (t % 2) * MEM:(t % 2 + 1) * MEM], ACT.Exp,
                      bias=a_nm[:, t:t + 1], scale=XHD ** -0.5, accum_out=a_sum[:, t:t + 1]).then_inc(a_ex, 1)
                if h + 1 < XH:
                    query_evac(h + 1)
                for q in range(4):
                    act.wait_ge(p_mm, 4 * h + q + 1)
                    A(r2[:, 2 * h + q // 2, (q % 2) * HALF:(q % 2 + 1) * HALF], bank[4 + q][:, :], ACT.Copy).then_inc(p_ev, 1)
            split_highs(1, r2, lambda: act.wait_ge(p_ev, 16))
            act.wait_ge(s_lo, 16)
            act.dma_start(post_gain2[:, :], a["norm_post_mem"][0].partition_broadcast(P)).then_inc(gain_in, 16)
            post_stats(1, junk4)
            for h in range(2):
                squares(PRE_FFN, h, r1, junk4, lambda t: act.wait_ge(o_x, 8 + t + 1))
            for h in range(2):
                root(PRE_FFN, h)
            highs(PRE_FFN, 16, act_hi)

            def pair(u, step, p, first=False):
                for b in range(4):
                    act.wait_ge(f_mm, u * 4 + (b + 1))
                    if not first:
                        act.wait_ge(f_cv, u * 7 + (-4 if b < 2 else -1))
                    A(up_raw[:, b // 2, FFN_CONV - 1 + (b % 2) * HALF:FFN_CONV - 1 + (b % 2 + 1) * HALF],
                      bank[b][:, :], ACT.Copy).then_inc(f_ev, 1)
                act.wait_ge(f_cv, u * 7 + 3)
                A(up_a[:, :], up_a[:, :], ACT.Gelu_apprx_tanh).then_inc(f_gl, 1)
                act.wait_ge(f_cv, u * 7 + 7)
                if step is not None:
                    act.wait_ge(d_mm, step * 16)
                A(f_hi[:, p, :], up_a[:, :], ACT.Copy).then_inc(f_h, 1)

            act.wait_ge(n_lo, NORM_G0[PRE_FFN] + 16)
            pair(0, None, 0, True)
            pair(1, None, 1)
            with act.Fori(1, FFN_STEPS) as s:
                pair(s * 2, s, 0)
                pair(s * 2 + 1, s, 1)
            act.wait_ge(d_ad, 4 + 16 * FFN_STEPS)
            act.dma_start(post_gain3[:, :], a["norm_post_ffn"][0].partition_broadcast(P)).then_inc(gain_in, 16)
            post_stats(2, junk5)

        @block.vector
        def _(dve):
            V = nc.vector
            for s in (cv, xe, gc, xd_s, sk, sc, xdd_s, pv, yy, ys):
                dve.sem_inc(s, LEAD)
            dve.sem_inc(ye, Y_LEAD)
            dve.sem_inc(d_ad, 4)

            dve.wait_ge(masks, 7)
            V.tensor_copy(after_r[:, :], after[:, :])
            for r, n in enumerate(ROW_COUNTS):
                dve.wait_ge(c_tr, 1)
                V.tensor_copy(consts[:, r, 0:n], bank[0][:, r * P:r * P + n]).then_inc(c_ev, 1)
            for h in range(2):
                dve.wait_ge(c_tr, 2 + h)
                V.tensor_tensor(ws_t[:, 4 * h:4 * h + 4, :], bank[1 + h][:, :].rearrange("p (g t) -> p g t", t=P),
                                tri[:, :].unsqueeze(1).to_broadcast([P, 4, P]), ALU.mult).then_inc(c_ev, 1)

            def variance(u, h):
                per = min(4, NORM_TILES[u])
                s = slice(per * h, per * (h + 1))
                dve.wait_ge(n_sq, NORM_T0[u] + per * (h + 1))
                V.tensor_scalar(stat_v[:, s], stat[:, s], 1.0 / DM, EPS, ALU.mult, ALU.add).then_inc(n_var, 1)
                dve.wait_ge(n_var, 2 * (NORM_H0[u] + h) + 1)
                V.reciprocal(stat_r[:, s], stat_v[:, s]).then_inc(n_var, 1)

            def scale(u, h, src, dst):
                per = min(4, NORM_TILES[u])
                dve.wait_ge(n_rt, NORM_H0[u] + h + 1)
                for t in range(per * h, per * (h + 1)):
                    V.tensor_scalar(dst[:, t, :], src[:, t, :], stat_s[:, t:t + 1], None, ALU.mult).then_inc(n_xs, 1)

            def lows(u, gain0, hi, lo):
                per = min(4, NORM_TILES[u])
                for q in range(NORM_TILES[u] // per * KT):
                    h, kt = q // KT, q % KT
                    s = slice(h * per * P, (h + 1) * per * P)
                    dve.wait_ge(n_hi, NORM_G0[u] + q + 1)
                    V.scalar_tensor_tensor(out=lo[:, kt, s], in0=bank[q % 8][:, 0:per * P],
                                           scalar=consts[:, 3, gain0 + kt:gain0 + kt + 1], in1=hi[:, kt, s].bitcast(F32),
                                           op0=ALU.mult, op1=ALU.subtract).then_inc(n_lo, 1)

            for h in range(2):
                variance(PRE_X, h)
            for h in range(2):
                scale(PRE_X, h, x_tok, x_tok)
            dve.wait_ge(dt_in, 16 * 4)
            V.tensor_copy(dtw_hi[:, :, :], dtw[:, :, :]).then_inc(dt_w, 1)
            dve.wait_ge(dt_w, 1)
            V.tensor_tensor(dtw_lo[:, :, :], dtw[:, :, :], dtw_hi[:, :, :].bitcast(F32), ALU.subtract).then_inc(dt_w, 1)
            lows(PRE_X, 0, act_hi, act_lo)

            n = [0]

            def step(ins):
                n[0] += 1
                ins.then_inc(dt_dve, 1)
                dve.wait_ge(dt_dve, n[0])
            dve.wait_ge(dt_mm, 1)
            step(V.tensor_tensor(dt_x[:, :, :], bank[0][:, 0:NT * HEADS].rearrange("p (c h) -> p c h", h=HEADS),
                                 dt_bias[:, :].unsqueeze(1).to_broadcast([P, NT, HEADS]), ALU.add))
            dve.wait_ge(dt_act, 2)
            step(V.tensor_scalar(dt_d[:, :, :], dt_e[:, :, :], 2.0, None, ALU.add))
            step(V.reciprocal(dt_r[:, :, :], dt_d[:, :, :]))
            step(V.scalar_tensor_tensor(out=dt_s[:, :, :], in0=dt_e[:, :, :], scalar=2.0, in1=dt_r[:, :, :],
                                        op0=ALU.mult, op1=ALU.mult))
            step(V.scalar_tensor_tensor(out=dt_q[:, :, :], in0=dt_s[:, :, :], scalar=0.25, in1=dt_s[:, :, :],
                                        op0=ALU.mult, op1=ALU.mult))
            step(V.tensor_scalar(dt_p[:, :, :], dt_q[:, :, :], 1.0 / 13, None, ALU.mult))
            for c in (11, 9, 7, 5, 3):
                step(V.scalar_tensor_tensor(out=dt_p[:, :, :], in0=dt_p[:, :, :], scalar=1.0 / c, in1=dt_q[:, :, :],
                                            op0=ALU.add, op1=ALU.mult))
            step(V.scalar_tensor_tensor(out=dt_p[:, :, :], in0=dt_p[:, :, :], scalar=1.0, in1=dt_s[:, :, :],
                                        op0=ALU.add, op1=ALU.mult))
            step(V.scalar_tensor_tensor(out=dt[:, :, :], in0=dt_x[:, :, :], scalar=0.0, in1=dt_p[:, :, :],
                                        op0=ALU.max, op1=ALU.add))
            dve.wait_ge(dt_act, 3)
            step(V.scalar_tensor_tensor(out=dA[:, :, :], in0=dt[:, :, :], scalar=-1.0,
                                        in1=neg_a[:, :].unsqueeze(1).to_broadcast([P, NT, HEADS]),
                                        op0=ALU.mult, op1=ALU.mult))
            step(V.tensor_copy(dA_hi[:, :, :], dA[:, :, :]))
            step(V.tensor_tensor(dA_lo[:, :, :], dA[:, :, :], dA_hi[:, :, :].bitcast(F32), ALU.subtract))
            assert n[0] == 16

            dve.wait_ge(n_lo, NORM_G0[1])
            V.memset(xbc_raw[:, :, 0:CONV - 1], 0.0)

            def heads(ap):
                return ap.rearrange("p (r d) -> p r d", d=HD)

            def ssd_group(g):
                dve.wait_ge(ye, yth(g, 0))
                cv_c = consts[:, 0, 0:(CONV + 1) * XBC_TILES].rearrange("p (k j) -> p k j", j=XBC_TILES)
                for dst, src in ((g_conv[:, :, 0:XG], cv_c[:, :, bass.ds(g * XG, XG)]),
                                 (g_conv[:, :, XG:XG + 1], cv_c[:, :, bass.ds(g + 16, 1)]),
                                 (g_conv[:, :, XG + 1:XG + 2], cv_c[:, :, bass.ds(g + 20, 1)]),
                                 (g_gain[:, :], consts[:, 3, bass.ds(g * XG + 40, XG)]),
                                 (g_skip[:, :], d_skip[:, bass.ds(g * HPG, HPG)]),
                                 (g_dt[:, :, :], dt[:, :, bass.ds(g * HPG, HPG)]),
                                 (g_hi[:, :, :], dA_hi[:, :, bass.ds(g * HPG, HPG)].bitcast(F32)),
                                 (g_lo[:, :, :], dA_lo[:, :, bass.ds(g * HPG, HPG)]),
                                 (g_dA[:, :, :], dA[:, :, bass.ds(g * HPG, HPG)])):
                    V.tensor_copy(dst, src).then_inc(gc, 1)
                dve.wait_ge(gc, nth(g, GC, GC))

                def convolve(idx):
                    dve.wait_ge(t_ev, nth(g, 12, 2 * idx + 2))
                    if idx in (1, 2, 3, 4):
                        dve.wait_ge(xt, g * 10 + 2 * idx)
                    elif idx == 5:
                        dve.wait_ge(sl, nth(g, 6, 5))
                    V.tensor_scalar(conv[:, :], xbc_raw[:, idx % 2, CONV - 1:CONV - 1 + SEQ],
                                    g_conv[:, CONV - 1, idx:idx + 1], g_conv[:, CONV, idx:idx + 1],
                                    ALU.mult, ALU.add).then_inc(cv, 1)
                    for k in range(CONV - 1):
                        dve.wait_ge(cv, nth(g, 24, 4 * idx + k + 1))
                        V.scalar_tensor_tensor(out=conv[:, :], in0=xbc_raw[:, idx % 2, k:k + SEQ],
                                               scalar=g_conv[:, k, idx:idx + 1], in1=conv[:, :],
                                               op0=ALU.mult, op1=ALU.add).then_inc(cv, 1)

                def token_evac(idx):
                    for h in range(2):
                        q = 2 * idx + h
                        dve.wait_ge(xt, g * 10 + (q + 1))
                        src = bank[4 + q % 4][:, :].rearrange("p (c d) -> p c d", d=P)
                        dst = b_tok[:, 4 * h:4 * h + 4, :] if idx == XG else xs[:, 4 * h:4 * h + 4, idx * P:(idx + 1) * P]
                        V.tensor_copy(dst, src).then_inc(xe, 1)
                for idx in range(6):
                    convolve(idx)
                    if idx:
                        token_evac(idx - 1)
                dve.wait_ge(pv, nth(g, 17, 0))
                V.memset(state[:, :], 0.0).then_inc(pv, 1)

                def before_chunk(c):
                    if c >= 2:
                        dve.wait_ge(yd, nth(g, 8, c - 1))
                    if c == 0:
                        dve.wait_ge(xe, nth(g, 10, 8))
                    V.tensor_tensor(heads(xd[:, c % 2, :]), heads(xs[:, c, :]), bc(g_dt[:, c, :], [P, HPG, HD]),
                                    ALU.mult).then_inc(xd_s, 1)
                    dve.wait_ge(xd_s, nth(g, 8, c + 1))
                    V.tensor_tensor(heads(xs[:, c, :]), heads(xs[:, c, :]), bc(g_skip[:, :], [P, HPG, HD]),
                                    ALU.mult).then_inc(sk, 1)

                def score(c):
                    dve.wait_ge(cb, g * 8 + (c + 1))
                    V.tensor_tensor(cb_m[:, :], bank[3][:, 0:P], tri[:, :], ALU.mult).then_inc(sc, 1)
                    for h in range(2):
                        dve.wait_ge(ex, nth(g, 16, 2 * c + h + 1))
                        dve.wait_ge(sc, nth(g, 24, 3 * c + 1))
                        s = scores[:, h, :].rearrange("p (r l) -> p r l", l=P)
                        V.tensor_tensor(s, s, cb_m[:, :].unsqueeze(1).to_broadcast([P, 4, P]), ALU.mult).then_inc(sc, 1)
                    if c:
                        dve.wait_ge(st, g * 8 + c)
                    V.tensor_tensor(heads(xdd[:, :]), heads(xd[:, c % 2, :]), bc(g_out[:, c, :], [P, HPG, HD]),
                                    ALU.mult).then_inc(xdd_s, 1)

                def combine(c):
                    dve.wait_ge(yo, g * 8 + (c + 1))
                    V.tensor_tensor(heads(y_sum[:, :]), heads(bank[7][:, :]), bc(g_in[:, c, :], [P, HPG, HD]),
                                    ALU.mult).then_inc(yy, 1)
                    V.tensor_tensor(heads(state[:, :]), heads(state[:, :]), bc(g_chunk[:, c, :], [P, HPG, HD]),
                                    ALU.mult).then_inc(pv, 1)
                    dve.wait_ge(yy, nth(g, 32, 4 * c + 1))
                    V.tensor_tensor(y_sum[:, :], y_sum[:, :], bank[6][:, :], ALU.add).then_inc(yy, 1)
                    dve.wait_ge(st, g * 8 + (c + 1))
                    dve.wait_ge(pv, nth(g, 17, 2 * c + 2))
                    V.tensor_tensor(state[:, :], state[:, :], bank[2][:, :], ALU.add).then_inc(pv, 1)
                    dve.wait_ge(yy, nth(g, 32, 4 * c + 2))
                    V.tensor_tensor(xs[:, c, :], xs[:, c, :], y_sum[:, :], ALU.add).then_inc(yy, 1)
                    dve.wait_ge(yy, nth(g, 32, 4 * c + 3))
                    V.tensor_tensor(xs[:, c, :], xs[:, c, :], zs[:, c, :], ALU.mult).then_inc(yy, 1)

                before_chunk(0)
                for c in range(NT):
                    score(c)
                    if c + 1 < NT:
                        before_chunk(c + 1)
                    combine(c)
                dve.wait_ge(sq, nth(g, 8, 8))
                V.tensor_scalar(stat_v[:, :], stat[:, :], 1.0 / HALF, EPS, ALU.mult, ALU.add).then_inc(ysv, 1)
                dve.wait_ge(ysv, g * 2 + 1)
                V.reciprocal(stat_r[:, :], stat_v[:, :]).then_inc(ysv, 1)
                dve.wait_ge(ysr, g + 1)
                for c in range(NT):
                    V.tensor_scalar(xs[:, c, :], xs[:, c, :], stat_s[:, c:c + 1], None, ALU.mult).then_inc(ys, 1)
                for c in range(NT):
                    dve.wait_ge(yt, g * 8 + (c + 1))
                    dve.wait_ge(y_st[c % 2], g * 64 + (16 * (c // 2) + 16))
                    V.tensor_tensor(y_t[:, c % 2, :, :], bank[c][:, :].rearrange("p (j t) -> p j t", t=P),
                                    bc(g_gain[:, :], [P, XG, P]), ALU.mult).then_inc(ye, 1)

            with dve.Fori(0, GROUPS) as g:
                ssd_group(g)

            dve.wait_ge(v_sq, 8)
            V.tensor_scalar(stat_v[:, :], stat[:, :], 1.0 / DM, EPS, ALU.mult, ALU.add).then_inc(v_var, 1)
            dve.wait_ge(v_var, 1)
            V.reciprocal(stat_r[:, :], stat_v[:, :]).then_inc(v_var, 1)
            dve.wait_ge(v_rt, 1)
            for t in range(NT):
                V.tensor_scalar(r1[:, t, :], r1[:, t, :], stat_s[:, t:t + 1], None, ALU.mult).then_inc(v_sc, 1)
            dve.wait_ge(bs_in, 16)

            def mix_low(q):
                dve.wait_ge(m_hi, q + 1)
                s = slice((q % 2) * HALF, (q % 2 + 1) * HALF)
                V.tensor_tensor(act_lo[:, q // 2, s], g_tmp[:, q % 2, :], act_hi[:, q // 2, s].bitcast(F32),
                                ALU.subtract).then_inc(m_lo, 1)
            for q in range(16):
                g = q // 2
                dve.wait_ge(m_mm, q + 1)
                if q >= 2:
                    dve.wait_ge(m_lo, q - 1)
                V.scalar_tensor_tensor(out=g_tmp[:, q % 2, :].rearrange("p (c t) -> p c t", t=P),
                                       in0=bank[q % 8][:, :].rearrange("p (c t) -> p c t", t=P),
                                       scalar=consts[:, 3, 32 + g:33 + g],
                                       in1=bs_bc[:, g, :].unsqueeze(1).to_broadcast([P, 4, P]),
                                       op0=ALU.mult, op1=ALU.add).then_inc(m_ev, 1)
                dve.wait_ge(slot_in[g], 16)
                dve.wait_ge(m_ev, 2 * q + 1)
                V.tensor_tensor(g_tmp[:, q % 2, :], g_tmp[:, q % 2, :], r2[:, g, (q % 2) * HALF:(q % 2 + 1) * HALF],
                                ALU.mult).then_inc(m_ev, 1)
                if q:
                    mix_low(q - 1)
            mix_low(15)

            def y_low(k):
                dve.wait_ge(b_hi, k + 1)
                V.tensor_tensor(act_lo[:, k % 8, :], y_in[:, k % 2, :], act_hi[:, k % 8, :].bitcast(F32),
                                ALU.subtract).then_inc(b_lo, 1)
            for part in range(3):
                for r in range(16):
                    j, s = r // 2, slice((r % 2) * HALF, (r % 2 + 1) * HALF)
                    q = 16 * part + r
                    dve.wait_ge(b_mm, q + 1)
                    dve.wait_ge(slot_in[j], 32 if part == 0 else 48)
                    if part == 0:
                        V.tensor_tensor(r1[:, j, s], bank[q % 8][:, :], r2[:, j, s], ALU.mult).then_inc(b_ev, 1)
                    else:
                        done = 16 + 2 * (q - 16)
                        if r >= 2 or part == 2:
                            dve.wait_ge(b_ev, done - 2)
                        V.tensor_tensor(g_tmp[:, r % 2, :], bank[q % 8][:, :], r2[:, j, s], ALU.mult).then_inc(b_ev, 1)
                        dve.wait_ge(b_ev, done + 1)
                        V.tensor_tensor(r1[:, j, s], r1[:, j, s], g_tmp[:, r % 2, :], ALU.add).then_inc(b_ev, 1)
                if part < 2:
                    for k in range(8 * part, 8 * part + 8):
                        y_low(k)

            def split_lows(u, src):
                for kt in range(KT):
                    dve.wait_ge(s_hi, 8 * u + kt + 1)
                    V.tensor_tensor(act_lo[:, kt, :], src[:, kt, :], act_hi[:, kt, :].bitcast(F32),
                                    ALU.subtract).then_inc(s_lo, 1)

            def out_evac(u, n):
                for t in range(NT):
                    dve.wait_ge(o_mm, 16 * u + 8 * n + t + 1)
                    V.tensor_copy(r2[:, t, n * HALF:(n + 1) * HALF], bank[t][:, :]).then_inc(o_ev, 1)

            def residual(u, gain):
                for h in range(2):
                    s = slice(4 * h, 4 * h + 4)
                    dve.wait_ge(o_sq, 8 * u + 4 * h + 4)
                    V.tensor_scalar(stat_v[:, s], stat[:, s], 1.0 / DM, EPS, ALU.mult, ALU.add).then_inc(o_var, 1)
                    dve.wait_ge(o_var, 4 * u + 2 * h + 1)
                    V.reciprocal(stat_r[:, s], stat_v[:, s]).then_inc(o_var, 1)
                dve.wait_ge(gain_in, 16 * (u + 1))
                if u == 0:
                    dve.wait_ge(xr_in, 16)
                for t in range(NT):
                    dve.wait_ge(o_rt, 2 * u + t // 4 + 1)
                    V.scalar_tensor_tensor(out=r2[:, t, :], in0=r2[:, t, :], scalar=stat_s[:, t:t + 1], in1=gain[:, :],
                                           op0=ALU.mult, op1=ALU.mult).then_inc(o_y, 1)
                    if t:
                        dve.wait_ge(o_y, 8 * u + t)
                        V.tensor_tensor(r1[:, t - 1, :], r1[:, t - 1, :], r2[:, t - 1, :], ALU.add).then_inc(o_x, 1)
                dve.wait_ge(o_y, 8 * u + 8)
                V.tensor_tensor(r1[:, 7, :], r1[:, 7, :], r2[:, 7, :], ALU.add).then_inc(o_x, 1)

            split_lows(0, r1)
            variance(PRE_MEM_TOK, 0)
            scale(PRE_MEM_TOK, 0, mem_tok, mem_tok)
            out_evac(0, 0)
            lows(PRE_MEM_TOK, 24, mem_hi, mem_lo)
            out_evac(0, 1)
            residual(0, post_gain)
            for h in range(2):
                variance(PRE_MEM, h)
            for h in range(2):
                scale(PRE_MEM, h, r1, r2)
            lows(PRE_MEM, 8, act_hi, act_lo)

            for h in range(XH):
                for b in range(4):
                    dve.wait_ge(s_mm, 4 * h + b + 1)
                    V.tensor_reduce(out=a_max[:, 2 * b:2 * b + 2], in_=bank[4 + b][:, :].rearrange("p (t m) -> p t m", m=MEM),
                                    axis=AX.X, op=ALU.max).then_inc(a_mx, 1)
                dve.wait_ge(a_mx, 5 * h + 4)
                V.tensor_scalar(a_nm[:, :], a_max[:, :], -(XHD ** -0.5), None, ALU.mult).then_inc(a_mx, 1)
                dve.wait_ge(a_ex, 8 * h + 8)
                V.reciprocal(a_rec[:, :], a_sum[:, :]).then_inc(a_pn, 1)
                dve.wait_ge(a_pn, 9 * h + 1)
                for t in range(NT):
                    V.tensor_scalar(prob[:, t, :], prob[:, t, :], a_rec[:, t:t + 1], None, ALU.mult).then_inc(a_pn, 1)
                for q in range(4):
                    dve.wait_ge(a_tr, 4 * h + q + 1)
                    V.tensor_copy(prob_t[:, q // 2, (q % 2) * HALF:(q % 2 + 1) * HALF], bank[4 + q][:, :]).then_inc(a_te, 1)
            split_lows(1, r2)
            for n in range(2):
                out_evac(1, n)
            residual(1, post_gain2)
            for h in range(2):
                variance(PRE_FFN, h)
            for h in range(2):
                scale(PRE_FFN, h, r1, r2)
            lows(PRE_FFN, 16, act_hi, act_lo)

            V.memset(up_raw[:, :, 0:FFN_CONV - 1], 0.0)
            V.memset(r2[:, :, :], 0.0).then_inc(o_y, 1)

            def tap(k, col):
                r, off = ((1, 0), (1, 44), (2, 0), (2, 44))[k]
                return consts[:, r, bass.ds(col + off, 1)]

            def conv_step(u, col, i):
                w, k = i // 3, i % 3
                dst = (up_a, up_b)[w]
                c = col + w * FFN_TILES
                if k == 0:
                    dve.wait_ge(f_ev, u * 4 + (2 * w + 2))
                    if w == 0 and not (isinstance(u, int) and u == 0):
                        dve.wait_ge(f_l, u)
                    V.tensor_scalar(dst[:, :], up_raw[:, w, FFN_CONV - 1:FFN_CONV - 1 + SEQ], tap(2, c), tap(3, c),
                                    ALU.mult, ALU.add).then_inc(f_cv, 1)
                else:
                    dve.wait_ge(f_cv, u * 7 + i)
                    V.scalar_tensor_tensor(out=dst[:, :], in0=up_raw[:, w, k - 1:k - 1 + SEQ], scalar=tap(k - 1, c),
                                           in1=dst[:, :], op0=ALU.mult, op1=ALU.add).then_inc(f_cv, 1)

            def gate_pair(u):
                dve.wait_ge(f_gl, u + 1)
                dve.wait_ge(f_cv, u * 7 + 6)
                V.tensor_tensor(up_a[:, :], up_a[:, :], up_b[:, :], ALU.mult).then_inc(f_cv, 1)

            def low_pair(u, p):
                dve.wait_ge(f_h, u + 1)
                V.tensor_tensor(f_lo[:, p, :], up_a[:, :], f_hi[:, p, :].bitcast(F32), ALU.subtract).then_inc(f_l, 1)

            def add(step, r):
                n, t = r // 8, r % 8
                dve.wait_ge(d_mm, step * 16 + (r + 1))
                dve.wait_ge(d_ad, step * 16 + (r + 3))
                s = r2[:, t, n * HALF:(n + 1) * HALF]
                V.tensor_tensor(s, s, bank[4 + r % 4][:, :], ALU.add).then_inc(d_ad, 1)

            for u in range(2):
                for i in range(6):
                    conv_step(u, u, i)
                gate_pair(u)
                low_pair(u, u)
            dve.wait_ge(o_y, 17)
            with dve.Fori(1, FFN_STEPS) as s:
                for r in range(16):
                    if r % 2 == 0 and r < 12:
                        conv_step(s * 2, s * 2, r // 2)
                    if r == 13:
                        gate_pair(s * 2)
                    add(s - 1, r)
                low_pair(s * 2, 0)
                for i in range(6):
                    conv_step(s * 2 + 1, s * 2 + 1, i)
                gate_pair(s * 2 + 1)
                low_pair(s * 2 + 1, 1)
            for r in range(16):
                add(FFN_STEPS - 1, r)
            residual_last(dve, V, r1, r2, post_gain3, stat, stat_v, stat_r, stat_s, o_sq, o_var, o_rt, o_y, o_x, gain_in)


def residual_last(dve, V, r1, r2, gain, stat, stat_v, stat_r, stat_s, o_sq, o_var, o_rt, o_y, o_x, gain_in):
    for h in range(2):
        s = slice(4 * h, 4 * h + 4)
        dve.wait_ge(o_sq, 16 + 4 * h + 4)
        V.tensor_scalar(stat_v[:, s], stat[:, s], 1.0 / DM, EPS, ALU.mult, ALU.add).then_inc(o_var, 1)
        dve.wait_ge(o_var, 8 + 2 * h + 1)
        V.reciprocal(stat_r[:, s], stat_v[:, s]).then_inc(o_var, 1)
    dve.wait_ge(gain_in, 48)
    for t in range(NT):
        dve.wait_ge(o_rt, 4 + t // 4 + 1)
        V.scalar_tensor_tensor(out=r2[:, t, :], in0=r2[:, t, :], scalar=stat_s[:, t:t + 1], in1=gain[:, :],
                               op0=ALU.mult, op1=ALU.mult).then_inc(o_y, 1)
        dve.wait_ge(o_y, 17 + t + 1)
        V.tensor_tensor(r1[:, t, :], r1[:, t, :], r2[:, t, :], ALU.add).then_inc(o_x, 1)


ROW_COUNTS = [120, 88, 88, 56]
GAIN_ROWS = ["norm_pre_mix", "norm_pre_mem", "norm_pre_ffn", "norm_mem_kv", "gm_v_norm"]
ROW_LOADS = 5 + len(GAIN_ROWS) + 1

_INS = ["x", "mem", "norm_pre_mix", "norm_post_mix", "norm_pre_mem", "norm_mem_kv", "norm_post_mem",
        "norm_pre_ffn", "norm_post_ffn", "w_in", "gm_v_norm", "gm_w_s", "gm_b_s", "ssd_conv_w", "ssd_conv_b",
        "ssd_dt_bias", "ssd_a_log", "ssd_d", "ssd_norm", "w_branch_a", "w_branch_b", "w_out",
        "xa_w_q", "xa_w_kv", "xa_w_o", "ffn_w_up", "ffn_conv_w", "ffn_conv_b", "ffn_w_down"]


def kernel(**inputs):
    import numpy as _np
    import concourse.bacc as _bacc
    from concourse import mybir as _mybir
    from concourse.bass_utils import run_bass_kernel_spmd as _run

    nc = _bacc.Bacc("TRN2", target_bir_lowering=False, num_devices=1)
    arrays, args = {}, {}
    for name in _INS:
        v = _np.ascontiguousarray(inputs[name])
        arrays[f"in_{name}"] = v
        args[name] = nc.dram_tensor(f"in_{name}", v.shape, _mybir.dt.from_np(v.dtype), kind="ExternalInput").ap()
    out = nc.dram_tensor("out_x", (1, SEQ, DM), _mybir.dt.float32, kind="ExternalOutput").ap()
    trunk(nc, args, out)
    r = _run(nc, [arrays], core_ids=[0])
    return r.results[0]["out_x"]
```

```python
import concourse.bass as bass
from concourse import mybir
from contextlib import ExitStack


F32 = mybir.dt.float32
F32R = mybir.dt.float32r
ALU = mybir.AluOpType
ACT = mybir.ActivationFunctionType
AX = mybir.AxisListType

P = 128
SEQ = 1024
DM = 1024
KT = DM // P
NT = SEQ // P
HALF = 512
MEM = 256
EPS = 1e-6

GROUPS = 4
HPG = 8
HD = 64
XG = HPG * HD // P
CONV = 4
XBC_TILES = 24
U_OFF, V_OFF, Z_OFF, XBC_OFF = 0, 1024, 2048, 4096
DT_OFF, GA_OFF, GB_OFF = 7168, 7200, 8224
HEADS = 32

FFN_TILES = 22
FFN_CONV = 3
FFN_STEPS = FFN_TILES // 2

XH = 4
XHD = 256

SSD_TILES = 16
W_SSD = 0
W_V = W_SSD + GROUPS * SSD_TILES
W_BRANCH = W_V + 8
W_OUT = W_BRANCH + 24
W_K = W_OUT + 8
W_VM = W_K + 8
W_Q = W_VM + 8
W_O = W_Q + 8
W_FFN = W_O + 8
FFN_W = 6

NORM_TILES = [8, 2, 8, 8]
NORM_T0 = [0, 8, 10, 18]
NORM_H0 = [0, 2, 3, 5]
NORM_G0 = [0, 16, 24, 40]
PRE_X, PRE_MEM_TOK, PRE_MEM, PRE_FFN = range(4)


def trunk(nc, a, out):
    ctx = ExitStack()

    def dram(name, shape):
        return nc.dram_tensor(name, shape, F32, kind="Internal").ap()

    gates_dram = dram("gates_scratch", (24, P, SEQ))
    ssd_dram = dram("ssd_scratch", (16, P, SEQ))

    with ctx:
        def sb(name, shape, dt=F32, c=ctx):
            return c.enter_context(nc.sbuf_tensor(name, shape, dt))

        def sem(name):
            return ctx.enter_context(nc.semaphore(name))

        act_hi = sb("act_hi", [P, KT, SEQ], F32R)
        act_lo = sb("act_lo", [P, KT, SEQ], F32R)
        w_raw = sb("w_raw", [P, 2, 1024])
        w_hi = sb("w_hi", [P, 2, 1024], F32R)
        w_lo = sb("w_lo", [P, 2, 1024], F32R)
        ident = sb("ident", [P, P])
        tri = sb("tri", [P, P])
        after = sb("after", [P, P])
        consts = sb("consts", [P, 4, P])
        stat = sb("stat", [P, 8])
        stat_v = sb("stat_v", [P, 8])
        stat_r = sb("stat_r", [P, 8])
        stat_s = sb("stat_s", [P, 8])
        ffn_conv_c = None

        ssd = ExitStack()
        ws_t = None
        keep = ExitStack()
        ws_t = sb("ws_t", [P, 8, P], c=keep)
        base = ExitStack()
        after_r = sb("after_r", [P, P], F32R, base)
        ones = sb("ones", [P, P], c=base)
        dt = sb("dt", [P, NT, HEADS], c=base)
        dA = sb("dA", [P, NT, HEADS], c=base)
        dA_hi = sb("dA_hi", [P, NT, HEADS], F32R, base)
        dA_lo = sb("dA_lo", [P, NT, HEADS], c=base)
        d_skip = sb("d_skip", [P, HEADS], c=base)

        setup = ExitStack()
        x_tok = sb("x_tok", [P, NT, DM], c=setup)
        rows = sb("rows", [P, 4, P], c=setup)
        ws_rows = sb("ws_rows", [P, 8, P], c=setup)
        junk = sb("junk", [P, DM], c=setup)
        dtw = sb("dtw", [P, KT, HEADS], c=setup)
        dtw_hi = sb("dtw_hi", [P, KT, HEADS], F32R, setup)
        dtw_lo = sb("dtw_lo", [P, KT, HEADS], F32R, setup)
        dt_bias = sb("dt_bias", [P, HEADS], c=setup)
        a_log = sb("a_log", [P, HEADS], c=setup)
        dt_x = sb("dt_x", [P, NT, HEADS], c=setup)
        dt_abs = sb("dt_abs", [P, NT, HEADS], c=setup)
        dt_e = sb("dt_e", [P, NT, HEADS], c=setup)
        dt_d = sb("dt_d", [P, NT, HEADS], c=setup)
        dt_r = sb("dt_r", [P, NT, HEADS], c=setup)
        dt_s = sb("dt_s", [P, NT, HEADS], c=setup)
        dt_q = sb("dt_q", [P, NT, HEADS], c=setup)
        dt_p = sb("dt_p", [P, NT, HEADS], c=setup)
        neg_a = sb("neg_a", [P, HEADS], c=setup)
        setup.close()

        xs = sb("xs", [P, NT, HALF], c=ssd)
        zs = sb("zs", [P, NT, HALF], c=ssd)
        b_t = sb("b_t", [P, SEQ], c=ssd)
        c_t = sb("c_t", [P, SEQ], c=ssd)
        b_tok = sb("b_tok", [P, NT, P], c=ssd)
        xbc_raw = sb("xbc_raw", [P, 2, CONV - 1 + SEQ], c=ssd)
        conv = sb("conv", [P, SEQ], c=ssd)
        gate_out = sb("gate_out", [P, 2, HALF], c=ssd)
        tri_hi = sb("tri_hi", [P, 2, HALF], F32R, ssd)
        tri_lo = sb("tri_lo", [P, 2, HALF], F32R, ssd)
        scores = sb("scores", [P, 2, HALF], c=ssd)
        cb_m = sb("cb_m", [P, P], c=ssd)
        xd = sb("xd", [P, 2, HALF], c=ssd)
        xdd = sb("xdd", [P, HALF], c=ssd)
        state = sb("state", [P, HALF], c=ssd)
        y_sum = sb("y_sum", [P, HALF], c=ssd)
        sq_junk = sb("sq_junk", [P, HALF], c=ssd)
        y_t = sb("y_t", [P, 2, XG, P], c=ssd)
        g_conv = sb("g_conv", [P, CONV + 1, XG + 2], c=ssd)
        g_dt = sb("g_dt", [P, NT, HPG], c=ssd)
        g_hi = sb("g_hi", [P, NT, HPG], c=ssd)
        g_lo = sb("g_lo", [P, NT, HPG], c=ssd)
        g_dA = sb("g_dA", [P, NT, HPG], c=ssd)
        decays = sb("decays", [P, 3, NT, HPG], c=ssd)
        g_in, g_out, g_chunk = (decays[:, i, :, :] for i in range(3))
        g_skip = sb("g_skip", [P, HPG], c=ssd)
        g_gain = sb("g_gain", [P, XG], c=ssd)
        ssd.close()
        base.close()

        mixp = ExitStack()
        r2 = sb("r2", [P, NT, DM], c=mixp)
        r1 = sb("r1", [P, NT, DM], c=mixp)
        bs_bc = sb("bs_bc", [P, 8, P], c=mixp)
        g_tmp = sb("g_tmp", [P, 2, HALF], c=mixp)
        y_in = sb("y_in", [P, 3, 4 * HALF], c=mixp)
        gate_in = sb("gate_in", [P, 3, SEQ], c=mixp)
        junk2 = sb("junk2", [P, DM], c=mixp)
        mixp.close()
        keep.close()

        later = ExitStack()
        pad = sb("ws_t_place", [P, 8, P], c=later)
        r2_ = sb("r2_place", [P, NT, DM], c=later)
        r1_ = sb("r1_place", [P, NT, DM], c=later)
        kv = ExitStack()
        k_t = sb("k_t", [P, 8, MEM], c=kv)
        v_tok = sb("v_tok", [P, 2, DM], c=kv)
        memp = ExitStack()
        mem_tok = sb("mem_tok", [P, 2, DM], c=memp)
        mem_hi = sb("mem_hi", [P, KT, MEM], F32R, memp)
        mem_lo = sb("mem_lo", [P, KT, MEM], F32R, memp)
        post_gain = sb("post_gain", [P, DM], c=memp)
        junk3 = sb("junk3", [P, DM], c=memp)
        memp.close()
        att = ExitStack()
        q_t = sb("q_t", [P, 2, SEQ], c=att)
        prob = sb("prob", [P, NT, MEM], c=att)
        prob_t = sb("prob_t", [P, 2, SEQ], c=att)
        a_max = sb("a_max", [P, 8], c=att)
        a_nm = sb("a_nm", [P, 8], c=att)
        a_sum = sb("a_sum", [P, 8], c=att)
        a_rec = sb("a_rec", [P, 8], c=att)
        att.close()
        post2 = ExitStack()
        post_gain2 = sb("post_gain2", [P, DM], c=post2)
        junk4 = sb("junk4", [P, DM], c=post2)
        post2.close()
        kv.close()
        ffn = ExitStack()
        up_raw = sb("up_raw", [P, 2, FFN_CONV - 1 + SEQ], c=ffn)
        up_a = sb("up_a", [P, SEQ], c=ffn)
        up_b = sb("up_b", [P, SEQ], c=ffn)
        f_hi = sb("f_hi", [P, 2, SEQ], F32R, ffn)
        f_lo = sb("f_lo", [P, 2, SEQ], F32R, ffn)
        ffn.close()
        post3 = ExitStack()
        post_gain3 = sb("post_gain3", [P, DM], c=post3)
        junk5 = sb("junk5", [P, DM], c=post3)
        post3.close()
        later.close()

        bank = [ctx.enter_context(nc.psum_tensor(f"bank{i}", [P, HALF], F32)) for i in range(8)]

        w_in = [sem(f"w_in{i}") for i in range(2)]
        w_hi_done = sem("w_hi_done")
        w_split = sem("w_split")
        w_begun = sem("w_begun")
        sp_held = sem("sp_held")
        held = sem("held")
        masks = sem("masks")
        rows_in, x_in, ws_in, dt_in = sem("rows_in"), sem("x_in"), sem("ws_in"), sem("dt_in")
        c_tr, c_ev = sem("c_tr"), sem("c_ev")
        n_sq, n_var, n_rt, n_xs = sem("n_sq"), sem("n_var"), sem("n_rt"), sem("n_xs")
        n_tr, n_hi, n_lo = sem("n_tr"), sem("n_hi"), sem("n_lo")
        dt_w, dt_mm, dt_dve, dt_act, dt_cum, dt_exp = [sem(f"dt_{n}") for n in ("w", "mm", "dve", "act", "cum", "exp")]
        z_mm, z_ev, t_mm, t_ev, cv, sl, xt, xe = [sem(n) for n in ("z_mm", "z_ev", "t_mm", "t_ev", "cv", "sl", "xt", "xe")]
        g_mm, g_ev = sem("g_mm"), sem("g_ev")
        g_st = [sem(f"g_st{i}") for i in range(2)]
        y_st = [sem(f"y_st{i}") for i in range(2)]
        gc = sem("group_consts")
        xd_s, sk, rh, seg, ex, cb, sc, xdd_s = [sem(n) for n in ("xd_done", "skip_done", "rh", "seg", "ex", "cb", "sc", "xdd_done")]
        yd, yo, st, pv, yy, sq, ysv, ysr, ys, yt, ye = [sem(n) for n in ("yd", "yo", "st", "pv", "yy", "sq", "ysv", "ysr", "ys", "yt", "ye")]
        v_mm, v_ev, v_sq, v_var, v_rt, v_sc = [sem(n) for n in ("v_mm", "v_ev", "v_sq", "v_var", "v_rt", "v_sc")]
        gate_ld = [sem(f"gate_ld{i}") for i in range(3)]
        m_mm, m_ev, b_cp = [sem(n) for n in ("m_mm", "m_ev", "b_cp")]
        bs_in = sem("bs_in")
        b_mm, b_ev, b_hi, b_lo = [sem(n) for n in ("b_mm", "b_ev", "b_hi", "b_lo")]
        y_ld = [sem(f"y_ld{i}") for i in range(3)]
        s_hi, s_lo = sem("s_hi"), sem("s_lo")
        o_mm, o_ev, o_sq, o_var, o_rt, o_y, o_x = [sem(n) for n in ("o_mm", "o_ev", "o_sq", "o_var", "o_rt", "o_y", "o_x")]
        gain_in, xr_in, mem_in = sem("gain_in"), sem("xr_in"), sem("mem_in")
        k_mm, k_ev = sem("k_mm"), sem("k_ev")
        q_mm, q_ev, s_mm, a_mx, a_ex, a_pn, a_tr, a_te, p_mm, p_ev = [sem(n) for n in ("q_mm", "q_ev", "s_mm", "a_mx", "a_ex", "a_pn", "a_tr", "a_te", "p_mm", "p_ev")]
        f_mm, f_ev, f_cv, f_gl, f_h, f_l, d_mm, d_ad = [sem(n) for n in ("f_mm", "f_ev", "f_cv", "f_gl", "f_h", "f_l", "d_mm", "d_ad")]
        out_st = sem("out_st")

        LEAD = 1
        Y_LEAD = LEAD + NT

        def nth(g, per, k):
            return g * per + (k + LEAD)

        def yth(g, k):
            return g * NT + (k + Y_LEAD)

        LAST = GROUPS - 1
        GC = 9

        def bc(ap, shape):
            return ap.unsqueeze(2).to_broadcast(shape)

        def wcols(slot, k):
            return w_hi[:, slot, k * P:(k + 1) * P], w_lo[:, slot, k * P:(k + 1) * P]

        def channels_half(slot, half, bk, first_inc, hi=act_hi, lo=act_lo, n=HALF, before=None):
            for kt in range(KT):
                if before:
                    before(kt)
                wh, wl = wcols(slot, kt)
                ah, al = (t[:, kt, half * n:(half + 1) * n] for t in (hi, lo))
                for i, (w, x) in enumerate(((wh, ah), (wh, al), (wl, ah))):
                    m = nc.tensor.matmul(bank[bk][:, 0:n], w, x, start=kt == 0 and i == 0,
                                         stop=kt == KT - 1 and i == 2)
                    if first_inc and kt == 0 and i == 0:
                        m.then_inc(w_begun, 1)
            return m

        def tokens_tile(slot, part, done, tiles=NT, hi=act_hi, lo=act_lo, free=None, bk0=0, ready=None):
            for kk in range(2):
                kt = 2 * part + kk
                wh, wl = (w[:, slot, kk * HALF:(kk + 1) * HALF] for w in (w_hi, w_lo))
                for t in range(tiles):
                    if ready and t % 4 == 0:
                        ready(kt, t // 4)
                    if kt == 0 and free:
                        free(t)
                    ah, al = (x[:, kt, t * P:(t + 1) * P] for x in (hi, lo))
                    for i, (x, w) in enumerate(((ah, wh), (ah, wl), (al, wh))):
                        m = nc.tensor.matmul(bank[bk0 + t][:, :], x, w, start=kt == 0 and i == 0,
                                             stop=kt == KT - 1 and i == 2)
                        if kk == 0 and t == 0 and i == 0:
                            m.then_inc(w_begun, 1)
                    if kt == KT - 1:
                        m.then_inc(done, 1)

        SPLITS = [(0, kt, 0, SEQ) for kt in range(KT)]
        SPLITS += [(p, kt, h * HALF, HALF) for p in (1, 2, 3) for h in range(2) for kt in range(KT)]

        def splits_done(p, h, kt):
            return kt + 1 if p == 0 else 8 + 16 * (p - 1) + 8 * h + kt + 1

        def split_source(k):
            p, kt, c0, n = SPLITS[k]
            if p == 0:
                return y_in[:, kt // 2 % 3, (kt % 2) * SEQ:(kt % 2 + 1) * SEQ]
            if p == 1:
                m = 4 + (k - 8) // 4
                return y_in[:, m % 3, (kt % 4) * HALF:(kt % 4 + 1) * HALF]
            if p == 2:
                return r2[:, c0 // P:c0 // P + 4, kt * P:(kt + 1) * P]
            return r1[:, kt, c0:c0 + n]

        def split_part(k, x):
            p, kt, c0, n = SPLITS[k]
            ap = x[:, kt, c0:c0 + n]
            return ap.rearrange("p (c t) -> p c t", t=P) if p == 2 else ap

        block = ctx.enter_context(nc.Block())

        @block.sync
        def _(sp):
            x_v = a["x"][0].rearrange("(t p) d -> p t d", p=P)
            for h in range(2):
                sp.dma_start(x_tok[:, 4 * h:4 * h + 4, :], x_v[:, 4 * h:4 * h + 4, :]).then_inc(x_in, 16)
            sp.dma_start(dtw[:, :, :], a["w_in"][0, :, DT_OFF:DT_OFF + HEADS].rearrange("(k p) c -> p k c", p=P)).then_inc(dt_in, 16)

            def load(i, slot, src, dst=None):
                if not (isinstance(i, int) and i < 2):
                    sp.wait_ge(w_split, i - 1)
                if not isinstance(i, int):
                    sp.sem_inc(sp_held, 1)
                sp.dma_start(w_raw[:, slot, :] if dst is None else dst, src).then_inc(w_in[slot], 16)

            def channel_tile(w, col):
                return w[:, bass.ds(col, P)].rearrange("(k p) c -> p k c", p=P)

            def token_tile(w, part, col):
                return w[2 * part * P:2 * (part + 1) * P, bass.ds(col, HALF)].rearrange("(k p) c -> p k c", p=P)

            def raw(slot, k):
                return w_raw[:, slot, :].rearrange("p (k c) -> p k c", k=k)

            win = a["w_in"][0]

            def ssd_cols(g):
                cols = [XBC_OFF + g * HALF + P * j for j in range(XG)]
                cols += [XBC_OFF + 2048 + g * P, XBC_OFF + 2560 + g * P]
                return cols + [off + g * 2 * P + P * j for off in (GA_OFF, GB_OFF, U_OFF) for j in range(2)]

            def ssd_loads(g, start=0):
                for j in range(start, SSD_TILES):
                    i = g * SSD_TILES + j
                    if j < 4:
                        load(i, j % 2, token_tile(win, j, Z_OFF + g * HALF), raw(j % 2, 2))
                    else:
                        load(i, j % 2, channel_tile(win, ssd_cols(g)[j - 4]), raw(j % 2, KT))

            ssd_loads(0)
            with sp.Fori(1, GROUPS) as g:
                ssd_loads(g)

            def token_loads(i0, w, col0=0):
                for n in range(2):
                    for part in range(4):
                        load(i0 + 4 * n + part, part % 2, token_tile(w, part, col0 + n * HALF), raw(part % 2, 2))

            def channel_loads(i0, w):
                for j in range(8):
                    load(i0 + j, j % 2, channel_tile(w, j * P), raw(j % 2, KT))

            token_loads(W_V, win, V_OFF)
            channel_loads(W_BRANCH, a["w_branch_b"][0, 0:DM, :])
            channel_loads(W_BRANCH + 8, a["w_branch_b"][0, DM:2 * DM, :])
            channel_loads(W_BRANCH + 16, a["w_branch_a"][0])
            token_loads(W_OUT, a["w_out"][0])
            channel_loads(W_K, a["xa_w_kv"][0, :, 0:DM])
            token_loads(W_VM, a["xa_w_kv"][0], DM)
            channel_loads(W_Q, a["xa_w_q"][0])
            token_loads(W_O, a["xa_w_o"][0])

            up, down = a["ffn_w_up"][0], a["ffn_w_down"][0]

            def up_loads(i, step, pair):
                col = step * 2 * P + pair * P
                load(i, 0, channel_tile(up, col), raw(0, KT))
                load(i + 1, 1, channel_tile(up, col + FFN_TILES * P), raw(1, KT))

            def down_loads(i, step):
                rows_v = down[bass.ds(step * 2 * P, 2 * P), :].rearrange("(k p) c -> p k c", p=P)
                for n in range(2):
                    load(i + n, n, rows_v[:, :, n * HALF:(n + 1) * HALF], raw(n, 2))

            up_loads(W_FFN, 0, 0)
            up_loads(W_FFN + 2, 0, 1)
            with sp.Fori(1, FFN_STEPS) as s:
                i = s * FFN_W + (W_FFN - 2)
                up_loads(i, s, 0)
                down_loads(i + 2, s - 1)
                up_loads(i + 4, s, 1)
            down_loads(W_FFN + 4 + (FFN_STEPS - 1) * FFN_W, FFN_STEPS - 1)

            out_v = out[0].rearrange("(t p) d -> p t d", p=P)
            for t in range(NT):
                sp.wait_ge(o_x, 16 + t + 1)
                sp.dma_start(out_v[:, t, :], r1[:, t, :]).then_inc(out_st, 16)
            sp.wait_ge(out_st, 16 * NT)

        @block.gpsimd
        def _(pool):
            nc.gpsimd.memset(ident[:, :], 0.0).then_inc(masks, 1)
            nc.gpsimd.memset(tri[:, :], 1.0).then_inc(masks, 1)
            nc.gpsimd.memset(after[:, :], 1.0).then_inc(masks, 1)
            nc.gpsimd.memset(ones[:, :], 1.0).then_inc(masks, 1)
            pool.wait_ge(masks, 4)
            nc.gpsimd.affine_select(out=ident[:, :], in_=ident[:, :], compare_op=ALU.not_equal, fill=1.0,
                                    base=0, pattern=[[-1, P]], channel_multiplier=1).then_inc(masks, 1)
            nc.gpsimd.affine_select(out=tri[:, :], in_=tri[:, :], compare_op=ALU.is_ge, fill=0.0,
                                    base=0, pattern=[[1, P]], channel_multiplier=-1).then_inc(masks, 1)
            nc.gpsimd.affine_select(out=after[:, :], in_=after[:, :], compare_op=ALU.is_gt, fill=0.0,
                                    base=0, pattern=[[-1, P]], channel_multiplier=1).then_inc(masks, 1)

            pool.sem_inc(rh, LEAD)

            def split(i, slot, loads):
                pool.wait_ge(w_begun, i + LEAD)
                pool.wait_ge(w_in[slot], loads * 16)
                if not isinstance(i, int):
                    pool.sem_inc(held, 1)
                nc.gpsimd.tensor_scalar(w_hi[:, slot, :], w_raw[:, slot, :], 1.0, 1.0, ALU.mult, ALU.mult).then_inc(w_hi_done, 1)
                pool.wait_ge(w_hi_done, i + 1)
                nc.gpsimd.tensor_tensor(w_lo[:, slot, :], w_raw[:, slot, :], w_hi[:, slot, :].bitcast(F32),
                                        ALU.subtract).then_inc(w_split, 1)

            def triangle(g, c):
                for h in range(2):
                    if c:
                        pool.wait_ge(seg, g * 16 + (2 * (c - 1) + h + 1))
                    else:
                        pool.wait_ge(gc, nth(g, GC, GC))
                    for dst, src in ((tri_hi, g_hi), (tri_lo, g_lo)):
                        nc.gpsimd.tensor_tensor(dst[:, h, :].rearrange("p (r l) -> p r l", l=P),
                                                bc(src[:, c, 4 * h:4 * h + 4], [P, 4, P]),
                                                tri[:, :].unsqueeze(1).to_broadcast([P, 4, P]), ALU.mult).then_inc(rh, 1)

            with pool.Fori(0, GROUPS) as g:
                def ssd_split(j):
                    split(g * SSD_TILES + j, j % 2, g * (SSD_TILES // 2) + (j // 2 + 1))
                for j in range(11):
                    ssd_split(j)
                triangle(g, 0)
                ssd_split(11)
                triangle(g, 1)
                ssd_split(12)
                triangle(g, 2)
                triangle(g, 3)
                ssd_split(13)
                triangle(g, 4)
                triangle(g, 5)
                ssd_split(14)
                triangle(g, 6)
                triangle(g, 7)
                ssd_split(15)

            def splits(i0, i1):
                with pool.Fori(i0 // 2, i1 // 2) as j:
                    for s in range(2):
                        split(j * 2 + s, s, j + 1)
            splits(W_V, W_FFN + FFN_STEPS * FFN_W)

        @block.tensor
        def _(pe):
            pe.sem_inc(yd, LEAD)
            pe.sem_inc(w_begun, LEAD)
            pe.wait_ge(masks, 7)
            pe.wait_ge(rows_in, 16 * ROW_LOADS)
            for r, n in enumerate(ROW_COUNTS):
                m = nc.tensor.transpose(bank[0][:, r * P:r * P + n], rows[0:n, r, :], ident[0:n, 0:n])
            m.then_inc(c_tr, 1)
            pe.wait_ge(ws_in, 16)
            for h in range(2):
                for i in range(4):
                    m = nc.tensor.transpose(bank[1 + h][:, i * P:(i + 1) * P], ws_rows[:, 4 * h + i, :], ident[:, :])
                m.then_inc(c_tr, 1)

            def norm_transposes(u, src, free=None):
                tiles = NORM_TILES[u]
                per = min(4, tiles)
                for h in range(tiles // per):
                    pe.wait_ge(n_xs, NORM_T0[u] + per * (h + 1))
                    for kt in range(KT):
                        q = h * KT + kt
                        if q >= 8:
                            pe.wait_ge(n_lo, NORM_G0[u] + q - 7)
                        elif free:
                            free(q)
                        for i in range(per):
                            m = nc.tensor.transpose(bank[q % 8][:, i * P:(i + 1) * P],
                                                    src[:, h * per + i, kt * P:(kt + 1) * P], ident[:, :])
                        m.then_inc(n_tr, 1)

            pe.wait_ge(c_ev, 6)
            norm_transposes(PRE_X, x_tok)

            pe.wait_ge(n_lo, NORM_G0[1])
            pe.wait_ge(dt_w, 2)
            for t in range(NT):
                for kt in range(KT):
                    ah, al = (x[:, kt, t * P:(t + 1) * P] for x in (act_hi, act_lo))
                    for i, (x, w) in enumerate(((ah, dtw_hi), (ah, dtw_lo), (al, dtw_hi))):
                        m = nc.tensor.matmul(bank[0][:, t * HEADS:(t + 1) * HEADS], x, w[:, kt, :],
                                             start=kt == 0 and i == 0, stop=kt == KT - 1 and i == 2)
            m.then_inc(dt_mm, 1)

            def seg_and_cb(g, c):
                for h in range(2):
                    pe.wait_ge(rh, nth(g, 32, 4 * c + 2 * h + 2))
                    pe.wait_ge(ex, nth(g, 16, 2 * c + h - 1 if c else 0))
                    for i, t in enumerate((tri_hi, tri_lo)):
                        m = nc.tensor.matmul(bank[4 + h][:, :], after_r[:, :], t[:, h, :], start=i == 0, stop=i == 1)
                    m.then_inc(seg, 1)
                pe.wait_ge(sc, nth(g, 24, 3 * c - 2 if c else 0))
                nc.tensor.matmul(bank[3][:, 0:P], b_t[:, c * P:(c + 1) * P], c_t[:, c * P:(c + 1) * P],
                                 start=True, stop=True).then_inc(cb, 1)

            def chunk_products(g, c):
                pe.wait_ge(sc, nth(g, 24, 3 * c + 3))
                pe.wait_ge(xd_s, nth(g, 8, c + 1))
                pe.wait_ge(yy, nth(g, 32, 4 * c - 2 if c else 0))
                for r in range(HPG):
                    m = nc.tensor.matmul(bank[6][:, r * HD:(r + 1) * HD],
                                         scores[:, r // 4, (r % 4) * P:(r % 4 + 1) * P],
                                         xd[:, c % 2, r * HD:(r + 1) * HD], start=True, stop=True)
                m.then_inc(yd, 1)
                pe.wait_ge(pv, nth(g, 17, 2 * c + 1))
                nc.tensor.matmul(bank[7][:, :], c_t[:, c * P:(c + 1) * P], state[:, :],
                                 start=True, stop=True).then_inc(yo, 1)
                pe.wait_ge(xdd_s, nth(g, 8, c + 1))
                nc.tensor.matmul(bank[2][:, :], b_tok[:, c, :], xdd[:, :], start=True, stop=True).then_inc(st, 1)

            def gate_half(g, q):
                j = 10 + q // 2
                if q % 2 == 0:
                    pe.wait_ge(w_split, g * SSD_TILES + (j + 1))
                if q < 2:
                    pe.wait_ge(t_ev, nth(g, 12, 9 + q))
                else:
                    pe.wait_ge(g_ev, nth(g, 12, q - 1))
                channels_half(j % 2, q % 2, q % 2, q % 2 == 0).then_inc(g_mm, 1)

            def to_tokens(g, idx):
                pe.wait_ge(sl, nth(g, 6, idx + 1))
                for h in range(2):
                    q = 2 * idx + h
                    pe.wait_ge(xe, nth(g, 10, max(0, q - 3)))
                    for i in range(4):
                        c = 4 * h + i
                        src = b_t if idx == XG else conv
                        m = nc.tensor.transpose(bank[4 + q % 4][:, i * P:(i + 1) * P], src[:, c * P:(c + 1) * P], ident[:, :])
                    m.then_inc(xt, 1)

            def ssd_group(g):
                def z_free(t):
                    pe.wait_ge(ye, yth(g, t + 1) - NT)
                for part in range(4):
                    pe.wait_ge(w_split, g * SSD_TILES + (part + 1))
                    tokens_tile(part % 2, part, z_mm, free=z_free)
                for idx in range(6):
                    pe.wait_ge(w_split, g * SSD_TILES + (4 + idx + 1))
                    for h in range(2):
                        b = 2 * (idx % 2) + h
                        if idx < 2:
                            pe.wait_ge(z_ev, nth(g, 8, b + 1))
                        else:
                            pe.wait_ge(t_ev, nth(g, 12, 2 * (idx - 2) + h + 1))
                        channels_half(idx % 2, h, b, h == 0).then_inc(t_mm, 1)
                    if idx == 0:
                        pe.wait_ge(z_ev, nth(g, 8, 8))
                        pe.wait_ge(gc, nth(g, GC, GC))
                        for i, mask in enumerate((tri, after, ones)):
                            m = nc.tensor.matmul(bank[7][:, i * NT * HPG:(i + 1) * NT * HPG], mask[:, :],
                                                 g_dA[:, :, :].rearrange("p c h -> p (c h)"), start=True, stop=True)
                        m.then_inc(dt_cum, 1)
                    if idx == 2:
                        pe.wait_ge(dt_exp, g + 1)
                    if idx >= 1:
                        to_tokens(g, idx - 1)
                for q in range(2):
                    gate_half(g, q)
                pe.wait_ge(xe, nth(g, 10, 10))
                pe.wait_ge(t_ev, nth(g, 12, 12))
                pe.wait_ge(sl, nth(g, 6, 6))
                seg_and_cb(g, 0)
                for c in range(NT):
                    gate_half(g, c + 2)
                    chunk_products(g, c)
                    if c + 1 < NT:
                        seg_and_cb(g, c + 1)
                for q in range(NT + 2, 12):
                    gate_half(g, q)
                for c in range(NT):
                    pe.wait_ge(ys, nth(g, 8, c + 1))
                    if c < 2:
                        pe.wait_ge(g_ev, nth(g, 12, 11 + c))
                    for i in range(XG):
                        m = nc.tensor.transpose(bank[c][:, i * P:(i + 1) * P], xs[:, c, i * P:(i + 1) * P], ident[:, :])
                    m.then_inc(yt, 1)

            pe.wait_ge(dt_dve, 1)
            with pe.Fori(0, GROUPS) as g:
                ssd_group(g)

            for n in range(2):
                def v_free(t, n=n):
                    if n:
                        pe.wait_ge(v_ev, t + 1)
                    else:
                        pe.wait_ge(ye, yth(LAST, t + 1))
                for part in range(4):
                    pe.wait_ge(w_split, W_V + 4 * n + part + 1)
                    tokens_tile(part % 2, part, v_mm, free=v_free)

            def mix(g):
                for h in range(2):
                    q = 2 * g + h
                    if q >= 4:
                        pe.wait_ge(m_ev, 2 * (q - 4) + 1)
                    for i in range(4):
                        m = nc.tensor.matmul(bank[4 + q % 4][:, i * P:(i + 1) * P],
                                             r2[:, 4 * h + i, g * P:(g + 1) * P], ws_t[:, g, :],
                                             start=True, stop=True)
                    m.then_inc(m_mm, 1)

            for part in range(3):
                for j in range(8):
                    pe.wait_ge(w_split, W_BRANCH + 8 * part + j + 1)
                    for h in range(2):
                        r = 16 * part + 2 * j + h
                        if r < 4:
                            pe.wait_ge(v_ev, 8 + r + 1)
                        elif r < 20:
                            pe.wait_ge(b_cp, r - 3)
                        else:
                            pe.wait_ge(b_ev, 2 * (r - 4 - 16) + 1)

                        def ready(kt, part=part, j=j, h=h):
                            if j == 0 and (part or h == 0):
                                pe.wait_ge(b_lo, splits_done(part, h, kt))
                        channels_half(j % 2, h, r % 4, h == 0, before=ready).then_inc(b_mm, 1)
                        if part == 0 and r >= 8:
                            if r == 8:
                                pe.wait_ge(v_sc, 8)
                            mix(r - 8)

            def out_product(u, i0, free0, between=None):
                for n in range(2):
                    def free(t, n=n):
                        if n and not between:
                            pe.wait_ge(o_ev, 16 * u + t + 1)
                        elif n:
                            pe.wait_ge(n_lo, NORM_G0[PRE_MEM_TOK] + t + 1)
                        else:
                            free0(t)

                    def ready(kt, h, n=n):
                        if n == 0 and u == 0:
                            pe.wait_ge(b_lo, splits_done(3, h, kt))
                        elif n == 0 and h == 0:
                            pe.wait_ge(s_lo, kt + 1)
                    for part in range(4):
                        pe.wait_ge(w_split, i0 + 4 * n + part + 1)
                        tokens_tile(part % 2, part, o_mm, free=free, ready=ready)
                    if n == 0 and between:
                        between()

            def mem_free(q):
                pe.wait_ge(o_ev, q + 1)
            out_product(0, W_OUT, lambda t: pe.wait_ge(b_ev, 32 + 2 * (12 + t % 4) + 1),
                        lambda: norm_transposes(PRE_MEM_TOK, mem_tok, mem_free))

            for j in range(8):
                pe.wait_ge(w_split, W_K + j + 1)
                pe.wait_ge(o_ev, 8 + j + 1)
                channels_half(j % 2, 0, j, True, mem_hi, mem_lo, MEM).then_inc(k_mm, 1)
            for n in range(2):
                for part in range(4):
                    pe.wait_ge(w_split, W_VM + 4 * n + part + 1)
                    tokens_tile(part % 2, part, k_mm, 2, mem_hi, mem_lo,
                                free=lambda t, n=n: pe.wait_ge(k_ev, 2 * n + t + 1), bk0=2 * n)
            pe.wait_ge(k_ev, 12)
            norm_transposes(PRE_MEM, r2)

            def queries(h):
                for d in range(2):
                    pe.wait_ge(w_split, W_Q + 2 * h + d + 1)
                    for half in range(2):
                        r = 4 * h + 2 * d + half
                        if h:
                            pe.wait_ge(q_ev, r - 3)

                        channels_half(d, half, 2 * d + half, half == 0).then_inc(q_mm, 1)

            pe.wait_ge(n_lo, NORM_G0[PRE_FFN])
            queries(0)
            for h in range(XH):
                pe.wait_ge(q_ev, 4 * h + 4)
                for t in range(NT):
                    b = 4 + t // 2
                    if h and t % 2 == 0:
                        pe.wait_ge(p_ev, 4 * (h - 1) + t // 2 + 1)
                    for d in range(2):
                        m = nc.tensor.matmul(bank[b][:, (t % 2) * MEM:(t % 2 + 1) * MEM], q_t[:, d, t * P:(t + 1) * P],
                                             k_t[:, 2 * h + d, :], start=d == 0, stop=d == 1)
                    if t % 2:
                        m.then_inc(s_mm, 1)
                if h + 1 < XH:
                    queries(h + 1)
                pe.wait_ge(a_pn, 9 * h + 9)
                for q in range(4):
                    for i in range(4):
                        t = 4 * (q % 2) + i
                        m = nc.tensor.transpose(bank[4 + q][:, i * P:(i + 1) * P],
                                                prob[:, t, (q // 2) * P:(q // 2 + 1) * P], ident[:, :])
                    m.then_inc(a_tr, 1)
                pe.wait_ge(a_te, 4 * h + 4)
                for q in range(4):
                    d, half = q // 2, q % 2
                    for mt in range(2):
                        m = nc.tensor.matmul(bank[4 + q][:, :], v_tok[:, mt, h * XHD + d * P:h * XHD + (d + 1) * P],
                                             prob_t[:, mt, half * HALF:(half + 1) * HALF], start=mt == 0, stop=mt == 1)
                    m.then_inc(p_mm, 1)
            out_product(1, W_O, lambda t: pe.wait_ge(p_ev, 16) if t >= 4 else pe.wait_ge(q_ev, 16))
            norm_transposes(PRE_FFN, r2, lambda q: pe.wait_ge(o_ev, 32))
            pe.wait_ge(n_lo, NORM_G0[PRE_FFN] + 16)

            def up_products(i, u, first=False):
                for w in range(2):
                    pe.wait_ge(w_split, i + (w + 1))
                    for half in range(2):
                        b = 2 * w + half
                        if not first:
                            pe.wait_ge(f_ev, u * 4 + (b - 3))
                        channels_half(w, half, b, half == 0).then_inc(f_mm, 1)

            def down_products(i, step):
                pe.wait_ge(f_l, step * 2 + 2)
                for n in range(2):
                    pe.wait_ge(w_split, i + (n + 1))
                    for t in range(NT):
                        r = 8 * n + t
                        pe.wait_ge(d_ad, step * 16 + (r + 1))
                        for k in range(2):
                            fh, fl = (x[:, k, t * P:(t + 1) * P] for x in (f_hi, f_lo))
                            wh, wl = (w[:, n, k * HALF:(k + 1) * HALF] for w in (w_hi, w_lo))
                            for j, (x, w) in enumerate(((fh, wh), (fh, wl), (fl, wh))):
                                m = nc.tensor.matmul(bank[4 + r % 4][:, :], x, w, start=k == 0 and j == 0,
                                                     stop=k == 1 and j == 2)
                                if t == 0 and k == 0 and j == 0:
                                    m.then_inc(w_begun, 1)
                        m.then_inc(d_mm, 1)

            up_products(W_FFN, 0, True)
            up_products(W_FFN + 2, 1)
            with pe.Fori(1, FFN_STEPS) as s:
                i = s * FFN_W + (W_FFN - 2)
                up_products(i, s * 2)
                down_products(i + 2, s - 1)
                up_products(i + 4, s * 2 + 1)
            down_products(W_FFN + 4 + (FFN_STEPS - 1) * FFN_W, FFN_STEPS - 1)

        @block.scalar
        def _(act):
            A = nc.scalar.activation
            for s in (z_ev, t_ev, sl, g_ev, ex, sq):
                act.sem_inc(s, LEAD)
            for s in (*g_st, *y_st):
                act.sem_inc(s, 16)

            def row_load(dst, src):
                act.dma_start(dst, src).then_inc(rows_in, 16)
            row_load(rows[0:96, 0, :], a["ssd_conv_w"][0].rearrange("k (j p) -> (k j) p", p=P))
            row_load(rows[96:120, 0, :], a["ssd_conv_b"][0].rearrange("(j p) -> j p", p=P))
            row_load(rows[0:88, 1, :], a["ffn_conv_w"][0, 0:2].rearrange("k (j p) -> (k j) p", p=P))
            row_load(rows[0:44, 2, :], a["ffn_conv_w"][0, 2].rearrange("(j p) -> j p", p=P))
            row_load(rows[44:88, 2, :], a["ffn_conv_b"][0].rearrange("(j p) -> j p", p=P))
            for i, n in enumerate(GAIN_ROWS):
                row_load(rows[8 * i:8 * i + 8, 3, :], a[n][0].rearrange("(j p) -> j p", p=P))
            row_load(rows[40:56, 3, :], a["ssd_norm"][0].rearrange("(j p) -> j p", p=P))
            act.dma_start(ws_rows[:, :, :], a["gm_w_s"][0].rearrange("g t s -> t g s")).then_inc(ws_in, 16)
            for dst, n in ((dt_bias, "ssd_dt_bias"), (a_log, "ssd_a_log"), (d_skip, "ssd_d")):
                act.dma_start(dst[:, :], a[n][0].partition_broadcast(P)).then_inc(dt_in, 16)

            def squares(u, h, src, jk, wait=None):
                per = min(4, NORM_TILES[u])
                for t in range(per * h, per * (h + 1)):
                    if wait:
                        wait(t)
                    if NORM_T0[u] + t:
                        act.wait_ge(n_sq, NORM_T0[u] + t)
                    A(jk[:, :], src[:, t, :], ACT.Square, accum_out=stat[:, t:t + 1]).then_inc(n_sq, 1)

            def root(u, h):
                per = min(4, NORM_TILES[u])
                act.wait_ge(n_var, 2 * (NORM_H0[u] + h) + 2)
                A(stat_s[:, per * h:per * (h + 1)], stat_r[:, per * h:per * (h + 1)], ACT.Sqrt).then_inc(n_rt, 1)

            def highs(u, gain0, hi):
                per = min(4, NORM_TILES[u])
                for q in range(NORM_TILES[u] // per * KT):
                    h, kt = q // KT, q % KT
                    act.wait_ge(n_tr, NORM_G0[u] + q + 1)
                    A(hi[:, kt, h * per * P:(h + 1) * per * P], bank[q % 8][:, 0:per * P], ACT.Copy,
                      scale=consts[:, 3, gain0 + kt:gain0 + kt + 1]).then_inc(n_hi, 1)

            for h in range(2):
                squares(PRE_X, h, x_tok, junk, lambda t: act.wait_ge(x_in, 32))
            for h in range(2):
                root(PRE_X, h)
            act.wait_ge(c_ev, 4)
            highs(PRE_X, 0, act_hi)

            act.wait_ge(dt_dve, 1)
            A(dt_abs[:, :, :], dt_x[:, :, :], ACT.Abs).then_inc(dt_act, 1)
            act.wait_ge(dt_act, 1)
            A(dt_e[:, :, :], dt_abs[:, :, :], ACT.Exp, scale=-1.0).then_inc(dt_act, 1)
            A(neg_a[:, :], a_log[:, :], ACT.Exp).then_inc(dt_act, 1)

            def gate_evac(g, q):
                act.wait_ge(g_st[q % 2], g * 96 + (16 * (q // 2) + 16))
                act.wait_ge(g_mm, nth(g, 12, q + 1) - LEAD)
                A(gate_out[:, q % 2, :], bank[q % 2][:, :], ACT.Sigmoid if q < 8 else ACT.Gelu_apprx_tanh).then_inc(g_ev, 1)
                act.wait_ge(g_ev, nth(g, 12, q + 1))
                tile = g * 2 + ((q // 4) * 8 + q // 2 % 2)
                act.dma_start(gates_dram[bass.ds(tile, 1), :, (q % 2) * HALF:(q % 2 + 1) * HALF].rearrange("j p t -> p (j t)"),
                              gate_out[:, q % 2, :]).then_inc(g_st[q % 2], 16)

            def ssd_group(g):
                for t in range(NT):
                    act.wait_ge(z_mm, g * 8 + (t + 1))
                    A(zs[:, t, :], bank[t][:, :], ACT.Silu).then_inc(z_ev, 1)

                def silu(idx):
                    act.wait_ge(cv, nth(g, 24, 4 * idx + 4))
                    dst = conv if idx < XG else b_t if idx == XG else c_t
                    A(dst[:, :], conv[:, :], ACT.Silu).then_inc(sl, 1)
                for idx in range(6):
                    for h in range(2):
                        if h and idx:
                            silu(idx - 1)
                        act.wait_ge(t_mm, g * 12 + (2 * idx + h + 1))
                        if h == 0:
                            act.wait_ge(cv, nth(g, 24, max(0, 4 * (idx - 1))))
                        A(xbc_raw[:, idx % 2, CONV - 1 + h * HALF:CONV - 1 + (h + 1) * HALF],
                          bank[2 * (idx % 2) + h][:, :], ACT.Copy).then_inc(t_ev, 1)
                    if idx == 0:
                        act.wait_ge(dt_cum, g + 1)
                        A(decays[:, :, :, :].rearrange("p i c h -> p (i c h)"), bank[7][:, 0:3 * NT * HPG],
                          ACT.Exp).then_inc(dt_exp, 1)
                silu(5)
                for q in range(2):
                    gate_evac(g, q)

                def square(c):
                    act.wait_ge(yy, nth(g, 32, 4 * c + 4))
                    act.wait_ge(sq, nth(g, 8, c))
                    A(sq_junk[:, :], xs[:, c, :], ACT.Square, accum_out=stat[:, c:c + 1]).then_inc(sq, 1)
                for c in range(NT):
                    for h in range(2):
                        act.wait_ge(seg, g * 16 + (2 * c + h + 1))
                        act.wait_ge(yd, nth(g, 8, c))
                        A(scores[:, h, :], bank[4 + h][:, :], ACT.Exp).then_inc(ex, 1)
                    gate_evac(g, c + 2)
                    if c:
                        square(c - 1)
                square(NT - 1)
                act.wait_ge(ysv, g * 2 + 2)
                A(stat_s[:, :], stat_r[:, :], ACT.Sqrt).then_inc(ysr, 1)
                for q in range(NT + 2, 12):
                    gate_evac(g, q)
                for c in range(NT):
                    act.wait_ge(ye, yth(g, c + 1))
                    act.dma_start(ssd_dram[bass.ds(g * XG, XG), :, c * P:(c + 1) * P].rearrange("j p t -> p j t"),
                                  y_t[:, c % 2, :, :]).then_inc(y_st[c % 2], 16)

            act.wait_ge(n_lo, NORM_G0[1])
            act.wait_ge(dt_dve, 16)
            with act.Fori(0, GROUPS) as g:
                ssd_group(g)

            for s in (*g_st,):
                act.wait_ge(s, 16 + 96 * GROUPS)
            for s in (*y_st,):
                act.wait_ge(s, 16 + 64 * GROUPS)
            def gate_load(k):
                if k >= 11:
                    act.wait_ge(b_ev, 4 * (k - 11) + 4)
                elif k >= 3:
                    act.wait_ge(m_ev, 4 * (k - 3) + 4)
                act.dma_start(gate_in[:, k % 3, :], gates_dram[(16, 8, 0)[k // 8] + k % 8]).then_inc(gate_ld[k % 3], 16)

            def y_load(m):
                if m >= 3:
                    act.wait_ge(b_lo, 2 * (m - 3) + 2 if m < 7 else 12)
                if m < 4:
                    src = ssd_dram[2 * m:2 * m + 2].rearrange("j p t -> p j t")
                else:
                    h, k = (m - 4) // 2, 8 + 4 * (m % 2)
                    src = ssd_dram[k:k + 4, :, h * HALF:(h + 1) * HALF].rearrange("j p t -> p j t")
                act.dma_start(y_in[:, m % 3, :].rearrange("p (j t) -> p j t", j=2 if m < 4 else 4), src).then_inc(y_ld[m % 3], 16)

            def high(k):
                p, kt, c0, n = SPLITS[k]
                if p < 2:
                    m = kt // 2 if p == 0 else 4 + (k - 8) // 4
                    act.wait_ge(y_ld[m % 3], 16 * (m // 3 + 1))
                if p == 0:
                    act.wait_ge(w_begun, W_V + 4 + kt // 2 + 2 + LEAD)
                else:
                    act.wait_ge(b_mm, 16 * p - 1 + c0 // HALF)
                if p == 2:
                    act.wait_ge(m_ev, 32)
                if p == 3:
                    act.wait_ge(b_ev, 32 + 2 * (2 * kt + c0 // HALF) + 2)
                A(split_part(k, act_hi), split_source(k), ACT.Copy).then_inc(b_hi, 1)

            for k in range(3):
                y_load(k)
                gate_load(k)
            act.dma_start(bs_bc[:, :, :], a["gm_b_s"][0].partition_broadcast(P)).then_inc(bs_in, 16)

            def v_evac(n):
                for t in range(NT):
                    act.wait_ge(v_mm, 8 * n + t + 1)
                    A(r2[:, t, n * HALF:(n + 1) * HALF], bank[t][:, :], ACT.Gelu_apprx_tanh).then_inc(v_ev, 1)
            v_evac(0)
            for k in range(6):
                high(k)
                if k >= 4:
                    y_load(k - 1)
            v_evac(1)
            high(6)
            high(7)
            for t in range(NT):
                act.wait_ge(v_ev, 8 + t + 1)
                if t:
                    act.wait_ge(v_sq, t)
                A(junk2[:, :], r2[:, t, :], ACT.Square, accum_out=stat[:, t:t + 1]).then_inc(v_sq, 1)
            act.wait_ge(v_var, 2)
            A(stat_s[:, :], stat_r[:, :], ACT.Sqrt).then_inc(v_rt, 1)
            y_load(5)
            y_load(6)

            def branch_evac(r):
                act.wait_ge(b_mm, r + 1)
                A(r1[:, r // 2, (r % 2) * HALF:(r % 2 + 1) * HALF], bank[r % 4][:, :], ACT.Copy).then_inc(b_cp, 1)
                if r >= 9:
                    gate_load(r - 6)
            for r in range(14):
                branch_evac(r)
            for k in range(8, 16):
                high(k)
            branch_evac(14)
            y_load(7)
            for k in range(16, 24):
                high(k)
            branch_evac(15)
            for k in range(10, 18):
                gate_load(k)
            for k in range(24, 32):
                high(k)
            gate_load(18)
            for k in range(32, 40):
                high(k)
            for k in range(19, 24):
                gate_load(k)
            for k in range(40, 56):
                high(k)

            def split_highs(src):
                act.wait_ge(p_ev, 16)
                for kt in range(KT):
                    A(act_hi[:, kt, :], src[:, kt, :], ACT.Copy).then_inc(s_hi, 1)

            act.dma_start(mem_tok[:, :, :], a["mem"][0].rearrange("(t p) d -> p t d", p=P)).then_inc(mem_in, 16)
            act.dma_start(post_gain[:, :], a["norm_post_mix"][0].partition_broadcast(P)).then_inc(gain_in, 16)
            act.wait_ge(b_lo, 56)
            act.dma_start(r1[:, :, :], a["x"][0].rearrange("(t p) d -> p t d", p=P)).then_inc(xr_in, 16)
            squares(PRE_MEM_TOK, 0, mem_tok, junk3, lambda t: act.wait_ge(mem_in, 16))
            root(PRE_MEM_TOK, 0)
            highs(PRE_MEM_TOK, 24, mem_hi)

            def post_stats(u, jk):
                for h in range(2):
                    for t in range(4 * h, 4 * h + 4):
                        if u < 2:
                            act.wait_ge(o_ev, 16 * u + 8 + t + 1)
                        if 8 * u + t:
                            act.wait_ge(o_sq, 8 * u + t)
                        A(jk[:, :], r2[:, t, :], ACT.Square, accum_out=stat[:, t:t + 1]).then_inc(o_sq, 1)
                for h in range(2):
                    act.wait_ge(o_var, 4 * u + 2 * h + 2)
                    A(stat_s[:, 4 * h:4 * h + 4], stat_r[:, 4 * h:4 * h + 4], ACT.Sqrt).then_inc(o_rt, 1)
            post_stats(0, junk3)
            for j in range(8):
                act.wait_ge(k_mm, j + 1)
                A(k_t[:, j, :], bank[j][:, 0:MEM], ACT.Copy).then_inc(k_ev, 1)
            for n in range(2):
                for t in range(2):
                    act.wait_ge(k_mm, 8 + 2 * n + t + 1)
                    A(v_tok[:, t, n * HALF:(n + 1) * HALF], bank[2 * n + t][:, :], ACT.Copy).then_inc(k_ev, 1)
            for h in range(2):
                squares(PRE_MEM, h, r1, junk3, lambda t: act.wait_ge(o_x, t + 1))
            for h in range(2):
                root(PRE_MEM, h)
            highs(PRE_MEM, 8, act_hi)

            def query_evac(h):
                for r in range(4):
                    act.wait_ge(q_mm, 4 * h + r + 1)
                    A(q_t[:, r // 2, (r % 2) * HALF:(r % 2 + 1) * HALF], bank[r][:, :], ACT.Copy).then_inc(q_ev, 1)
            act.wait_ge(n_lo, NORM_G0[PRE_FFN])
            query_evac(0)
            for h in range(XH):
                for t in range(NT):
                    act.wait_ge(a_mx, 5 * h + 5)
                    if h:
                        act.wait_ge(a_tr, 4 * h)
                    A(prob[:, t, :], bank[4 + t // 2][:, (t % 2) * MEM:(t % 2 + 1) * MEM], ACT.Exp,
                      bias=a_nm[:, t:t + 1], scale=XHD ** -0.5, accum_out=a_sum[:, t:t + 1]).then_inc(a_ex, 1)
                if h + 1 < XH:
                    query_evac(h + 1)
                for q in range(4):
                    act.wait_ge(p_mm, 4 * h + q + 1)
                    A(r2[:, 2 * h + q // 2, (q % 2) * HALF:(q % 2 + 1) * HALF], bank[4 + q][:, :], ACT.Copy).then_inc(p_ev, 1)
            split_highs(r2)
            act.wait_ge(s_lo, 8)
            act.dma_start(post_gain2[:, :], a["norm_post_mem"][0].partition_broadcast(P)).then_inc(gain_in, 16)
            post_stats(1, junk4)
            for h in range(2):
                squares(PRE_FFN, h, r1, junk4, lambda t: act.wait_ge(o_x, 8 + t + 1))
            for h in range(2):
                root(PRE_FFN, h)
            highs(PRE_FFN, 16, act_hi)

            def pair(u, step, p, first=False):
                for b in range(4):
                    act.wait_ge(f_mm, u * 4 + (b + 1))
                    if not first:
                        act.wait_ge(f_cv, u * 7 + (-4 if b < 2 else -1))
                    A(up_raw[:, b // 2, FFN_CONV - 1 + (b % 2) * HALF:FFN_CONV - 1 + (b % 2 + 1) * HALF],
                      bank[b][:, :], ACT.Copy).then_inc(f_ev, 1)
                act.wait_ge(f_cv, u * 7 + 3)
                A(up_a[:, :], up_a[:, :], ACT.Gelu_apprx_tanh).then_inc(f_gl, 1)
                act.wait_ge(f_cv, u * 7 + 7)
                if step is not None:
                    act.wait_ge(d_mm, step * 16)
                A(f_hi[:, p, :], up_a[:, :], ACT.Copy).then_inc(f_h, 1)

            act.wait_ge(n_lo, NORM_G0[PRE_FFN] + 16)
            pair(0, None, 0, True)
            pair(1, None, 1)
            with act.Fori(1, FFN_STEPS) as s:
                pair(s * 2, s, 0)
                pair(s * 2 + 1, s, 1)
            act.wait_ge(d_ad, 4 + 16 * FFN_STEPS)
            act.dma_start(post_gain3[:, :], a["norm_post_ffn"][0].partition_broadcast(P)).then_inc(gain_in, 16)
            post_stats(2, junk5)

        @block.vector
        def _(dve):
            V = nc.vector
            for s in (cv, xe, gc, xd_s, sk, sc, xdd_s, pv, yy, ys):
                dve.sem_inc(s, LEAD)
            dve.sem_inc(ye, Y_LEAD)
            dve.sem_inc(d_ad, 4)

            dve.wait_ge(masks, 7)
            V.tensor_copy(after_r[:, :], after[:, :])
            for r, n in enumerate(ROW_COUNTS):
                dve.wait_ge(c_tr, 1)
                V.tensor_copy(consts[:, r, 0:n], bank[0][:, r * P:r * P + n]).then_inc(c_ev, 1)
            for h in range(2):
                dve.wait_ge(c_tr, 2 + h)
                V.tensor_tensor(ws_t[:, 4 * h:4 * h + 4, :], bank[1 + h][:, :].rearrange("p (g t) -> p g t", t=P),
                                tri[:, :].unsqueeze(1).to_broadcast([P, 4, P]), ALU.mult).then_inc(c_ev, 1)

            def variance(u, h):
                per = min(4, NORM_TILES[u])
                s = slice(per * h, per * (h + 1))
                dve.wait_ge(n_sq, NORM_T0[u] + per * (h + 1))
                V.tensor_scalar(stat_v[:, s], stat[:, s], 1.0 / DM, EPS, ALU.mult, ALU.add).then_inc(n_var, 1)
                dve.wait_ge(n_var, 2 * (NORM_H0[u] + h) + 1)
                V.reciprocal(stat_r[:, s], stat_v[:, s]).then_inc(n_var, 1)

            def scale(u, h, src, dst):
                per = min(4, NORM_TILES[u])
                dve.wait_ge(n_rt, NORM_H0[u] + h + 1)
                for t in range(per * h, per * (h + 1)):
                    V.tensor_scalar(dst[:, t, :], src[:, t, :], stat_s[:, t:t + 1], None, ALU.mult).then_inc(n_xs, 1)

            def lows(u, gain0, hi, lo):
                per = min(4, NORM_TILES[u])
                for q in range(NORM_TILES[u] // per * KT):
                    h, kt = q // KT, q % KT
                    s = slice(h * per * P, (h + 1) * per * P)
                    dve.wait_ge(n_hi, NORM_G0[u] + q + 1)
                    V.scalar_tensor_tensor(out=lo[:, kt, s], in0=bank[q % 8][:, 0:per * P],
                                           scalar=consts[:, 3, gain0 + kt:gain0 + kt + 1], in1=hi[:, kt, s].bitcast(F32),
                                           op0=ALU.mult, op1=ALU.subtract).then_inc(n_lo, 1)

            for h in range(2):
                variance(PRE_X, h)
            for h in range(2):
                scale(PRE_X, h, x_tok, x_tok)
            dve.wait_ge(dt_in, 16 * 4)
            V.tensor_copy(dtw_hi[:, :, :], dtw[:, :, :]).then_inc(dt_w, 1)
            dve.wait_ge(dt_w, 1)
            V.tensor_tensor(dtw_lo[:, :, :], dtw[:, :, :], dtw_hi[:, :, :].bitcast(F32), ALU.subtract).then_inc(dt_w, 1)
            lows(PRE_X, 0, act_hi, act_lo)

            n = [0]

            def step(ins):
                n[0] += 1
                ins.then_inc(dt_dve, 1)
                dve.wait_ge(dt_dve, n[0])
            dve.wait_ge(dt_mm, 1)
            step(V.tensor_tensor(dt_x[:, :, :], bank[0][:, 0:NT * HEADS].rearrange("p (c h) -> p c h", h=HEADS),
                                 dt_bias[:, :].unsqueeze(1).to_broadcast([P, NT, HEADS]), ALU.add))
            dve.wait_ge(dt_act, 2)
            step(V.tensor_scalar(dt_d[:, :, :], dt_e[:, :, :], 2.0, None, ALU.add))
            step(V.reciprocal(dt_r[:, :, :], dt_d[:, :, :]))
            step(V.scalar_tensor_tensor(out=dt_s[:, :, :], in0=dt_e[:, :, :], scalar=2.0, in1=dt_r[:, :, :],
                                        op0=ALU.mult, op1=ALU.mult))
            step(V.scalar_tensor_tensor(out=dt_q[:, :, :], in0=dt_s[:, :, :], scalar=0.25, in1=dt_s[:, :, :],
                                        op0=ALU.mult, op1=ALU.mult))
            step(V.tensor_scalar(dt_p[:, :, :], dt_q[:, :, :], 1.0 / 13, None, ALU.mult))
            for c in (11, 9, 7, 5, 3):
                step(V.scalar_tensor_tensor(out=dt_p[:, :, :], in0=dt_p[:, :, :], scalar=1.0 / c, in1=dt_q[:, :, :],
                                            op0=ALU.add, op1=ALU.mult))
            step(V.scalar_tensor_tensor(out=dt_p[:, :, :], in0=dt_p[:, :, :], scalar=1.0, in1=dt_s[:, :, :],
                                        op0=ALU.add, op1=ALU.mult))
            step(V.scalar_tensor_tensor(out=dt[:, :, :], in0=dt_x[:, :, :], scalar=0.0, in1=dt_p[:, :, :],
                                        op0=ALU.max, op1=ALU.add))
            dve.wait_ge(dt_act, 3)
            step(V.scalar_tensor_tensor(out=dA[:, :, :], in0=dt[:, :, :], scalar=-1.0,
                                        in1=neg_a[:, :].unsqueeze(1).to_broadcast([P, NT, HEADS]),
                                        op0=ALU.mult, op1=ALU.mult))
            step(V.tensor_copy(dA_hi[:, :, :], dA[:, :, :]))
            step(V.tensor_tensor(dA_lo[:, :, :], dA[:, :, :], dA_hi[:, :, :].bitcast(F32), ALU.subtract))
            assert n[0] == 16

            dve.wait_ge(n_lo, NORM_G0[1])
            V.memset(xbc_raw[:, :, 0:CONV - 1], 0.0)

            def heads(ap):
                return ap.rearrange("p (r d) -> p r d", d=HD)

            def ssd_group(g):
                dve.wait_ge(ye, yth(g, 0))
                cv_c = consts[:, 0, 0:(CONV + 1) * XBC_TILES].rearrange("p (k j) -> p k j", j=XBC_TILES)
                for dst, src in ((g_conv[:, :, 0:XG], cv_c[:, :, bass.ds(g * XG, XG)]),
                                 (g_conv[:, :, XG:XG + 1], cv_c[:, :, bass.ds(g + 16, 1)]),
                                 (g_conv[:, :, XG + 1:XG + 2], cv_c[:, :, bass.ds(g + 20, 1)]),
                                 (g_gain[:, :], consts[:, 3, bass.ds(g * XG + 40, XG)]),
                                 (g_skip[:, :], d_skip[:, bass.ds(g * HPG, HPG)]),
                                 (g_dt[:, :, :], dt[:, :, bass.ds(g * HPG, HPG)]),
                                 (g_hi[:, :, :], dA_hi[:, :, bass.ds(g * HPG, HPG)].bitcast(F32)),
                                 (g_lo[:, :, :], dA_lo[:, :, bass.ds(g * HPG, HPG)]),
                                 (g_dA[:, :, :], dA[:, :, bass.ds(g * HPG, HPG)])):
                    V.tensor_copy(dst, src).then_inc(gc, 1)
                dve.wait_ge(gc, nth(g, GC, GC))

                def convolve(idx):
                    dve.wait_ge(t_ev, nth(g, 12, 2 * idx + 2))
                    if idx in (1, 2, 3, 4):
                        dve.wait_ge(xt, g * 10 + 2 * idx)
                    elif idx == 5:
                        dve.wait_ge(sl, nth(g, 6, 5))
                    V.tensor_scalar(conv[:, :], xbc_raw[:, idx % 2, CONV - 1:CONV - 1 + SEQ],
                                    g_conv[:, CONV - 1, idx:idx + 1], g_conv[:, CONV, idx:idx + 1],
                                    ALU.mult, ALU.add).then_inc(cv, 1)
                    for k in range(CONV - 1):
                        dve.wait_ge(cv, nth(g, 24, 4 * idx + k + 1))
                        V.scalar_tensor_tensor(out=conv[:, :], in0=xbc_raw[:, idx % 2, k:k + SEQ],
                                               scalar=g_conv[:, k, idx:idx + 1], in1=conv[:, :],
                                               op0=ALU.mult, op1=ALU.add).then_inc(cv, 1)

                def token_evac(idx):
                    for h in range(2):
                        q = 2 * idx + h
                        dve.wait_ge(xt, g * 10 + (q + 1))
                        src = bank[4 + q % 4][:, :].rearrange("p (c d) -> p c d", d=P)
                        dst = b_tok[:, 4 * h:4 * h + 4, :] if idx == XG else xs[:, 4 * h:4 * h + 4, idx * P:(idx + 1) * P]
                        V.tensor_copy(dst, src).then_inc(xe, 1)
                for idx in range(6):
                    convolve(idx)
                    if idx:
                        token_evac(idx - 1)
                dve.wait_ge(pv, nth(g, 17, 0))
                V.memset(state[:, :], 0.0).then_inc(pv, 1)

                def before_chunk(c):
                    if c >= 2:
                        dve.wait_ge(yd, nth(g, 8, c - 1))
                    if c == 0:
                        dve.wait_ge(xe, nth(g, 10, 8))
                    V.tensor_tensor(heads(xd[:, c % 2, :]), heads(xs[:, c, :]), bc(g_dt[:, c, :], [P, HPG, HD]),
                                    ALU.mult).then_inc(xd_s, 1)
                    dve.wait_ge(xd_s, nth(g, 8, c + 1))
                    V.tensor_tensor(heads(xs[:, c, :]), heads(xs[:, c, :]), bc(g_skip[:, :], [P, HPG, HD]),
                                    ALU.mult).then_inc(sk, 1)

                def score(c):
                    dve.wait_ge(cb, g * 8 + (c + 1))
                    V.tensor_tensor(cb_m[:, :], bank[3][:, 0:P], tri[:, :], ALU.mult).then_inc(sc, 1)
                    for h in range(2):
                        dve.wait_ge(ex, nth(g, 16, 2 * c + h + 1))
                        dve.wait_ge(sc, nth(g, 24, 3 * c + 1))
                        s = scores[:, h, :].rearrange("p (r l) -> p r l", l=P)
                        V.tensor_tensor(s, s, cb_m[:, :].unsqueeze(1).to_broadcast([P, 4, P]), ALU.mult).then_inc(sc, 1)
                    if c:
                        dve.wait_ge(st, g * 8 + c)
                    V.tensor_tensor(heads(xdd[:, :]), heads(xd[:, c % 2, :]), bc(g_out[:, c, :], [P, HPG, HD]),
                                    ALU.mult).then_inc(xdd_s, 1)

                def combine(c):
                    dve.wait_ge(yo, g * 8 + (c + 1))
                    V.tensor_tensor(heads(y_sum[:, :]), heads(bank[7][:, :]), bc(g_in[:, c, :], [P, HPG, HD]),
                                    ALU.mult).then_inc(yy, 1)
                    V.tensor_tensor(heads(state[:, :]), heads(state[:, :]), bc(g_chunk[:, c, :], [P, HPG, HD]),
                                    ALU.mult).then_inc(pv, 1)
                    dve.wait_ge(yy, nth(g, 32, 4 * c + 1))
                    V.tensor_tensor(y_sum[:, :], y_sum[:, :], bank[6][:, :], ALU.add).then_inc(yy, 1)
                    dve.wait_ge(st, g * 8 + (c + 1))
                    dve.wait_ge(pv, nth(g, 17, 2 * c + 2))
                    V.tensor_tensor(state[:, :], state[:, :], bank[2][:, :], ALU.add).then_inc(pv, 1)
                    dve.wait_ge(yy, nth(g, 32, 4 * c + 2))
                    V.tensor_tensor(xs[:, c, :], xs[:, c, :], y_sum[:, :], ALU.add).then_inc(yy, 1)
                    dve.wait_ge(yy, nth(g, 32, 4 * c + 3))
                    V.tensor_tensor(xs[:, c, :], xs[:, c, :], zs[:, c, :], ALU.mult).then_inc(yy, 1)

                before_chunk(0)
                for c in range(NT):
                    score(c)
                    if c + 1 < NT:
                        before_chunk(c + 1)
                    combine(c)
                dve.wait_ge(sq, nth(g, 8, 8))
                V.tensor_scalar(stat_v[:, :], stat[:, :], 1.0 / HALF, EPS, ALU.mult, ALU.add).then_inc(ysv, 1)
                dve.wait_ge(ysv, g * 2 + 1)
                V.reciprocal(stat_r[:, :], stat_v[:, :]).then_inc(ysv, 1)
                dve.wait_ge(ysr, g + 1)
                for c in range(NT):
                    V.tensor_scalar(xs[:, c, :], xs[:, c, :], stat_s[:, c:c + 1], None, ALU.mult).then_inc(ys, 1)
                for c in range(NT):
                    dve.wait_ge(yt, g * 8 + (c + 1))
                    dve.wait_ge(y_st[c % 2], g * 64 + (16 * (c // 2) + 16))
                    V.tensor_tensor(y_t[:, c % 2, :, :], bank[c][:, :].rearrange("p (j t) -> p j t", t=P),
                                    bc(g_gain[:, :], [P, XG, P]), ALU.mult).then_inc(ye, 1)

            with dve.Fori(0, GROUPS) as g:
                ssd_group(g)

            def low(k):
                dve.wait_ge(b_hi, k + 1)
                V.tensor_tensor(split_part(k, act_lo), split_source(k), split_part(k, act_hi).bitcast(F32),
                                ALU.subtract).then_inc(b_lo, 1)

            for k in range(8):
                low(k)
            dve.wait_ge(v_sq, 8)
            V.tensor_scalar(stat_v[:, :], stat[:, :], 1.0 / DM, EPS, ALU.mult, ALU.add).then_inc(v_var, 1)
            dve.wait_ge(v_var, 1)
            V.reciprocal(stat_r[:, :], stat_v[:, :]).then_inc(v_var, 1)
            dve.wait_ge(v_rt, 1)
            for t in range(NT):
                V.tensor_scalar(r2[:, t, :], r2[:, t, :], stat_s[:, t:t + 1], None, ALU.mult).then_inc(v_sc, 1)
            dve.wait_ge(bs_in, 16)

            def mix(g):
                for h in range(2):
                    q = 2 * g + h
                    out_q = r2[:, 4 * h:4 * h + 4, g * P:(g + 1) * P]
                    dve.wait_ge(m_mm, q + 1)
                    V.scalar_tensor_tensor(out=out_q, in0=bank[4 + q % 4][:, :].rearrange("p (c t) -> p c t", t=P),
                                           scalar=consts[:, 3, 32 + g:33 + g],
                                           in1=bs_bc[:, g, :].unsqueeze(1).to_broadcast([P, 4, P]),
                                           op0=ALU.mult, op1=ALU.add).then_inc(m_ev, 1)
                    dve.wait_ge(gate_ld[g % 3], 16 * (g // 3 + 1))
                    dve.wait_ge(m_ev, 2 * q + 1)
                    V.tensor_tensor(out_q, out_q, gate_in[:, g % 3, h * HALF:(h + 1) * HALF].rearrange("p (c t) -> p c t", t=P),
                                    ALU.mult).then_inc(m_ev, 1)
            for g in range(6):
                mix(g)
            for k in range(8, 16):
                low(k)
            mix(6)
            for k in range(16, 24):
                low(k)
            mix(7)

            for q in range(32):
                j, h = q // 2 % 8, q % 2
                k = 8 + q // 2
                s = slice(h * HALF, (h + 1) * HALF)
                gate = gate_in[:, k % 3, s]
                dve.wait_ge(b_mm, 16 + q + 1)
                dve.wait_ge(gate_ld[k % 3], 16 * (k // 3 + 1))
                if q < 16:
                    dve.wait_ge(b_cp, q + 1)
                    V.tensor_tensor(r1[:, j, s], r1[:, j, s], bank[q % 4][:, :], ALU.add).then_inc(b_ev, 1)
                    dve.wait_ge(b_ev, 2 * q + 1)
                    V.tensor_tensor(r1[:, j, s], r1[:, j, s], gate, ALU.mult).then_inc(b_ev, 1)
                else:
                    dve.wait_ge(b_ev, 2 * q - 2)
                    V.tensor_tensor(g_tmp[:, h, :], bank[q % 4][:, :], gate, ALU.mult).then_inc(b_ev, 1)
                    dve.wait_ge(b_ev, 2 * q + 1)
                    V.tensor_tensor(r1[:, j, s], r1[:, j, s], g_tmp[:, h, :], ALU.add).then_inc(b_ev, 1)
                if q in (14, 15, 30, 31):
                    first = 24 + 16 * (q // 16) + 8 * h
                    for i in range(first, first + 8):
                        low(i)

            def out_evac(u, n):
                for t in range(NT):
                    dve.wait_ge(o_mm, 16 * u + 8 * n + t + 1)
                    V.tensor_copy(r2[:, t, n * HALF:(n + 1) * HALF], bank[t][:, :]).then_inc(o_ev, 1)

            def residual(u, gain):
                for h in range(2):
                    s = slice(4 * h, 4 * h + 4)
                    dve.wait_ge(o_sq, 8 * u + 4 * h + 4)
                    V.tensor_scalar(stat_v[:, s], stat[:, s], 1.0 / DM, EPS, ALU.mult, ALU.add).then_inc(o_var, 1)
                    dve.wait_ge(o_var, 4 * u + 2 * h + 1)
                    V.reciprocal(stat_r[:, s], stat_v[:, s]).then_inc(o_var, 1)
                dve.wait_ge(gain_in, 16 * (u + 1))
                if u == 0:
                    dve.wait_ge(xr_in, 16)
                for t in range(NT):
                    dve.wait_ge(o_rt, 2 * u + t // 4 + 1)
                    V.scalar_tensor_tensor(out=r2[:, t, :], in0=r2[:, t, :], scalar=stat_s[:, t:t + 1], in1=gain[:, :],
                                           op0=ALU.mult, op1=ALU.mult).then_inc(o_y, 1)
                    if t:
                        dve.wait_ge(o_y, 8 * u + t)
                        V.tensor_tensor(r1[:, t - 1, :], r1[:, t - 1, :], r2[:, t - 1, :], ALU.add).then_inc(o_x, 1)
                dve.wait_ge(o_y, 8 * u + 8)
                V.tensor_tensor(r1[:, 7, :], r1[:, 7, :], r2[:, 7, :], ALU.add).then_inc(o_x, 1)

            variance(PRE_MEM_TOK, 0)
            scale(PRE_MEM_TOK, 0, mem_tok, mem_tok)
            out_evac(0, 0)
            lows(PRE_MEM_TOK, 24, mem_hi, mem_lo)
            out_evac(0, 1)
            residual(0, post_gain)
            for h in range(2):
                variance(PRE_MEM, h)
            for h in range(2):
                scale(PRE_MEM, h, r1, r2)
            lows(PRE_MEM, 8, act_hi, act_lo)

            for h in range(XH):
                for b in range(4):
                    dve.wait_ge(s_mm, 4 * h + b + 1)
                    V.tensor_reduce(out=a_max[:, 2 * b:2 * b + 2], in_=bank[4 + b][:, :].rearrange("p (t m) -> p t m", m=MEM),
                                    axis=AX.X, op=ALU.max).then_inc(a_mx, 1)
                dve.wait_ge(a_mx, 5 * h + 4)
                V.tensor_scalar(a_nm[:, :], a_max[:, :], -(XHD ** -0.5), None, ALU.mult).then_inc(a_mx, 1)
                dve.wait_ge(a_ex, 8 * h + 8)
                V.reciprocal(a_rec[:, :], a_sum[:, :]).then_inc(a_pn, 1)
                dve.wait_ge(a_pn, 9 * h + 1)
                for t in range(NT):
                    V.tensor_scalar(prob[:, t, :], prob[:, t, :], a_rec[:, t:t + 1], None, ALU.mult).then_inc(a_pn, 1)
                for q in range(4):
                    dve.wait_ge(a_tr, 4 * h + q + 1)
                    V.tensor_copy(prob_t[:, q // 2, (q % 2) * HALF:(q % 2 + 1) * HALF], bank[4 + q][:, :]).then_inc(a_te, 1)
            for kt in range(KT):
                dve.wait_ge(s_hi, kt + 1)
                V.tensor_tensor(act_lo[:, kt, :], r2[:, kt, :], act_hi[:, kt, :].bitcast(F32), ALU.subtract).then_inc(s_lo, 1)
            for n in range(2):
                out_evac(1, n)
            residual(1, post_gain2)
            for h in range(2):
                variance(PRE_FFN, h)
            for h in range(2):
                scale(PRE_FFN, h, r1, r2)
            lows(PRE_FFN, 16, act_hi, act_lo)

            V.memset(up_raw[:, :, 0:FFN_CONV - 1], 0.0)
            V.memset(r2[:, :, :], 0.0).then_inc(o_y, 1)

            def tap(k, col):
                r, off = ((1, 0), (1, 44), (2, 0), (2, 44))[k]
                return consts[:, r, bass.ds(col + off, 1)]

            def conv_step(u, col, i):
                w, k = i // 3, i % 3
                dst = (up_a, up_b)[w]
                c = col + w * FFN_TILES
                if k == 0:
                    dve.wait_ge(f_ev, u * 4 + (2 * w + 2))
                    if w == 0 and not (isinstance(u, int) and u == 0):
                        dve.wait_ge(f_l, u)
                    V.tensor_scalar(dst[:, :], up_raw[:, w, FFN_CONV - 1:FFN_CONV - 1 + SEQ], tap(2, c), tap(3, c),
                                    ALU.mult, ALU.add).then_inc(f_cv, 1)
                else:
                    dve.wait_ge(f_cv, u * 7 + i)
                    V.scalar_tensor_tensor(out=dst[:, :], in0=up_raw[:, w, k - 1:k - 1 + SEQ], scalar=tap(k - 1, c),
                                           in1=dst[:, :], op0=ALU.mult, op1=ALU.add).then_inc(f_cv, 1)

            def gate_pair(u):
                dve.wait_ge(f_gl, u + 1)
                dve.wait_ge(f_cv, u * 7 + 6)
                V.tensor_tensor(up_a[:, :], up_a[:, :], up_b[:, :], ALU.mult).then_inc(f_cv, 1)

            def low_pair(u, p):
                dve.wait_ge(f_h, u + 1)
                V.tensor_tensor(f_lo[:, p, :], up_a[:, :], f_hi[:, p, :].bitcast(F32), ALU.subtract).then_inc(f_l, 1)

            def add(step, r):
                n, t = r // 8, r % 8
                dve.wait_ge(d_mm, step * 16 + (r + 1))
                dve.wait_ge(d_ad, step * 16 + (r + 3))
                s = r2[:, t, n * HALF:(n + 1) * HALF]
                V.tensor_tensor(s, s, bank[4 + r % 4][:, :], ALU.add).then_inc(d_ad, 1)

            for u in range(2):
                for i in range(6):
                    conv_step(u, u, i)
                gate_pair(u)
                low_pair(u, u)
            dve.wait_ge(o_y, 17)
            with dve.Fori(1, FFN_STEPS) as s:
                for r in range(16):
                    if r % 2 == 0 and r < 12:
                        conv_step(s * 2, s * 2, r // 2)
                    if r == 13:
                        gate_pair(s * 2)
                    add(s - 1, r)
                low_pair(s * 2, 0)
                for i in range(6):
                    conv_step(s * 2 + 1, s * 2 + 1, i)
                gate_pair(s * 2 + 1)
                low_pair(s * 2 + 1, 1)
            for r in range(16):
                add(FFN_STEPS - 1, r)
            residual_last(dve, V, r1, r2, post_gain3, stat, stat_v, stat_r, stat_s, o_sq, o_var, o_rt, o_y, o_x, gain_in)


def residual_last(dve, V, r1, r2, gain, stat, stat_v, stat_r, stat_s, o_sq, o_var, o_rt, o_y, o_x, gain_in):
    for h in range(2):
        s = slice(4 * h, 4 * h + 4)
        dve.wait_ge(o_sq, 16 + 4 * h + 4)
        V.tensor_scalar(stat_v[:, s], stat[:, s], 1.0 / DM, EPS, ALU.mult, ALU.add).then_inc(o_var, 1)
        dve.wait_ge(o_var, 8 + 2 * h + 1)
        V.reciprocal(stat_r[:, s], stat_v[:, s]).then_inc(o_var, 1)
    dve.wait_ge(gain_in, 48)
    for t in range(NT):
        dve.wait_ge(o_rt, 4 + t // 4 + 1)
        V.scalar_tensor_tensor(out=r2[:, t, :], in0=r2[:, t, :], scalar=stat_s[:, t:t + 1], in1=gain[:, :],
                               op0=ALU.mult, op1=ALU.mult).then_inc(o_y, 1)
        dve.wait_ge(o_y, 17 + t + 1)
        V.tensor_tensor(r1[:, t, :], r1[:, t, :], r2[:, t, :], ALU.add).then_inc(o_x, 1)


ROW_COUNTS = [120, 88, 88, 56]
GAIN_ROWS = ["norm_pre_mix", "norm_pre_mem", "norm_pre_ffn", "norm_mem_kv", "gm_v_norm"]
ROW_LOADS = 5 + len(GAIN_ROWS) + 1

_INS = ["x", "mem", "norm_pre_mix", "norm_post_mix", "norm_pre_mem", "norm_mem_kv", "norm_post_mem",
        "norm_pre_ffn", "norm_post_ffn", "w_in", "gm_v_norm", "gm_w_s", "gm_b_s", "ssd_conv_w", "ssd_conv_b",
        "ssd_dt_bias", "ssd_a_log", "ssd_d", "ssd_norm", "w_branch_a", "w_branch_b", "w_out",
        "xa_w_q", "xa_w_kv", "xa_w_o", "ffn_w_up", "ffn_conv_w", "ffn_conv_b", "ffn_w_down"]


def kernel(**inputs):
    import numpy as _np
    import concourse.bacc as _bacc
    from concourse import mybir as _mybir
    from concourse.bass_utils import run_bass_kernel_spmd as _run

    nc = _bacc.Bacc("TRN2", target_bir_lowering=False, num_devices=1)
    arrays, args = {}, {}
    for name in _INS:
        v = _np.ascontiguousarray(inputs[name])
        arrays[f"in_{name}"] = v
        args[name] = nc.dram_tensor(f"in_{name}", v.shape, _mybir.dt.from_np(v.dtype), kind="ExternalInput").ap()
    out = nc.dram_tensor("out_x", (1, SEQ, DM), _mybir.dt.float32, kind="ExternalOutput").ap()
    trunk(nc, args, out)
    r = _run(nc, [arrays], core_ids=[0])
    return r.results[0]["out_x"]
```

```python
import concourse.bass as bass
from concourse import mybir
from contextlib import ExitStack


F32 = mybir.dt.float32
F32R = mybir.dt.float32r
ALU = mybir.AluOpType
ACT = mybir.ActivationFunctionType
AX = mybir.AxisListType

P = 128
SEQ = 1024
DM = 1024
KT = DM // P
NT = SEQ // P
HALF = 512
MEM = 256
EPS = 1e-6

GROUPS = 4
HPG = 8
HD = 64
XG = HPG * HD // P
CONV = 4
XBC_TILES = 24
U_OFF, V_OFF, Z_OFF, XBC_OFF = 0, 1024, 2048, 4096
DT_OFF, GA_OFF, GB_OFF = 7168, 7200, 8224
HEADS = 32

FFN_TILES = 22
FFN_CONV = 3
FFN_STEPS = FFN_TILES // 2

XH = 4
XHD = 256

SSD_TILES = 16
W_SSD = 0
W_V = W_SSD + GROUPS * SSD_TILES
W_BRANCH = W_V + 8
W_OUT = W_BRANCH + 24
W_VM = W_OUT + 8
W_Q = W_VM + 4
W_O = W_Q + 8
W_FFN = W_O + 8
FFN_W = 6
KV_TILES = 12
KV_AFTER = {2: range(0, 3), 3: range(3, 6), 4: range(6, 8), 5: range(8, 10), 6: range(10, 12)}
W_LAST = W_FFN - 2 + (FFN_STEPS - 1) * FFN_W
LAST_ORDER = [(n, t - 3 * n) for t in range(NT + 3) for n in range(2) if 0 <= t - 3 * n < NT]
POOL_ADDS = 6

NORM_TILES = [8, 2, 8, 8]
NORM_T0 = [0, 8, 10, 18]
NORM_H0 = [0, 8, 9, 17]
NORM_G0 = [0, 16, 24, 40]
PRE_X, PRE_MEM_TOK, PRE_MEM, PRE_FFN = range(4)


def trunk(nc, a, out):
    ctx = ExitStack()

    def dram(name, shape):
        return nc.dram_tensor(name, shape, F32, kind="Internal").ap()

    gates_dram = dram("gates_scratch", (24, P, SEQ))
    ssd_dram = dram("ssd_scratch", (16, P, SEQ))

    with ctx:
        def sb(name, shape, dt=F32, c=ctx):
            return c.enter_context(nc.sbuf_tensor(name, shape, dt))

        def sem(name):
            return ctx.enter_context(nc.semaphore(name))

        act_hi = sb("act_hi", [P, KT, SEQ], F32R)
        act_lo = sb("act_lo", [P, KT, SEQ], F32R)
        w_raw = sb("w_raw", [P, 2, 1024])
        w_hi = sb("w_hi", [P, 2, 1024], F32R)
        w_lo = sb("w_lo", [P, 2, 1024], F32R)
        ident = sb("ident", [P, P])
        tri = sb("tri", [P, P])
        after = sb("after", [P, P])
        consts = sb("consts", [P, 4, P])
        stat = sb("stat", [P, 8])
        stat_v = sb("stat_v", [P, 8])
        stat_r = sb("stat_r", [P, 8])
        stat_s = sb("stat_s", [P, 8])
        stat_n = sb("stat_n", [P, 8])
        stat_w = sb("stat_w", [P, 8])

        ssd = ExitStack()
        keep = ExitStack()
        ws_t = sb("ws_t", [P, 8, P], c=keep)
        base = ExitStack()
        after_r = sb("after_r", [P, P], F32R, base)
        ones = sb("ones", [P, P], c=base)
        dt = sb("dt", [P, NT, HEADS], c=base)
        dA = sb("dA", [P, NT, HEADS], c=base)
        dA_hi = sb("dA_hi", [P, NT, HEADS], F32R, base)
        dA_lo = sb("dA_lo", [P, NT, HEADS], c=base)
        d_skip = sb("d_skip", [P, HEADS], c=base)

        setup = ExitStack()
        x_tok = sb("x_tok", [P, NT, DM], c=setup)
        rows = sb("rows", [P, 4, P], c=setup)
        ws_rows = sb("ws_rows", [P, 8, P], c=setup)
        junk = sb("junk", [P, DM], c=setup)
        dtw = sb("dtw", [P, KT, HEADS], c=setup)
        dtw_hi = sb("dtw_hi", [P, KT, HEADS], F32R, setup)
        dtw_lo = sb("dtw_lo", [P, KT, HEADS], F32R, setup)
        dt_bias = sb("dt_bias", [P, HEADS], c=setup)
        a_log = sb("a_log", [P, HEADS], c=setup)
        dt_x = sb("dt_x", [P, NT, HEADS], c=setup)
        dt_abs = sb("dt_abs", [P, NT, HEADS], c=setup)
        dt_e = sb("dt_e", [P, NT, HEADS], c=setup)
        dt_d = sb("dt_d", [P, NT, HEADS], c=setup)
        dt_r = sb("dt_r", [P, NT, HEADS], c=setup)
        dt_s = sb("dt_s", [P, NT, HEADS], c=setup)
        dt_q = sb("dt_q", [P, NT, HEADS], c=setup)
        dt_p = sb("dt_p", [P, NT, HEADS], c=setup)
        neg_a = sb("neg_a", [P, HEADS], c=setup)
        dt_heads = sb("dt_heads", [HEADS, SEQ], c=setup)
        setup.close()

        xs = sb("xs", [P, NT, HALF], c=ssd)
        zs = sb("zs", [P, NT, HALF], c=ssd)
        b_t = sb("b_t", [P, SEQ], c=ssd)
        c_t = sb("c_t", [P, SEQ], c=ssd)
        b_tok = sb("b_tok", [P, NT, P], c=ssd)
        xbc_raw = sb("xbc_raw", [P, 2, CONV - 1 + SEQ], c=ssd)
        conv = sb("conv", [P, SEQ], c=ssd)
        gate_out = sb("gate_out", [P, 2, HALF], c=ssd)
        tri_hi = sb("tri_hi", [P, 2, HALF], F32R, ssd)
        tri_lo = sb("tri_lo", [P, 2, HALF], F32R, ssd)
        scores = sb("scores", [P, 2, HALF], c=ssd)
        cb_m = sb("cb_m", [P, P], c=ssd)
        xd = sb("xd", [P, 2, HALF], c=ssd)
        xdd = sb("xdd", [P, HALF], c=ssd)
        state = sb("state", [P, HALF], c=ssd)
        y_sum = sb("y_sum", [P, HALF], c=ssd)
        sq_junk = sb("sq_junk", [P, HALF], c=ssd)
        g_conv = sb("g_conv", [P, CONV + 1, XG + 2], c=ssd)
        g_dt = sb("g_dt", [P, NT, HPG], c=ssd)
        g_hi = sb("g_hi", [P, NT, HPG], c=ssd)
        g_lo = sb("g_lo", [P, NT, HPG], c=ssd)
        g_dA = sb("g_dA", [P, NT, HPG], c=ssd)
        decays = sb("decays", [P, 3, NT, HPG], c=ssd)
        g_in, g_out, g_chunk = (decays[:, i, :, :] for i in range(3))
        g_skip = sb("g_skip", [P, HPG], c=ssd)
        g_gain = sb("g_gain", [P, XG], c=ssd)
        ssd.close()
        base.close()

        mixp = ExitStack()
        r2 = sb("r2", [P, NT, DM], c=mixp)
        r1 = sb("r1", [P, NT, DM], c=mixp)
        bs_bc = sb("bs_bc", [P, 8, P], c=mixp)
        junk2 = sb("junk2", [P, DM], c=mixp)
        y_in = sb("y_in", [P, 3, 4 * HALF], c=mixp)
        gate_in = sb("gate_in", [P, 3, SEQ], c=mixp)
        g_tmp = sb("g_tmp", [P, 2, HALF], c=mixp)
        mixp.close()
        keep.close()

        later = ExitStack()
        pad = sb("ws_t_place", [P, 8, P], c=later)
        kvw = ExitStack()
        mem_tok = sb("mem_tok", [P, 2, DM], c=kvw)
        kv_raw = sb("kv_raw", [P, 2, 1024], c=kvw)
        kv_hi = sb("kv_hi", [P, 2, 1024], F32R, kvw)
        kv_lo = sb("kv_lo", [P, 2, 1024], F32R, kvw)
        kvw.close()
        r2_ = sb("r2_place", [P, NT, DM], c=later)
        r1_ = sb("r1_place", [P, NT, DM], c=later)
        kv = ExitStack()
        v_tok = sb("v_tok", [P, 2, DM], c=kv)
        k_t = sb("k_t", [P, 8, MEM], c=kv)
        memp = ExitStack()
        mem_hi = sb("mem_hi", [P, KT, MEM], F32R, memp)
        mem_lo = sb("mem_lo", [P, KT, MEM], F32R, memp)
        post_gain = sb("post_gain", [P, DM], c=memp)
        junk3 = sb("junk3", [P, DM], c=memp)
        bank_junk3 = sb("bank_junk3", [P, HALF], c=memp)
        memp.close()
        att = ExitStack()
        q_t = sb("q_t", [P, 2, SEQ], c=att)
        prob = sb("prob", [P, NT, MEM], c=att)
        prob_t = sb("prob_t", [P, 2, SEQ], c=att)
        a_max = sb("a_max", [P, 8], c=att)
        a_nm = sb("a_nm", [P, 8], c=att)
        a_sum = sb("a_sum", [P, 8], c=att)
        a_rec = sb("a_rec", [P, 8], c=att)
        att.close()
        post2 = ExitStack()
        post_gain2 = sb("post_gain2", [P, DM], c=post2)
        junk4 = sb("junk4", [P, DM], c=post2)
        bank_junk4 = sb("bank_junk4", [P, HALF], c=post2)
        post2.close()
        kv.close()
        ffn = ExitStack()
        up_raw = sb("up_raw", [P, 2, FFN_CONV - 1 + SEQ], c=ffn)
        up_a = sb("up_a", [P, SEQ], c=ffn)
        up_b = sb("up_b", [P, SEQ], c=ffn)
        f_hi = sb("f_hi", [P, 4, SEQ], F32R, ffn)
        f_lo = sb("f_lo", [P, 4, SEQ], F32R, ffn)
        ffn.close()
        post3 = ExitStack()
        post_gain3 = sb("post_gain3", [P, DM], c=post3)
        junk5 = sb("junk5", [P, DM], c=post3)
        post3.close()
        later.close()

        bank = [ctx.enter_context(nc.psum_tensor(f"bank{i}", [P, HALF], F32)) for i in range(8)]

        w_in = [sem(f"w_in{i}") for i in range(2)]
        w_hi_done = sem("w_hi_done")
        w_split = sem("w_split")
        w_begun = sem("w_begun")
        held = sem("held")
        sp_held = sem("sp_held")
        masks = sem("masks")
        x_in = [sem(f"x_in{i}") for i in range(4)]
        gains_in, dtw_in = sem("gains_in"), sem("dtw_in")
        rows_in, dt_cp, ws_in, dt_in = sem("rows_in"), sem("dt_cp"), sem("ws_in"), sem("dt_in")
        c_tr, c_ev = sem("c_tr"), sem("c_ev")
        n_sq, n_var, n_rt, n_xs = sem("n_sq"), sem("n_var"), sem("n_rt"), sem("n_xs")
        n_xa = sem("n_xa")
        n_tr, n_hi, n_lo = sem("n_tr"), sem("n_hi"), sem("n_lo")
        dt_w, dt_mm, dt_dve, dt_act, dt_cum, dt_exp = [sem(f"dt_{n}") for n in ("w", "mm", "dve", "act", "cum", "exp")]
        z_mm, z_ev, t_mm, t_ev, cv, sl, xt, xe = [sem(n) for n in ("z_mm", "z_ev", "t_mm", "t_ev", "cv", "sl", "xt", "xe")]
        g_mm, g_ev = sem("g_mm"), sem("g_ev")
        g_st = [sem(f"g_st{i}") for i in range(2)]
        y_st = sem("y_st")
        gc = sem("group_consts")
        xd_s, sk, rh, seg, ex, cb, sc, xdd_s = [sem(n) for n in ("xd_done", "skip_done", "rh", "seg", "ex", "cb", "sc", "xdd_done")]
        yd, yo, st, pv, yy, sq, ysv, ysr, ys, yt, ye = [sem(n) for n in ("yd", "yo", "st", "pv", "yy", "sq", "ysv", "ysr", "ys", "yt", "ye")]
        v_mm, v_ev, v_sq, v_var, v_rt, v_sc = [sem(n) for n in ("v_mm", "v_ev", "v_sq", "v_var", "v_rt", "v_sc")]
        gate_ld = [sem(f"gate_ld{i}") for i in range(3)]
        m_mm, m_ev, b_cp = [sem(n) for n in ("m_mm", "m_ev", "b_cp")]
        bs_in = sem("bs_in")
        b_mm, b_ev, b_hi, b_lo = [sem(n) for n in ("b_mm", "b_ev", "b_hi", "b_lo")]
        y_ld = [sem(f"y_ld{i}") for i in range(3)]
        s_hi, s_lo = sem("s_hi"), sem("s_lo")
        o_mm, o_ev, o_sq, o_var, o_rt, o_y, o_x = [sem(n) for n in ("o_mm", "o_ev", "o_sq", "o_var", "o_rt", "o_y", "o_x")]
        gain_in, xr_in, mem_in = sem("gain_in"), sem("xr_in"), sem("mem_in")
        kv_in = [sem(f"kv_in{i}") for i in range(2)]
        kv_begun, kv_h, kv_l = sem("kv_begun"), sem("kv_h"), sem("kv_l")
        k_mm, k_ev = sem("k_mm"), sem("k_ev")
        q_mm, q_ev, s_mm, a_mx, a_ex, a_pn, a_tr, a_te, p_mm, p_ev = [sem(n) for n in ("q_mm", "q_ev", "s_mm", "a_mx", "a_ex", "a_pn", "a_tr", "a_te", "p_mm", "p_ev")]
        f_mm, f_ev, f_cv, f_gl, f_h, f_l, d_mm, d_ad = [sem(n) for n in ("f_mm", "f_ev", "f_cv", "f_gl", "f_h", "f_l", "d_mm", "d_ad")]
        out_st = sem("out_st")
        o_xp = sem("o_xp")

        NORMS = (PRE_MEM, PRE_FFN)
        FIRST_ORDER = (0, 2, 1, 3)
        LEAD = 1
        Y_LEAD = LEAD + NT

        def nth(g, per, k):
            return g * per + (k + LEAD)

        def yth(g, k):
            return g * NT + (k + Y_LEAD)

        LAST = GROUPS - 1
        GC = 9

        def y_half(h):
            return zs[:, 4 * h:4 * h + 4, :].rearrange("p a b -> p (a b)").rearrange("p (j c t) -> p j c t", j=XG, c=4)

        def bc(ap, shape):
            return ap.unsqueeze(2).to_broadcast(shape)

        RING = (w_hi, w_lo, w_begun)
        KV_RING = (kv_hi, kv_lo, kv_begun)

        def norm_bank(u, q):
            if u != PRE_MEM_TOK and q < 8:
                return q
            return 4 + q % 4

        def channels_half(slot, half, bk, first_inc, hi=act_hi, lo=act_lo, n=HALF, before=None, ring=RING):
            for kt in range(KT):
                if before:
                    before(kt)
                wh, wl = (w[:, slot, kt * P:(kt + 1) * P] for w in ring[:2])
                ah, al = (t[:, kt, half * n:(half + 1) * n] for t in (hi, lo))
                for i, (w, x) in enumerate(((wh, ah), (wh, al), (wl, ah))):
                    m = nc.tensor.matmul(bank[bk][:, 0:n], w, x, start=kt == 0 and i == 0,
                                         stop=kt == KT - 1 and i == 2)
                    if first_inc and kt == 0 and i == 0:
                        m.then_inc(ring[2], 1)
            return m

        def tokens_block(slot, part, t, bk, hi=act_hi, lo=act_lo, begins=False, kk_only=None, ring=RING):
            for kk in range(2) if kk_only is None else [kk_only]:
                kt = 2 * part + kk
                wh, wl = (w[:, slot, kk * HALF:(kk + 1) * HALF] for w in ring[:2])
                ah, al = (x[:, kt, t * P:(t + 1) * P] for x in (hi, lo))
                for i, (x, w) in enumerate(((ah, wh), (ah, wl), (al, wh))):
                    m = nc.tensor.matmul(bank[bk][:, :], x, w, start=kt == 0 and i == 0,
                                         stop=kt == KT - 1 and i == 2)
                    if begins and kk == 0 and i == 0:
                        m.then_inc(ring[2], 1)
            return m

        def tokens_tile(slot, part, done, tiles=NT, hi=act_hi, lo=act_lo, free=None, bk0=0, ready=None, ring=RING):
            for kk in range(2):
                kt = 2 * part + kk
                for t in range(tiles):
                    if ready and t % 4 == 0:
                        ready(kt, t // 4)
                    if kt == 0 and free:
                        free(t)
                    m = tokens_block(slot, part, t, bk0 + t, hi, lo, begins=t == 0, kk_only=kk, ring=ring)
                    if kt == KT - 1:
                        m.then_inc(done, 1)

        SPLITS = [(0, kt, 0, SEQ) for kt in range(KT)]
        SPLITS += [(p, kt, h * HALF, HALF) for p in (1, 2, 3) for h in range(2) for kt in range(KT)]

        def splits_done(p, h, kt):
            return kt + 1 if p == 0 else 8 + 16 * (p - 1) + 8 * h + kt + 1

        def split_source(k):
            p, kt, c0, n = SPLITS[k]
            if p == 0:
                return y_in[:, kt // 2 % 3, (kt % 2) * SEQ:(kt % 2 + 1) * SEQ]
            if p == 1:
                m = 4 + (k - 8) // 4
                return y_in[:, m % 3, (kt % 4) * HALF:(kt % 4 + 1) * HALF]
            if p == 2:
                return r2[:, c0 // P:c0 // P + 4, kt * P:(kt + 1) * P]
            return r1[:, kt, c0:c0 + n]

        def split_part(k, x):
            p, kt, c0, n = SPLITS[k]
            ap = x[:, kt, c0:c0 + n]
            return ap.rearrange("p (c t) -> p c t", t=P) if p == 2 else ap

        block = ctx.enter_context(nc.Block())

        @block.sync
        def _(sp):
            x_v = a["x"][0].rearrange("(t p) d -> p t d", p=P)
            for i in range(4):
                if i == 2:
                    sp.dma_start(dtw[:, :, :], a["w_in"][0, :, DT_OFF:DT_OFF + HEADS].rearrange("(k p) c -> p k c", p=P)).then_inc(dtw_in, 16)
                    sp.wait_ge(rows_in, 16 * ROW_LOADS)
                    sp.wait_ge(gains_in, 16 * (len(GAIN_ROWS) + 1))
                sp.dma_start(x_tok[:, 2 * i:2 * i + 2, :], x_v[:, 2 * i:2 * i + 2, :]).then_inc(x_in[i], 16)
            sp.dma_start(ws_rows[:, :, :], a["gm_w_s"][0].rearrange("g t s -> t g s")).then_inc(ws_in, 16)
            for dst, n in ((dt_bias, "ssd_dt_bias"), (a_log, "ssd_a_log"), (d_skip, "ssd_d")):
                sp.dma_start(dst[:, :], a[n][0].partition_broadcast(P)).then_inc(dt_in, 16)

            def load(i, slot, src, dst=None):
                if not (isinstance(i, int) and i < 2):
                    sp.wait_ge(w_split, i - 1)
                if not isinstance(i, int):
                    sp.sem_inc(sp_held, 1)
                sp.dma_start(w_raw[:, slot, :] if dst is None else dst, src).then_inc(w_in[slot], 16)

            def channel_tile(w, col):
                return w[:, bass.ds(col, P)].rearrange("(k p) c -> p k c", p=P)

            def token_tile(w, part, col):
                return w[2 * part * P:2 * (part + 1) * P, bass.ds(col, HALF)].rearrange("(k p) c -> p k c", p=P)

            def raw(slot, k):
                return w_raw[:, slot, :].rearrange("p (k c) -> p k c", k=k)

            win = a["w_in"][0]

            def ssd_cols(g):
                cols = [XBC_OFF + g * HALF + P * j for j in range(XG)]
                cols += [XBC_OFF + 2048 + g * P, XBC_OFF + 2560 + g * P]
                return cols + [off + g * 2 * P + P * j for off in (GA_OFF, GB_OFF, U_OFF) for j in range(2)]

            def ssd_loads(g, start=0):
                for j in range(start, SSD_TILES):
                    i = g * SSD_TILES + j
                    if j < 4:
                        load(i, j % 2, token_tile(win, j, Z_OFF + g * HALF), raw(j % 2, 2))
                    else:
                        load(i, j % 2, channel_tile(win, ssd_cols(g)[j - 4]), raw(j % 2, KT))

            ssd_loads(0)
            with sp.Fori(1, GROUPS) as g:
                ssd_loads(g)

            def token_loads(i0, w, col0=0, halves=2):
                for n in range(halves):
                    for part in range(4):
                        load(i0 + 4 * n + part, part % 2, token_tile(w, part, col0 + n * HALF), raw(part % 2, 2))

            def channel_loads(i0, w):
                for j in range(8):
                    load(i0 + j, j % 2, channel_tile(w, j * P), raw(j % 2, KT))

            token_loads(W_V, win, V_OFF)
            channel_loads(W_BRANCH, a["w_branch_b"][0, 0:DM, :])
            channel_loads(W_BRANCH + 8, a["w_branch_b"][0, DM:2 * DM, :])
            channel_loads(W_BRANCH + 16, a["w_branch_a"][0])
            token_loads(W_OUT, a["w_out"][0])
            token_loads(W_VM, a["xa_w_kv"][0], DM + HALF, 1)
            channel_loads(W_Q, a["xa_w_q"][0])
            token_loads(W_O, a["xa_w_o"][0])

            up, down = a["ffn_w_up"][0], a["ffn_w_down"][0]

            def up_loads(i, step, pair):
                col = step * 2 * P + pair * P
                load(i, 0, channel_tile(up, col), raw(0, KT))
                load(i + 1, 1, channel_tile(up, col + FFN_TILES * P), raw(1, KT))

            def down_loads(i, step):
                rows_v = down[bass.ds(step * 2 * P, 2 * P), :].rearrange("(k p) c -> p k c", p=P)
                for n in range(2):
                    load(i + n, n, rows_v[:, :, n * HALF:(n + 1) * HALF], raw(n, 2))

            up_loads(W_FFN, 0, 0)
            up_loads(W_FFN + 2, 0, 1)
            with sp.Fori(1, FFN_STEPS - 1) as s:
                i = s * FFN_W + (W_FFN - 2)
                up_loads(i, s, 0)
                down_loads(i + 2, s - 1)
                up_loads(i + 4, s, 1)
            up_loads(W_LAST, FFN_STEPS - 1, 0)
            up_loads(W_LAST + 2, FFN_STEPS - 1, 1)
            down_loads(W_LAST + 4, FFN_STEPS - 2)
            down_loads(W_LAST + 6, FFN_STEPS - 1)

            out_v = out[0].rearrange("(t p) d -> p t d", p=P)
            for t in range(NT):
                if t < POOL_ADDS:
                    sp.wait_ge(o_xp, t + 1)
                else:
                    sp.wait_ge(o_x, 16 + t - POOL_ADDS + 1)
                sp.dma_start(out_v[:, t, :], r1[:, t, :]).then_inc(out_st, 16)
            sp.wait_ge(out_st, 16 * NT)

        @block.gpsimd
        def _(pool):
            nc.gpsimd.memset(ident[:, :], 0.0).then_inc(masks, 1)
            nc.gpsimd.memset(tri[:, :], 1.0).then_inc(masks, 1)
            nc.gpsimd.memset(after[:, :], 1.0).then_inc(masks, 1)
            nc.gpsimd.memset(ones[:, :], 1.0).then_inc(masks, 1)
            pool.wait_ge(masks, 4)
            nc.gpsimd.affine_select(out=ident[:, :], in_=ident[:, :], compare_op=ALU.not_equal, fill=1.0,
                                    base=0, pattern=[[-1, P]], channel_multiplier=1).then_inc(masks, 1)
            nc.gpsimd.affine_select(out=tri[:, :], in_=tri[:, :], compare_op=ALU.is_ge, fill=0.0,
                                    base=0, pattern=[[1, P]], channel_multiplier=-1).then_inc(masks, 1)
            nc.gpsimd.affine_select(out=after[:, :], in_=after[:, :], compare_op=ALU.is_gt, fill=0.0,
                                    base=0, pattern=[[-1, P]], channel_multiplier=1).then_inc(masks, 1)

            for i, n in enumerate(GAIN_ROWS):
                pool.dma_start(rows[8 * i:8 * i + 8, 3, :], a[n][0].rearrange("(j p) -> j p", p=P)).then_inc(gains_in, 16)
            pool.dma_start(rows[40:56, 3, :], a["ssd_norm"][0].rearrange("(j p) -> j p", p=P)).then_inc(gains_in, 16)

            pool.sem_inc(rh, LEAD)

            def split(i, slot, loads):
                pool.wait_ge(w_begun, i + LEAD)
                pool.wait_ge(w_in[slot], loads * 16)
                if not isinstance(i, int):
                    pool.sem_inc(held, 1)
                nc.gpsimd.tensor_scalar(w_hi[:, slot, :], w_raw[:, slot, :], 1.0, 1.0, ALU.mult, ALU.mult).then_inc(w_hi_done, 1)
                pool.wait_ge(w_hi_done, i + 1)
                nc.gpsimd.tensor_tensor(w_lo[:, slot, :], w_raw[:, slot, :], w_hi[:, slot, :].bitcast(F32),
                                        ALU.subtract).then_inc(w_split, 1)

            def triangle(g, c):
                for h in range(2):
                    if c:
                        pool.wait_ge(seg, g * 16 + (2 * (c - 1) + h + 1))
                    else:
                        pool.wait_ge(gc, nth(g, GC, GC))
                    for dst, src in ((tri_hi, g_hi), (tri_lo, g_lo)):
                        nc.gpsimd.tensor_tensor(dst[:, h, :].rearrange("p (r l) -> p r l", l=P),
                                                bc(src[:, c, 4 * h:4 * h + 4], [P, 4, P]),
                                                tri[:, :].unsqueeze(1).to_broadcast([P, 4, P]), ALU.mult).then_inc(rh, 1)

            with pool.Fori(0, GROUPS) as g:
                def ssd_split(j):
                    split(g * SSD_TILES + j, j % 2, g * (SSD_TILES // 2) + (j // 2 + 1))
                for j in range(11):
                    ssd_split(j)
                triangle(g, 0)
                ssd_split(11)
                triangle(g, 1)
                ssd_split(12)
                triangle(g, 2)
                triangle(g, 3)
                ssd_split(13)
                triangle(g, 4)
                triangle(g, 5)
                ssd_split(14)
                triangle(g, 6)
                triangle(g, 7)
                ssd_split(15)

            def splits(i0, i1):
                with pool.Fori(i0 // 2, i1 // 2) as j:
                    for s in range(2):
                        split(j * 2 + s, s, j + 1)
            splits(W_V, W_FFN + FFN_STEPS * FFN_W)

            for t in range(POOL_ADDS):
                pool.wait_ge(o_y, 1 + t + 1)
                nc.gpsimd.tensor_tensor(r1[:, t, :], r1[:, t, :], r2[:, t, :], ALU.add).then_inc(o_xp, 1)

        @block.tensor
        def _(pe):
            pe.sem_inc(yd, LEAD)
            pe.sem_inc(w_begun, LEAD)
            pe.wait_ge(masks, 7)

            def constants():
                pe.wait_ge(rows_in, 16 * ROW_LOADS)
                pe.wait_ge(gains_in, 16 * (len(GAIN_ROWS) + 1))
                for r, n in enumerate(ROW_COUNTS):
                    m = nc.tensor.transpose(bank[7][:, r * P:r * P + n], rows[0:n, r, :], ident[0:n, 0:n])
                m.then_inc(c_tr, 1)

            def norm_transposes(u, src, free=None, halves=None, after=None):
                tiles = NORM_TILES[u]
                per = min(4, tiles)
                for h in range(tiles // per) if halves is None else halves:
                    if u < PRE_MEM:
                        pe.wait_ge(n_xs, NORM_T0[u] + per * (h + 1))
                    else:
                        pe.wait_ge(n_xs, NORM_T0[PRE_MEM] + 4 * (u - PRE_MEM) + 2 * (h + 1))
                        pe.wait_ge(n_xa, 4 * (u - PRE_MEM) + 2 * (h + 1))
                    for kt in range(KT):
                        q = h * KT + kt
                        if q >= 8 or q >= 4 and u == PRE_MEM_TOK:
                            pe.wait_ge(n_lo, NORM_G0[u] + q - 3)
                        elif free:
                            free(q)
                        for i in range(per):
                            m = nc.tensor.transpose(bank[norm_bank(u, q)][:, i * P:(i + 1) * P],
                                                    src[:, h * per + i, kt * P:(kt + 1) * P], ident[:, :])
                        m.then_inc(n_tr, 1)
                        if after:
                            after(q)

            def dt_product(h, kt):
                if h == 0 and kt == 0:
                    pe.wait_ge(dt_w, 2)
                pe.wait_ge(n_lo, 8 * h + kt + 1)
                ah, al = (x[:, kt, h * HALF:(h + 1) * HALF] for x in (act_hi, act_lo))
                for i, (w, x) in enumerate(((dtw_hi, ah), (dtw_lo, ah), (dtw_hi, al))):
                    m = nc.tensor.matmul(bank[h][0:HEADS, :], w[:, kt, :], x,
                                         start=kt == 0 and i == 0, stop=kt == KT - 1 and i == 2)
                if kt == KT - 1:
                    m.then_inc(dt_mm, 1)
            constants()
            norm_transposes(PRE_X, x_tok, lambda q: pe.wait_ge(c_ev, 4) if q == 7 else None, [0])
            for kt in range(KT):
                dt_product(0, kt)
            norm_transposes(PRE_X, x_tok, halves=[1], after=lambda q: dt_product(1, q - 9) if q > 8 else None)
            dt_product(1, KT - 1)
            pe.wait_ge(ws_in, 16)
            for h in range(2):
                for i in range(4):
                    m = nc.tensor.transpose(bank[3 + h][:, i * P:(i + 1) * P], ws_rows[:, 4 * h + i, :], ident[:, :])
                m.then_inc(c_tr, 1)
            pe.wait_ge(dt_cp, 2)
            for t in range(NT):
                m = nc.tensor.transpose(bank[2][:, t * HEADS:(t + 1) * HEADS], dt_heads[:, t * P:(t + 1) * P],
                                        ident[0:HEADS, 0:HEADS])
            m.then_inc(dt_mm, 1)

            def seg_and_cb(g, c):
                for h in range(2):
                    pe.wait_ge(rh, nth(g, 32, 4 * c + 2 * h + 2))
                    pe.wait_ge(ex, nth(g, 16, 2 * c + h - 1 if c else 0))
                    for i, t in enumerate((tri_hi, tri_lo)):
                        m = nc.tensor.matmul(bank[4 + h][:, :], after_r[:, :], t[:, h, :], start=i == 0, stop=i == 1)
                    m.then_inc(seg, 1)
                pe.wait_ge(sc, nth(g, 24, 3 * c - 2 if c else 0))
                nc.tensor.matmul(bank[3][:, 0:P], b_t[:, c * P:(c + 1) * P], c_t[:, c * P:(c + 1) * P],
                                 start=True, stop=True).then_inc(cb, 1)

            def chunk_products(g, c):
                pe.wait_ge(sc, nth(g, 24, 3 * c + 3))
                pe.wait_ge(xd_s, nth(g, 8, c + 1))
                pe.wait_ge(yy, nth(g, 32, 4 * c - 2 if c else 0))
                for r in range(HPG):
                    m = nc.tensor.matmul(bank[6][:, r * HD:(r + 1) * HD],
                                         scores[:, r // 4, (r % 4) * P:(r % 4 + 1) * P],
                                         xd[:, c % 2, r * HD:(r + 1) * HD], start=True, stop=True)
                m.then_inc(yd, 1)
                pe.wait_ge(pv, nth(g, 17, 2 * c + 1))
                nc.tensor.matmul(bank[7][:, :], c_t[:, c * P:(c + 1) * P], state[:, :],
                                 start=True, stop=True).then_inc(yo, 1)
                pe.wait_ge(xdd_s, nth(g, 8, c + 1))
                nc.tensor.matmul(bank[2][:, :], b_tok[:, c, :], xdd[:, :], start=True, stop=True).then_inc(st, 1)

            def gate_half(g, q):
                j = 10 + q // 2
                if q % 2 == 0:
                    pe.wait_ge(w_split, g * SSD_TILES + (j + 1))
                if q < 2:
                    pe.wait_ge(t_ev, nth(g, 12, 9 + q))
                else:
                    pe.wait_ge(g_ev, nth(g, 12, q - 1))
                channels_half(j % 2, q % 2, q % 2, q % 2 == 0).then_inc(g_mm, 1)

            def to_tokens(g, idx):
                pe.wait_ge(sl, nth(g, 6, idx + 1))
                for h in range(2):
                    q = 2 * idx + h
                    pe.wait_ge(xe, nth(g, 10, max(0, q - 3)))
                    for i in range(4):
                        c = 4 * h + i
                        src = b_t if idx == XG else conv
                        m = nc.tensor.transpose(bank[4 + q % 4][:, i * P:(i + 1) * P], src[:, c * P:(c + 1) * P], ident[:, :])
                    m.then_inc(xt, 1)

            def ssd_group(g):
                def z_free(t):
                    pe.wait_ge(ye, yth(g, t + 1) - NT)
                for part in range(4):
                    pe.wait_ge(w_split, g * SSD_TILES + (part + 1))
                    tokens_tile(part % 2, part, z_mm, free=z_free)
                for idx in range(6):
                    pe.wait_ge(w_split, g * SSD_TILES + (4 + idx + 1))
                    for h in range(2):
                        b = 2 * (idx % 2) + h
                        if idx < 2:
                            pe.wait_ge(z_ev, nth(g, 8, b + 1))
                        else:
                            pe.wait_ge(t_ev, nth(g, 12, 2 * (idx - 2) + h + 1))
                        channels_half(idx % 2, h, b, h == 0).then_inc(t_mm, 1)
                    if idx == 0:
                        pe.wait_ge(z_ev, nth(g, 8, 8))
                        pe.wait_ge(gc, nth(g, GC, GC))
                        for i, mask in enumerate((tri, after, ones)):
                            m = nc.tensor.matmul(bank[7][:, i * NT * HPG:(i + 1) * NT * HPG], mask[:, :],
                                                 g_dA[:, :, :].rearrange("p c h -> p (c h)"), start=True, stop=True)
                        m.then_inc(dt_cum, 1)
                    if idx == 2:
                        pe.wait_ge(dt_exp, g + 1)
                    if idx >= 1:
                        to_tokens(g, idx - 1)
                for q in range(2):
                    gate_half(g, q)
                pe.wait_ge(xe, nth(g, 10, 10))
                pe.wait_ge(t_ev, nth(g, 12, 12))
                pe.wait_ge(sl, nth(g, 6, 6))
                seg_and_cb(g, 0)
                for c in range(NT):
                    gate_half(g, c + 2)
                    chunk_products(g, c)
                    if c + 1 < NT:
                        seg_and_cb(g, c + 1)
                for q in range(NT + 2, 12):
                    gate_half(g, q)
                for c in range(NT):
                    pe.wait_ge(ys, nth(g, 8, c + 1))
                    if c < 2:
                        pe.wait_ge(g_ev, nth(g, 12, 11 + c))
                    for i in range(XG):
                        m = nc.tensor.transpose(bank[c][:, i * P:(i + 1) * P], xs[:, c, i * P:(i + 1) * P], ident[:, :])
                    m.then_inc(yt, 1)

            pe.wait_ge(dt_dve, 1)
            pe.wait_ge(c_ev, 6)
            with pe.Fori(0, GROUPS) as g:
                ssd_group(g)

            for n in range(2):
                def v_free(t, n=n):
                    if n:
                        pe.wait_ge(v_ev, t + 1)
                    else:
                        pe.wait_ge(ye, yth(LAST, t + 1))
                for part in range(4):
                    pe.wait_ge(w_split, W_V + 4 * n + part + 1)
                    tokens_tile(part % 2, part, v_mm, free=v_free)

            def mix(g):
                for h in range(2):
                    q = 2 * g + h
                    if q >= 4:
                        pe.wait_ge(m_ev, 2 * (q - 4) + 1)
                    for i in range(4):
                        m = nc.tensor.matmul(bank[4 + q % 4][:, i * P:(i + 1) * P],
                                             r2[:, 4 * h + i, g * P:(g + 1) * P], ws_t[:, g, :],
                                             start=True, stop=True)
                    m.then_inc(m_mm, 1)

            def branch_tile(part, j, i):
                pe.wait_ge(w_split, W_BRANCH + i + 1)
                for h in range(2):
                    r = 16 * part + 2 * j + h
                    if r < 4:
                        pe.wait_ge(v_ev, 8 + r + 1)
                    elif r < 20:
                        pe.wait_ge(b_cp, r - 3)
                    else:
                        pe.wait_ge(b_ev, 2 * (r - 4 - 16) + 1)

                    def ready(kt, part=part, h=h):
                        if j == 0 and (part or h == 0):
                            pe.wait_ge(b_lo, splits_done(part, h, kt))
                    channels_half(i % 2, h, r % 4, h == 0, before=ready).then_inc(b_mm, 1)
                    if part == 0 and r >= 8:
                        if r == 8:
                            pe.wait_ge(v_sc, 8)
                        mix(r - 8)

            for part in range(2):
                for j in range(8):
                    branch_tile(part, j, 8 * part + j)
            def kv_product(m):
                pe.wait_ge(kv_l, m + 1)
                if m < 4:
                    pe.wait_ge(n_lo, NORM_G0[PRE_MEM])
                elif m <= 8:
                    pe.wait_ge(k_ev, m - 3)
                if m < 8:
                    channels_half(m % 2, 0, 4 + m % 4, True, mem_hi, mem_lo, MEM, ring=KV_RING).then_inc(k_mm, 1)
                else:
                    tokens_tile(m % 2, m - 8, k_mm, 2, mem_hi, mem_lo, bk0=4, ring=KV_RING,
                                free=lambda t: pe.wait_ge(k_ev, 4 + t + 1))

            for j in range(8):
                branch_tile(2, j, 16 + j)
                if j == 1:
                    norm_transposes(PRE_MEM_TOK, mem_tok, lambda q: pe.wait_ge(m_ev, 32))
                for m in KV_AFTER.get(j, ()):
                    kv_product(m)

            OUT_LAG = 3

            def out_product(u, i0, free0):
                for n in range(2):
                    def free(t, n=n):
                        if n:
                            pe.wait_ge(o_ev, 16 * u + t + 1)
                            pe.wait_ge(o_sq, 16 * u + t + 1)
                        else:
                            free0(t)

                    def ready(kt, h, n=n):
                        if n == 0 and u == 0:
                            pe.wait_ge(b_lo, splits_done(3, h, kt))
                        elif n == 0 and h == 0:
                            pe.wait_ge(s_lo, kt + 1)
                    for part in range(4 - 2 * n):
                        pe.wait_ge(w_split, i0 + 4 * n + part + 1)
                        tokens_tile(part % 2, part, o_mm, free=free, ready=ready)
                pe.wait_ge(w_split, i0 + 7)
                for t in range(NT + OUT_LAG):
                    if t < NT:
                        m = tokens_block(0, 2, t, t, begins=t == 0)
                        if t == NT - 1:
                            m.then_inc(w_begun, 1)
                    if t == OUT_LAG:
                        pe.wait_ge(w_split, i0 + 8)
                    if t >= OUT_LAG:
                        tokens_block(1, 3, t - OUT_LAG, t - OUT_LAG).then_inc(o_mm, 1)

            def mix_banks(t):
                if t < 4:
                    pe.wait_ge(b_ev, 32 + 2 * (12 + t) + 1)
                else:
                    pe.wait_ge(k_ev, 10)
            out_product(0, W_OUT, mix_banks)

            def banks_read(u):
                def free(q):
                    pe.wait_ge(o_ev, 16 * u + 8 + q + 1)
                    pe.wait_ge(o_sq, 16 * u + 8 + q + 1)
                return free

            for part in range(4):
                pe.wait_ge(w_split, W_VM + part + 1)
                tokens_tile(part % 2, part, k_mm, 2, mem_hi, mem_lo, free=banks_read(0))

            def values_read(q):
                if q < 2:
                    pe.wait_ge(k_ev, 10 + q + 1)
                else:
                    banks_read(0)(q)
            norm_transposes(PRE_MEM, r2, values_read, [0])

            def first_queries():
                for half in range(2):
                    if half:
                        norm_transposes(PRE_MEM, r2, halves=[1])
                    for d in range(2):
                        pe.wait_ge(w_split, W_Q + d + 1)

                        def ready(kt, half=half, d=d):
                            if d == 0:
                                pe.wait_ge(n_lo, NORM_G0[PRE_MEM] + 8 * half + kt + 1)
                        channels_half(d, half, 2 * d + half, half == d, before=ready).then_inc(q_mm, 1)

            def queries(h):
                for d in range(2):
                    pe.wait_ge(w_split, W_Q + 2 * h + d + 1)
                    for half in range(2):
                        b = 2 * d + half
                        pe.wait_ge(q_ev, FIRST_ORDER.index(b) + 1 if h == 1 else 4 * h + b - 3)
                        channels_half(d, half, b, half == 0).then_inc(q_mm, 1)

            first_queries()
            pe.wait_ge(n_lo, NORM_G0[PRE_FFN])
            pe.wait_ge(k_ev, 12)
            for h in range(XH):
                pe.wait_ge(q_ev, 4 * h + 4)
                for t in range(NT):
                    b = 4 + t // 2
                    if h and t % 2 == 0:
                        pe.wait_ge(p_ev, 4 * (h - 1) + t // 2 + 1)
                    for d in range(2):
                        m = nc.tensor.matmul(bank[b][:, (t % 2) * MEM:(t % 2 + 1) * MEM], q_t[:, d, t * P:(t + 1) * P],
                                             k_t[:, 2 * h + d, :], start=d == 0, stop=d == 1)
                    if t % 2:
                        m.then_inc(s_mm, 1)
                if h + 1 < XH:
                    queries(h + 1)
                for i in range(4):
                    half, mt = i // 2, i % 2
                    pe.wait_ge(a_pn, 10 * h + 5 * (half + 1))
                    for k in range(4):
                        m = nc.tensor.transpose(bank[4 + i][:, k * P:(k + 1) * P],
                                                prob[:, 4 * half + k, mt * P:(mt + 1) * P], ident[:, :])
                    m.then_inc(a_tr, 1)
                for i in range(4):
                    half, d = i // 2, i % 2
                    pe.wait_ge(a_te, 4 * h + 2 * (half + 1))
                    for mt in range(2):
                        m = nc.tensor.matmul(bank[4 + i][:, :], v_tok[:, mt, h * XHD + d * P:h * XHD + (d + 1) * P],
                                             prob_t[:, mt, half * HALF:(half + 1) * HALF], start=mt == 0, stop=mt == 1)
                    m.then_inc(p_mm, 1)
            out_product(1, W_O, lambda t: pe.wait_ge(p_ev, 16) if t >= 4 else pe.wait_ge(q_ev, 16))

            norm_transposes(PRE_FFN, r2, banks_read(1), [0])

            def first_products():
                for half in range(2):
                    if half:
                        norm_transposes(PRE_FFN, r2, halves=[1])
                    for w in range(2):
                        pe.wait_ge(w_split, W_FFN + (w + 1))

                        def ready(kt, half=half, w=w):
                            if w == 0:
                                pe.wait_ge(n_lo, NORM_G0[PRE_FFN] + 8 * half + kt + 1)
                        channels_half(w, half, 2 * w + half, half == w, before=ready).then_inc(f_mm, 1)

            def up_products(i, u):
                for w in range(2):
                    pe.wait_ge(w_split, i + (w + 1))
                    for half in range(2):
                        b = 2 * w + half
                        if isinstance(u, int) and u == 1:
                            pe.wait_ge(f_ev, FIRST_ORDER.index(b) + 1)
                        else:
                            pe.wait_ge(f_ev, u * 4 + (b - 3))
                        channels_half(w, half, b, half == 0).then_inc(f_mm, 1)

            def down_block(step, r, n, t, f0, begins=False):
                pe.wait_ge(d_ad, step * 16 + (r + 1))
                for k in range(2):
                    fh, fl = (x[:, f0 + k, t * P:(t + 1) * P] for x in (f_hi, f_lo))
                    wh, wl = (w[:, n, k * HALF:(k + 1) * HALF] for w in (w_hi, w_lo))
                    for j, (x, w) in enumerate(((fh, wh), (fh, wl), (fl, wh))):
                        m = nc.tensor.matmul(bank[4 + r % 4][:, :], x, w, start=k == 0 and j == 0,
                                             stop=k == 1 and j == 2)
                        if begins and k == 0 and j == 0:
                            m.then_inc(w_begun, 1)
                m.then_inc(d_mm, 1)

            def down_products(i, step):
                pe.wait_ge(f_l, step * 2 + 2)
                for n in range(2):
                    pe.wait_ge(w_split, i + (n + 1))
                    for t in range(NT):
                        down_block(step, 8 * n + t, n, t, 0, t == 0)

            first_products()
            up_products(W_FFN + 2, 1)
            with pe.Fori(1, FFN_STEPS - 1) as s:
                i = s * FFN_W + (W_FFN - 2)
                up_products(i, s * 2)
                down_products(i + 2, s - 1)
                up_products(i + 4, s * 2 + 1)
            last = FFN_STEPS - 1
            up_products(W_LAST, 2 * last)
            up_products(W_LAST + 2, 2 * last + 1)
            down_products(W_LAST + 4, last - 1)
            pe.wait_ge(f_l, 2 * last + 2)
            for r, (n, t) in enumerate(LAST_ORDER):
                if t == 0:
                    pe.wait_ge(w_split, W_LAST + 7 + n)
                down_block(last, r, n, t, 2, r == 0)

        @block.scalar
        def _(act):
            A = nc.scalar.activation
            for s in (z_ev, t_ev, sl, g_ev, ex, sq):
                act.sem_inc(s, LEAD)
            for s in (*g_st, y_st):
                act.sem_inc(s, 16)

            def row_load(dst, src):
                act.dma_start(dst, src).then_inc(rows_in, 16)
            row_load(rows[0:96, 0, :], a["ssd_conv_w"][0].rearrange("k (j p) -> (k j) p", p=P))
            row_load(rows[96:120, 0, :], a["ssd_conv_b"][0].rearrange("(j p) -> j p", p=P))
            row_load(rows[0:88, 1, :], a["ffn_conv_w"][0, 0:2].rearrange("k (j p) -> (k j) p", p=P))
            row_load(rows[0:44, 2, :], a["ffn_conv_w"][0, 2].rearrange("(j p) -> j p", p=P))
            row_load(rows[44:88, 2, :], a["ffn_conv_b"][0].rearrange("(j p) -> j p", p=P))

            def square(u, t, src, jk):
                if NORM_T0[u] + t:
                    act.wait_ge(n_sq, NORM_T0[u] + t)
                A(jk[:, :], src[:, t, :], ACT.Square, accum_out=stat[:, t:t + 1]).then_inc(n_sq, 1)

            def root(u, t, n=1):
                act.wait_ge(n_var, 2 * (NORM_H0[u] + t) + 2)
                A(stat_s[:, t:t + n], stat_r[:, t:t + n], ACT.Sqrt).then_inc(n_rt, 1)

            def norm_high(u, gain0, q, hi=act_hi):
                per = min(4, NORM_TILES[u]) * P
                h, kt = q // KT, q % KT
                act.wait_ge(n_tr, NORM_G0[u] + q + 1)
                A(hi[:, kt, h * per:(h + 1) * per], bank[norm_bank(u, q)][:, 0:per], ACT.Copy,
                  scale=consts[:, 3, gain0 + kt:gain0 + kt + 1]).then_inc(n_hi, 1)

            for t in range(4):
                act.wait_ge(x_in[t // 2], 16)
                square(PRE_X, t, x_tok, junk)
                if t:
                    root(PRE_X, t - 1)
            root(PRE_X, 3)
            act.wait_ge(c_ev, 4)
            for q in range(16):
                if q % 2 == 0 and q < 8:
                    t = 4 + q // 2
                    act.wait_ge(x_in[t // 2], 16)
                    square(PRE_X, t, x_tok, junk)
                    root(PRE_X, t)
                norm_high(PRE_X, 0, q)

            act.wait_ge(dt_dve, 1)
            A(dt_abs[:, :, :], dt_x[:, :, :], ACT.Abs).then_inc(dt_act, 1)
            act.wait_ge(dt_act, 1)
            A(dt_e[:, :, :], dt_abs[:, :, :], ACT.Exp, scale=-1.0).then_inc(dt_act, 1)
            A(neg_a[:, :], a_log[:, :], ACT.Exp).then_inc(dt_act, 1)

            def gate_evac(g, q):
                act.wait_ge(g_st[q % 2], g * 96 + (16 * (q // 2) + 16))
                act.wait_ge(g_mm, nth(g, 12, q + 1) - LEAD)
                A(gate_out[:, q % 2, :], bank[q % 2][:, :], ACT.Sigmoid if q < 8 else ACT.Gelu_apprx_tanh).then_inc(g_ev, 1)
                act.wait_ge(g_ev, nth(g, 12, q + 1))
                tile = g * 2 + ((q // 4) * 8 + q // 2 % 2)
                act.dma_start(gates_dram[bass.ds(tile, 1), :, (q % 2) * HALF:(q % 2 + 1) * HALF].rearrange("j p t -> p (j t)"),
                              gate_out[:, q % 2, :]).then_inc(g_st[q % 2], 16)

            def ssd_group(g):
                act.wait_ge(y_st, g * 32 + 16)
                for t in range(NT):
                    act.wait_ge(z_mm, g * 8 + (t + 1))
                    A(zs[:, t, :], bank[t][:, :], ACT.Silu).then_inc(z_ev, 1)

                def silu(idx):
                    act.wait_ge(cv, nth(g, 24, 4 * idx + 4))
                    dst = conv if idx < XG else b_t if idx == XG else c_t
                    A(dst[:, :], conv[:, :], ACT.Silu).then_inc(sl, 1)
                for idx in range(6):
                    for h in range(2):
                        if h and idx:
                            silu(idx - 1)
                        act.wait_ge(t_mm, g * 12 + (2 * idx + h + 1))
                        if h == 0:
                            act.wait_ge(cv, nth(g, 24, max(0, 4 * (idx - 1))))
                        A(xbc_raw[:, idx % 2, CONV - 1 + h * HALF:CONV - 1 + (h + 1) * HALF],
                          bank[2 * (idx % 2) + h][:, :], ACT.Copy).then_inc(t_ev, 1)
                    if idx == 0:
                        act.wait_ge(dt_cum, g + 1)
                        A(decays[:, :, :, :].rearrange("p i c h -> p (i c h)"), bank[7][:, 0:3 * NT * HPG],
                          ACT.Exp).then_inc(dt_exp, 1)
                silu(5)
                for q in range(2):
                    gate_evac(g, q)

                def y_square(c):
                    act.wait_ge(yy, nth(g, 32, 4 * c + 4))
                    act.wait_ge(sq, nth(g, 8, c))
                    A(sq_junk[:, :], xs[:, c, :], ACT.Square, accum_out=stat[:, c:c + 1]).then_inc(sq, 1)
                for c in range(NT):
                    for h in range(2):
                        act.wait_ge(seg, g * 16 + (2 * c + h + 1))
                        act.wait_ge(yd, nth(g, 8, c))
                        A(scores[:, h, :], bank[4 + h][:, :], ACT.Exp).then_inc(ex, 1)
                    gate_evac(g, c + 2)
                    if c:
                        y_square(c - 1)
                y_square(NT - 1)
                act.wait_ge(ysv, g * 2 + 2)
                A(stat_s[:, :], stat_r[:, :], ACT.Sqrt).then_inc(ysr, 1)
                for q in range(NT + 2, 12):
                    gate_evac(g, q)
                for h in range(2):
                    act.wait_ge(ye, yth(g, 4 * h + 4))
                    act.dma_start(ssd_dram[bass.ds(g * XG, XG), :, h * HALF:(h + 1) * HALF].rearrange("j p t -> p j t"),
                                  y_half(h).rearrange("p j c t -> p j (c t)")).then_inc(y_st, 16)

            act.wait_ge(n_lo, NORM_G0[1])
            act.wait_ge(dt_dve, 16)
            with act.Fori(0, GROUPS) as g:
                ssd_group(g)

            for s in (*g_st,):
                act.wait_ge(s, 16 + 96 * GROUPS)
            act.wait_ge(y_st, 16 + 32 * GROUPS)
            def gate_load(k):
                if k >= 11:
                    act.wait_ge(b_ev, 4 * (k - 11) + 4)
                elif k >= 3:
                    act.wait_ge(m_ev, 4 * (k - 3) + 4)
                act.dma_start(gate_in[:, k % 3, :], gates_dram[(16, 8, 0)[k // 8] + k % 8]).then_inc(gate_ld[k % 3], 16)

            def y_load(m):
                if m >= 3:
                    act.wait_ge(b_lo, 2 * (m - 3) + 2 if m < 7 else 12)
                if m < 4:
                    src = ssd_dram[2 * m:2 * m + 2].rearrange("j p t -> p j t")
                else:
                    h, k = (m - 4) // 2, 8 + 4 * (m % 2)
                    src = ssd_dram[k:k + 4, :, h * HALF:(h + 1) * HALF].rearrange("j p t -> p j t")
                act.dma_start(y_in[:, m % 3, :].rearrange("p (j t) -> p j t", j=2 if m < 4 else 4), src).then_inc(y_ld[m % 3], 16)

            def high(k):
                p, kt, c0, n = SPLITS[k]
                if p < 2:
                    m = kt // 2 if p == 0 else 4 + (k - 8) // 4
                    act.wait_ge(y_ld[m % 3], 16 * (m // 3 + 1))
                if p == 0:
                    act.wait_ge(w_begun, W_V + 4 + kt // 2 + 2 + LEAD)
                else:
                    act.wait_ge(b_mm, 16 * p - 1 + c0 // HALF)
                if p == 2:
                    act.wait_ge(m_ev, 32)
                if p == 3:
                    act.wait_ge(b_ev, 32 + 2 * (2 * kt + c0 // HALF) + 2)
                A(split_part(k, act_hi), split_source(k), ACT.Copy).then_inc(b_hi, 1)

            for k in range(3):
                y_load(k)
                gate_load(k)
            act.dma_start(bs_bc[:, :, :], a["gm_b_s"][0].partition_broadcast(P)).then_inc(bs_in, 16)

            def v_evac(n):
                for t in range(NT):
                    act.wait_ge(v_mm, 8 * n + t + 1)
                    A(r2[:, t, n * HALF:(n + 1) * HALF], bank[t][:, :], ACT.Gelu_apprx_tanh).then_inc(v_ev, 1)
            v_evac(0)
            for k in range(6):
                high(k)
                if k >= 4:
                    y_load(k - 1)
            v_evac(1)
            high(6)
            high(7)
            for t in range(NT):
                act.wait_ge(v_ev, 8 + t + 1)
                if t:
                    act.wait_ge(v_sq, t)
                A(junk2[:, :], r2[:, t, :], ACT.Square, accum_out=stat[:, t:t + 1]).then_inc(v_sq, 1)
            act.wait_ge(v_var, 2)
            A(stat_s[:, :], stat_r[:, :], ACT.Sqrt).then_inc(v_rt, 1)
            y_load(5)
            y_load(6)

            def branch_evac(r):
                act.wait_ge(b_mm, r + 1)
                A(r1[:, r // 2, (r % 2) * HALF:(r % 2 + 1) * HALF], bank[r % 4][:, :], ACT.Copy).then_inc(b_cp, 1)
                if r >= 9:
                    gate_load(r - 6)
            for r in range(14):
                branch_evac(r)
            for k in range(8, 16):
                high(k)
            branch_evac(14)
            y_load(7)
            for k in range(16, 24):
                high(k)
            branch_evac(15)
            for k in range(10, 18):
                gate_load(k)
            for k in range(24, 32):
                high(k)
            gate_load(18)
            for k in range(32, 40):
                high(k)
            act.wait_ge(b_lo, 40)
            act.dma_start(mem_tok[:, :, :], a["mem"][0].rearrange("(t p) d -> p t d", p=P)).then_inc(mem_in, 16)
            gate_load(19)
            act.wait_ge(mem_in, 16)
            for t in range(2):
                square(PRE_MEM_TOK, t, mem_tok, junk2)
            root(PRE_MEM_TOK, 0, 2)
            gate_load(20)
            for q in range(8):
                norm_high(PRE_MEM_TOK, 24, q, mem_hi)

            def kv_load(m):
                if m >= 2:
                    act.wait_ge(kv_l, m - 1)
                w = a["xa_w_kv"][0]
                if m < 8:
                    src = w[:, m * P:(m + 1) * P]
                else:
                    src = w[2 * (m - 8) * P:2 * (m - 7) * P, DM:DM + HALF]
                act.dma_start(kv_raw[:, m % 2, :].rearrange("p (k c) -> p k c", k=KT if m < 8 else 2),
                              src.rearrange("(k p) c -> p k c", p=P)).then_inc(kv_in[m % 2], 16)

            def kv_high(m):
                act.wait_ge(kv_in[m % 2], 16 * (m // 2 + 1))
                if m >= 2:
                    act.wait_ge(kv_begun, m)
                A(kv_hi[:, m % 2, :], kv_raw[:, m % 2, :], ACT.Copy).then_inc(kv_h, 1)
                if m + 2 < KV_TILES:
                    kv_load(m + 2)
            kv_load(0)
            kv_load(1)
            kv_high(0)
            kv_high(1)
            for j in range(2, 7):
                if j <= 4:
                    gate_load(19 + j)
                for m in KV_AFTER[j]:
                    if 2 <= m + 1 < KV_TILES:
                        kv_high(m + 1)
                    if m < 8:
                        act.wait_ge(k_mm, m + 1)
                        A(k_t[:, m, :], bank[4 + m % 4][:, 0:MEM], ACT.Copy).then_inc(k_ev, 1)
            for t in range(2):
                act.wait_ge(k_mm, 8 + t + 1)
                A(v_tok[:, t, 0:HALF], bank[4 + t][:, :], ACT.Copy).then_inc(k_ev, 1)
            for k in range(40, 56):
                high(k)

            def split_high(kt):
                act.wait_ge(p_ev, 4 * (kt // 2 + 1))
                A(act_hi[:, kt, :], r2[:, kt, :], ACT.Copy).then_inc(s_hi, 1)

            def bank_square(u, n, t, jk):
                act.wait_ge(o_mm, 16 * u + 8 * n + t + 1)
                if u + n + t:
                    act.wait_ge(o_sq, 16 * u + 8 * n + t)
                if n:
                    act.wait_ge(n_rt, NORM_H0[2 + u])
                A(jk, bank[t][:, :], ACT.Square, accum_out=(stat_n, stat)[n][:, t:t + 1]).then_inc(o_sq, 1)

            act.dma_start(post_gain[:, :], a["norm_post_mix"][0].partition_broadcast(P)).then_inc(gain_in, 16)
            act.wait_ge(b_lo, 56)
            act.dma_start(r1[:, :, :], a["x"][0].rearrange("(t p) d -> p t d", p=P)).then_inc(xr_in, 16)
            for t in range(NT):
                bank_square(0, 0, t, bank_junk3[:, :])

            def pre_square(u, t, jk):
                act.wait_ge(o_x, 8 * u + t + 1)
                square(NORMS[u], t, r1, jk)

            def post_root(u, t):
                act.wait_ge(o_var, 17 * u + 2 * t + 3)
                A(stat_s[:, t:t + 1], stat_r[:, t:t + 1], ACT.Sqrt).then_inc(o_rt, 1)

            def pre_scale(u, t):
                act.wait_ge(n_rt, NORM_H0[NORMS[u]] + t + 1)
                A(r2[:, t, :], r1[:, t, :], ACT.Copy, scale=stat_s[:, t:t + 1]).then_inc(n_xa, 1)

            def post_norm(u, jk, bank_jk):
                for t in range(NT):
                    bank_square(u, 1, t, bank_jk)
                    if t >= 3:
                        root(NORMS[u], t - 3)
                    if t >= 2:
                        pre_square(u, t - 2, jk)
                    post_root(u, t)
                    if t >= 3 and t % 2:
                        pre_scale(u, t - 3)

            def first_highs(u, gain0, jk):
                for q in range(8):
                    if q == 0:
                        root(NORMS[u], NT - 3)
                    if q == 4:
                        pre_scale(u, NT - 2)
                    if 1 <= q < 3:
                        pre_square(u, NT - 3 + q, jk)
                        root(NORMS[u], NT - 3 + q)
                    norm_high(NORMS[u], gain0, q)

            post_norm(0, junk3, bank_junk3[:, :])
            def last_scales(u, jk):
                root(NORMS[u], NT - 3)
                for t in (NT - 2, NT - 1):
                    pre_square(u, t, jk)
                    root(NORMS[u], t)
                pre_scale(u, NT - 2)
            last_scales(0, junk3)
            for t in range(2):
                act.wait_ge(k_mm, 10 + t + 1)
                A(v_tok[:, t, HALF:DM], bank[t][:, :], ACT.Copy).then_inc(k_ev, 1)
            for q in range(16):
                norm_high(PRE_MEM, 8, q)

            def query_evac(h):
                for i in range(4):
                    r = FIRST_ORDER[i] if h == 0 else i
                    act.wait_ge(q_mm, 4 * h + i + 1)
                    A(q_t[:, r // 2, (r % 2) * HALF:(r % 2 + 1) * HALF], bank[r][:, :], ACT.Copy).then_inc(q_ev, 1)
            act.wait_ge(n_lo, NORM_G0[PRE_FFN])
            query_evac(0)
            for h in range(XH):
                for t in range(NT):
                    act.wait_ge(a_mx, 6 * h + 3 * (t // 4 + 1))
                    if h:
                        act.wait_ge(a_tr, 4 * h)
                    A(prob[:, t, :], bank[4 + t // 2][:, (t % 2) * MEM:(t % 2 + 1) * MEM], ACT.Exp,
                      bias=a_nm[:, t:t + 1], scale=XHD ** -0.5, accum_out=a_sum[:, t:t + 1]).then_inc(a_ex, 1)
                if h + 1 < XH:
                    query_evac(h + 1)
                if h == XH - 1:
                    act.wait_ge(q_mm, 4 * XH)
                    for kt in range(6):
                        split_high(kt)
                for i in range(4):
                    act.wait_ge(p_mm, 4 * h + i + 1)
                    A(r2[:, 2 * h + i % 2, (i // 2) * HALF:(i // 2 + 1) * HALF], bank[4 + i][:, :], ACT.Copy).then_inc(p_ev, 1)
            split_high(6)
            split_high(7)
            act.wait_ge(s_lo, 8)
            act.dma_start(post_gain2[:, :], a["norm_post_mem"][0].partition_broadcast(P)).then_inc(gain_in, 16)
            for t in range(NT):
                bank_square(1, 0, t, bank_junk4[:, :])
            post_norm(1, junk4, bank_junk4[:, :])
            first_highs(1, 16, junk4)

            def raw_evac(u, b, first=False):
                if not first:
                    act.wait_ge(f_cv, u * 7 + (-4 if b < 2 else -1))
                A(up_raw[:, b // 2, FFN_CONV - 1 + (b % 2) * HALF:FFN_CONV - 1 + (b % 2 + 1) * HALF],
                  bank[b][:, :], ACT.Copy).then_inc(f_ev, 1)

            def gated(u, step, p):
                act.wait_ge(f_cv, u * 7 + 3)
                A(up_a[:, :], up_a[:, :], ACT.Gelu_apprx_tanh).then_inc(f_gl, 1)
                act.wait_ge(f_cv, u * 7 + 7)
                if step is not None:
                    act.wait_ge(d_mm, step * 16)
                A(f_hi[:, p, :], up_a[:, :], ACT.Copy).then_inc(f_h, 1)

            def pair(u, step, p):
                for b in range(4):
                    act.wait_ge(f_mm, u * 4 + (b + 1))
                    raw_evac(u, b)
                gated(u, step, p)

            for q in range(8, 16):
                norm_high(PRE_FFN, 16, q)
            act.wait_ge(n_lo, NORM_G0[PRE_FFN] + 16)
            for i, b in enumerate(FIRST_ORDER):
                act.wait_ge(f_mm, i + 1)
                raw_evac(0, b, True)
            gated(0, None, 0)
            pair(1, None, 1)
            with act.Fori(1, FFN_STEPS - 1) as s:
                pair(s * 2, s, 0)
                pair(s * 2 + 1, s, 1)
            last = FFN_STEPS - 1
            pair(2 * last, None, 2)
            pair(2 * last + 1, None, 3)
            act.dma_start(post_gain3[:, :], a["norm_post_ffn"][0].partition_broadcast(P)).then_inc(gain_in, 16)
            for t in range(NT):
                act.wait_ge(d_ad, 4 + 16 * last + LAST_ORDER.index((1, t)) + 1)
                act.wait_ge(o_sq, 32 + t)
                A(junk5[:, :], r2[:, t, :], ACT.Square, accum_out=stat[:, t:t + 1]).then_inc(o_sq, 1)
                act.wait_ge(o_var, 34 + 2 * t + 2)
                A(stat_s[:, t:t + 1], stat_r[:, t:t + 1], ACT.Sqrt).then_inc(o_rt, 1)

        @block.vector
        def _(dve):
            V = nc.vector
            for s in (cv, xe, gc, xd_s, sk, sc, xdd_s, pv, yy, ys):
                dve.sem_inc(s, LEAD)
            dve.sem_inc(ye, Y_LEAD)
            dve.sem_inc(d_ad, 4)

            dve.wait_ge(masks, 7)
            V.tensor_copy(after_r[:, :], after[:, :])
            def variance(u, t, n=1, between=None):
                dve.wait_ge(n_sq, NORM_T0[u] + t + n)
                s = slice(t, t + n)
                V.tensor_scalar(stat_v[:, s], stat[:, s], 1.0 / DM, EPS, ALU.mult, ALU.add).then_inc(n_var, 1)
                if between:
                    between()
                dve.wait_ge(n_var, 2 * (NORM_H0[u] + t) + 1)
                V.reciprocal(stat_r[:, s], stat_v[:, s]).then_inc(n_var, 1)

            def scale(u, t, src, dst):
                dve.wait_ge(n_rt, NORM_H0[u] + (0 if u == PRE_MEM_TOK else t) + 1)
                V.tensor_scalar(dst[:, t, :], src[:, t, :], stat_s[:, t:t + 1], None, ALU.mult).then_inc(n_xs, 1)

            def norm_low(u, gain0, q, hi=act_hi, lo=act_lo):
                per = min(4, NORM_TILES[u]) * P
                h, kt = q // KT, q % KT
                s = slice(h * per, (h + 1) * per)
                dve.wait_ge(n_hi, NORM_G0[u] + q + 1)
                V.scalar_tensor_tensor(out=lo[:, kt, s], in0=bank[norm_bank(u, q)][:, 0:per],
                                       scalar=consts[:, 3, gain0 + kt:gain0 + kt + 1], in1=hi[:, kt, s].bitcast(F32),
                                       op0=ALU.mult, op1=ALU.subtract).then_inc(n_lo, 1)

            def scale_x(t):
                variance(PRE_X, t)
                scale(PRE_X, t, x_tok, x_tok)
            for t in range(4):
                scale_x(t)
            for r, n in enumerate(ROW_COUNTS):
                dve.wait_ge(c_tr, 1)
                V.tensor_copy(consts[:, r, 0:n], bank[7][:, r * P:r * P + n]).then_inc(c_ev, 1)
            for q in range(16):
                if q % 2 == 0 and q < 8:
                    scale_x(4 + q // 2)
                norm_low(PRE_X, 0, q)
                if q == 0:
                    dve.wait_ge(dtw_in, 16)
                    V.tensor_copy(dtw_hi[:, :, :], dtw[:, :, :]).then_inc(dt_w, 1)
                    dve.wait_ge(dt_w, 1)
                    V.tensor_tensor(dtw_lo[:, :, :], dtw[:, :, :], dtw_hi[:, :, :].bitcast(F32), ALU.subtract).then_inc(dt_w, 1)
            dve.wait_ge(dt_in, 16 * 3)
            dve.wait_ge(dt_mm, 1)
            V.tensor_copy(dt_heads[:, 0:HALF], bank[0][0:HEADS, :]).then_inc(dt_cp, 1)
            dve.wait_ge(dt_mm, 2)
            V.tensor_copy(dt_heads[:, HALF:SEQ], bank[1][0:HEADS, :]).then_inc(dt_cp, 1)
            for h in range(2):
                dve.wait_ge(c_tr, 2 + h)
                V.tensor_tensor(ws_t[:, 4 * h:4 * h + 4, :], bank[3 + h][:, :].rearrange("p (g t) -> p g t", t=P),
                                tri[:, :].unsqueeze(1).to_broadcast([P, 4, P]), ALU.mult).then_inc(c_ev, 1)

            n = [0]

            def step(ins):
                n[0] += 1
                ins.then_inc(dt_dve, 1)
                dve.wait_ge(dt_dve, n[0])
            dve.wait_ge(dt_mm, 3)
            step(V.tensor_tensor(dt_x[:, :, :], bank[2][:, 0:NT * HEADS].rearrange("p (c h) -> p c h", h=HEADS),
                                 dt_bias[:, :].unsqueeze(1).to_broadcast([P, NT, HEADS]), ALU.add))
            dve.wait_ge(dt_act, 2)
            step(V.tensor_scalar(dt_d[:, :, :], dt_e[:, :, :], 2.0, None, ALU.add))
            step(V.reciprocal(dt_r[:, :, :], dt_d[:, :, :]))
            step(V.scalar_tensor_tensor(out=dt_s[:, :, :], in0=dt_e[:, :, :], scalar=2.0, in1=dt_r[:, :, :],
                                        op0=ALU.mult, op1=ALU.mult))
            step(V.scalar_tensor_tensor(out=dt_q[:, :, :], in0=dt_s[:, :, :], scalar=0.25, in1=dt_s[:, :, :],
                                        op0=ALU.mult, op1=ALU.mult))
            step(V.tensor_scalar(dt_p[:, :, :], dt_q[:, :, :], 1.0 / 13, None, ALU.mult))
            for c in (11, 9, 7, 5, 3):
                step(V.scalar_tensor_tensor(out=dt_p[:, :, :], in0=dt_p[:, :, :], scalar=1.0 / c, in1=dt_q[:, :, :],
                                            op0=ALU.add, op1=ALU.mult))
            step(V.scalar_tensor_tensor(out=dt_p[:, :, :], in0=dt_p[:, :, :], scalar=1.0, in1=dt_s[:, :, :],
                                        op0=ALU.add, op1=ALU.mult))
            step(V.scalar_tensor_tensor(out=dt[:, :, :], in0=dt_x[:, :, :], scalar=0.0, in1=dt_p[:, :, :],
                                        op0=ALU.max, op1=ALU.add))
            dve.wait_ge(dt_act, 3)
            step(V.scalar_tensor_tensor(out=dA[:, :, :], in0=dt[:, :, :], scalar=-1.0,
                                        in1=neg_a[:, :].unsqueeze(1).to_broadcast([P, NT, HEADS]),
                                        op0=ALU.mult, op1=ALU.mult))
            step(V.tensor_copy(dA_hi[:, :, :], dA[:, :, :]))
            step(V.tensor_tensor(dA_lo[:, :, :], dA[:, :, :], dA_hi[:, :, :].bitcast(F32), ALU.subtract))
            assert n[0] == 16

            dve.wait_ge(n_lo, NORM_G0[1])
            V.memset(xbc_raw[:, :, 0:CONV - 1], 0.0)

            def heads(ap):
                return ap.rearrange("p (r d) -> p r d", d=HD)

            def ssd_group(g):
                dve.wait_ge(ye, yth(g, 0))
                cv_c = consts[:, 0, 0:(CONV + 1) * XBC_TILES].rearrange("p (k j) -> p k j", j=XBC_TILES)
                for dst, src in ((g_conv[:, :, 0:XG], cv_c[:, :, bass.ds(g * XG, XG)]),
                                 (g_conv[:, :, XG:XG + 1], cv_c[:, :, bass.ds(g + 16, 1)]),
                                 (g_conv[:, :, XG + 1:XG + 2], cv_c[:, :, bass.ds(g + 20, 1)]),
                                 (g_gain[:, :], consts[:, 3, bass.ds(g * XG + 40, XG)]),
                                 (g_skip[:, :], d_skip[:, bass.ds(g * HPG, HPG)]),
                                 (g_dt[:, :, :], dt[:, :, bass.ds(g * HPG, HPG)]),
                                 (g_hi[:, :, :], dA_hi[:, :, bass.ds(g * HPG, HPG)].bitcast(F32)),
                                 (g_lo[:, :, :], dA_lo[:, :, bass.ds(g * HPG, HPG)]),
                                 (g_dA[:, :, :], dA[:, :, bass.ds(g * HPG, HPG)])):
                    V.tensor_copy(dst, src).then_inc(gc, 1)
                dve.wait_ge(gc, nth(g, GC, GC))

                def convolve(idx):
                    dve.wait_ge(t_ev, nth(g, 12, 2 * idx + 2))
                    if idx in (1, 2, 3, 4):
                        dve.wait_ge(xt, g * 10 + 2 * idx)
                    elif idx == 5:
                        dve.wait_ge(sl, nth(g, 6, 5))
                    V.tensor_scalar(conv[:, :], xbc_raw[:, idx % 2, CONV - 1:CONV - 1 + SEQ],
                                    g_conv[:, CONV - 1, idx:idx + 1], g_conv[:, CONV, idx:idx + 1],
                                    ALU.mult, ALU.add).then_inc(cv, 1)
                    for k in range(CONV - 1):
                        dve.wait_ge(cv, nth(g, 24, 4 * idx + k + 1))
                        V.scalar_tensor_tensor(out=conv[:, :], in0=xbc_raw[:, idx % 2, k:k + SEQ],
                                               scalar=g_conv[:, k, idx:idx + 1], in1=conv[:, :],
                                               op0=ALU.mult, op1=ALU.add).then_inc(cv, 1)

                def token_evac(idx):
                    for h in range(2):
                        q = 2 * idx + h
                        dve.wait_ge(xt, g * 10 + (q + 1))
                        src = bank[4 + q % 4][:, :].rearrange("p (c d) -> p c d", d=P)
                        dst = b_tok[:, 4 * h:4 * h + 4, :] if idx == XG else xs[:, 4 * h:4 * h + 4, idx * P:(idx + 1) * P]
                        V.tensor_copy(dst, src).then_inc(xe, 1)
                for idx in range(6):
                    convolve(idx)
                    if idx:
                        token_evac(idx - 1)
                dve.wait_ge(pv, nth(g, 17, 0))
                V.memset(state[:, :], 0.0).then_inc(pv, 1)

                def before_chunk(c):
                    if c >= 2:
                        dve.wait_ge(yd, nth(g, 8, c - 1))
                    if c == 0:
                        dve.wait_ge(xe, nth(g, 10, 8))
                    V.tensor_tensor(heads(xd[:, c % 2, :]), heads(xs[:, c, :]), bc(g_dt[:, c, :], [P, HPG, HD]),
                                    ALU.mult).then_inc(xd_s, 1)
                    dve.wait_ge(xd_s, nth(g, 8, c + 1))
                    V.tensor_tensor(heads(xs[:, c, :]), heads(xs[:, c, :]), bc(g_skip[:, :], [P, HPG, HD]),
                                    ALU.mult).then_inc(sk, 1)

                def score(c):
                    dve.wait_ge(cb, g * 8 + (c + 1))
                    V.tensor_tensor(cb_m[:, :], bank[3][:, 0:P], tri[:, :], ALU.mult).then_inc(sc, 1)
                    for h in range(2):
                        dve.wait_ge(ex, nth(g, 16, 2 * c + h + 1))
                        dve.wait_ge(sc, nth(g, 24, 3 * c + 1))
                        s = scores[:, h, :].rearrange("p (r l) -> p r l", l=P)
                        V.tensor_tensor(s, s, cb_m[:, :].unsqueeze(1).to_broadcast([P, 4, P]), ALU.mult).then_inc(sc, 1)
                    if c:
                        dve.wait_ge(st, g * 8 + c)
                    V.tensor_tensor(heads(xdd[:, :]), heads(xd[:, c % 2, :]), bc(g_out[:, c, :], [P, HPG, HD]),
                                    ALU.mult).then_inc(xdd_s, 1)

                def combine(c):
                    dve.wait_ge(yo, g * 8 + (c + 1))
                    V.tensor_tensor(heads(y_sum[:, :]), heads(bank[7][:, :]), bc(g_in[:, c, :], [P, HPG, HD]),
                                    ALU.mult).then_inc(yy, 1)
                    V.tensor_tensor(heads(state[:, :]), heads(state[:, :]), bc(g_chunk[:, c, :], [P, HPG, HD]),
                                    ALU.mult).then_inc(pv, 1)
                    dve.wait_ge(yy, nth(g, 32, 4 * c + 1))
                    V.tensor_tensor(y_sum[:, :], y_sum[:, :], bank[6][:, :], ALU.add).then_inc(yy, 1)
                    dve.wait_ge(st, g * 8 + (c + 1))
                    dve.wait_ge(pv, nth(g, 17, 2 * c + 2))
                    V.tensor_tensor(state[:, :], state[:, :], bank[2][:, :], ALU.add).then_inc(pv, 1)
                    dve.wait_ge(yy, nth(g, 32, 4 * c + 2))
                    V.tensor_tensor(xs[:, c, :], xs[:, c, :], y_sum[:, :], ALU.add).then_inc(yy, 1)
                    dve.wait_ge(yy, nth(g, 32, 4 * c + 3))
                    V.tensor_tensor(xs[:, c, :], xs[:, c, :], zs[:, c, :], ALU.mult).then_inc(yy, 1)

                before_chunk(0)
                for c in range(NT):
                    score(c)
                    if c + 1 < NT:
                        before_chunk(c + 1)
                    combine(c)
                dve.wait_ge(sq, nth(g, 8, 8))
                V.tensor_scalar(stat_v[:, :], stat[:, :], 1.0 / HALF, EPS, ALU.mult, ALU.add).then_inc(ysv, 1)
                dve.wait_ge(ysv, g * 2 + 1)
                V.reciprocal(stat_r[:, :], stat_v[:, :]).then_inc(ysv, 1)
                dve.wait_ge(ysr, g + 1)
                for c in range(NT):
                    V.tensor_scalar(xs[:, c, :], xs[:, c, :], stat_s[:, c:c + 1], None, ALU.mult).then_inc(ys, 1)
                for c in range(NT):
                    dve.wait_ge(yt, g * 8 + (c + 1))
                    V.tensor_tensor(y_half(c // 4)[:, :, c % 4, :], bank[c][:, :].rearrange("p (j t) -> p j t", t=P),
                                    bc(g_gain[:, :], [P, XG, P]), ALU.mult).then_inc(ye, 1)

            with dve.Fori(0, GROUPS) as g:
                ssd_group(g)

            def low(k):
                dve.wait_ge(b_hi, k + 1)
                V.tensor_tensor(split_part(k, act_lo), split_source(k), split_part(k, act_hi).bitcast(F32),
                                ALU.subtract).then_inc(b_lo, 1)

            for k in range(8):
                low(k)
            dve.wait_ge(v_sq, 8)
            V.tensor_scalar(stat_v[:, :], stat[:, :], 1.0 / DM, EPS, ALU.mult, ALU.add).then_inc(v_var, 1)
            dve.wait_ge(v_var, 1)
            V.reciprocal(stat_r[:, :], stat_v[:, :]).then_inc(v_var, 1)
            dve.wait_ge(v_rt, 1)
            for t in range(NT):
                V.tensor_scalar(r2[:, t, :], r2[:, t, :], stat_s[:, t:t + 1], None, ALU.mult).then_inc(v_sc, 1)
            dve.wait_ge(bs_in, 16)

            def mix(g):
                for h in range(2):
                    q = 2 * g + h
                    out_q = r2[:, 4 * h:4 * h + 4, g * P:(g + 1) * P]
                    dve.wait_ge(m_mm, q + 1)
                    V.scalar_tensor_tensor(out=out_q, in0=bank[4 + q % 4][:, :].rearrange("p (c t) -> p c t", t=P),
                                           scalar=consts[:, 3, 32 + g:33 + g],
                                           in1=bs_bc[:, g, :].unsqueeze(1).to_broadcast([P, 4, P]),
                                           op0=ALU.mult, op1=ALU.add).then_inc(m_ev, 1)
                    dve.wait_ge(gate_ld[g % 3], 16 * (g // 3 + 1))
                    dve.wait_ge(m_ev, 2 * q + 1)
                    V.tensor_tensor(out_q, out_q, gate_in[:, g % 3, h * HALF:(h + 1) * HALF].rearrange("p (c t) -> p c t", t=P),
                                    ALU.mult).then_inc(m_ev, 1)
            for g in range(6):
                mix(g)
            for k in range(8, 16):
                low(k)
            mix(6)
            for k in range(16, 24):
                low(k)
            mix(7)

            def kv_low(m):
                dve.wait_ge(kv_h, m + 1)
                V.tensor_tensor(kv_lo[:, m % 2, :], kv_raw[:, m % 2, :], kv_hi[:, m % 2, :].bitcast(F32),
                                ALU.subtract).then_inc(kv_l, 1)

            for q in range(32):
                j, h = q // 2 % 8, q % 2
                k = 8 + q // 2
                s = slice(h * HALF, (h + 1) * HALF)
                gate = gate_in[:, k % 3, s]
                dve.wait_ge(b_mm, 16 + q + 1)
                dve.wait_ge(gate_ld[k % 3], 16 * (k // 3 + 1))
                if q < 16:
                    dve.wait_ge(b_cp, q + 1)
                    V.tensor_tensor(r1[:, j, s], r1[:, j, s], bank[q % 4][:, :], ALU.add).then_inc(b_ev, 1)
                    dve.wait_ge(b_ev, 2 * q + 1)
                    V.tensor_tensor(r1[:, j, s], r1[:, j, s], gate, ALU.mult).then_inc(b_ev, 1)
                else:
                    dve.wait_ge(b_ev, 2 * q - 2)
                    V.tensor_tensor(g_tmp[:, h, :], bank[q % 4][:, :], gate, ALU.mult).then_inc(b_ev, 1)
                    dve.wait_ge(b_ev, 2 * q + 1)
                    V.tensor_tensor(r1[:, j, s], r1[:, j, s], g_tmp[:, h, :], ALU.add).then_inc(b_ev, 1)
                if q == 17:
                    variance(PRE_MEM_TOK, 0, 2)
                    for t in range(2):
                        scale(PRE_MEM_TOK, t, mem_tok, mem_tok)
                if q == 19:
                    for k in range(8):
                        norm_low(PRE_MEM_TOK, 24, k, mem_hi, mem_lo)
                    kv_low(0)
                    kv_low(1)
                if q % 2 and (q - 16) // 2 in KV_AFTER:
                    for m in KV_AFTER[(q - 16) // 2]:
                        if 2 <= m + 1 < KV_TILES:
                            kv_low(m + 1)
                if q in (14, 15, 30, 31):
                    first = 24 + 16 * (q // 16) + 8 * h
                    for i in range(first, first + 8):
                        low(i)

            def out_evac(u, n, t, gain):
                dve.wait_ge(o_sq, 16 * u + 8 * n + t + 1)
                s = slice(n * HALF, (n + 1) * HALF)
                V.tensor_tensor(r2[:, t, s], bank[t][:, :], gain[:, s], ALU.mult).then_inc(o_ev, 1)

            def first_stats(u):
                dve.wait_ge(o_sq, 16 * u + 8)
                V.tensor_scalar(stat_w[:, :], stat_n[:, :], 1.0 / DM, EPS, ALU.mult, ALU.add).then_inc(o_var, 1)

            def post_var(u, t, between):
                dve.wait_ge(o_sq, 16 * u + 8 + t + 1)
                dve.wait_ge(o_var, 17 * u + 2 * t + 1)
                V.scalar_tensor_tensor(out=stat_v[:, t:t + 1], in0=stat[:, t:t + 1], scalar=1.0 / DM,
                                       in1=stat_w[:, t:t + 1], op0=ALU.mult, op1=ALU.add).then_inc(o_var, 1)
                between()
                dve.wait_ge(o_var, 17 * u + 2 * t + 2)
                V.reciprocal(stat_r[:, t:t + 1], stat_v[:, t:t + 1]).then_inc(o_var, 1)

            def residual(u, t):
                dve.wait_ge(o_rt, 8 * u + t + 1)
                dve.wait_ge(o_ev, 16 * u + 8 + t + 1)
                V.scalar_tensor_tensor(out=r1[:, t, :], in0=r2[:, t, :], scalar=stat_s[:, t:t + 1], in1=r1[:, t, :],
                                       op0=ALU.mult, op1=ALU.add).then_inc(o_x, 1)

            def post_norm(u, gain):
                first_stats(u)
                for t in range(NT):
                    post_var(u, t, lambda: out_evac(u, 1, t, gain))
                    if t >= 2:
                        variance(NORMS[u], t - 2, between=lambda: residual(u, t - 1))
                    elif t:
                        residual(u, t - 1)
                    if t >= 3 and t % 2 == 0:
                        scale(NORMS[u], t - 3, r1, r2)

            dve.wait_ge(gain_in, 16)
            for t in range(NT):
                out_evac(0, 0, t, post_gain)
            dve.wait_ge(xr_in, 16)
            post_norm(0, post_gain)

            def norm_lows(u, gain0):
                residual(u, NT - 1)
                scale(NORMS[u], NT - 3, r1, r2)
                if u == 0:
                    for t in (NT - 2, NT - 1):
                        variance(NORMS[u], t)
                for q in range(16):
                    if q == 4:
                        scale(NORMS[u], NT - 1, r1, r2)
                    if u and q < 2:
                        variance(NORMS[u], NT - 2 + q)
                    norm_low(NORMS[u], gain0, q)
            norm_lows(0, 8)

            for h in range(XH):
                for b in range(4):
                    dve.wait_ge(s_mm, 4 * h + b + 1)
                    V.tensor_reduce(out=a_max[:, 2 * b:2 * b + 2], in_=bank[4 + b][:, :].rearrange("p (t m) -> p t m", m=MEM),
                                    axis=AX.X, op=ALU.max).then_inc(a_mx, 1)
                    if b % 2:
                        s = slice(2 * b - 2, 2 * b + 2)
                        dve.wait_ge(a_mx, 6 * h + (2 if b == 1 else 5))
                        V.tensor_scalar(a_nm[:, s], a_max[:, s], -(XHD ** -0.5), None, ALU.mult).then_inc(a_mx, 1)
                for half in range(2):
                    s = slice(4 * half, 4 * half + 4)
                    dve.wait_ge(a_ex, 8 * h + 4 * (half + 1))
                    V.reciprocal(a_rec[:, s], a_sum[:, s]).then_inc(a_pn, 1)
                    dve.wait_ge(a_pn, 10 * h + 5 * half + 1)
                    for t in range(4 * half, 4 * half + 4):
                        V.tensor_scalar(prob[:, t, :], prob[:, t, :], a_rec[:, t:t + 1], None, ALU.mult).then_inc(a_pn, 1)
                for i in range(4):
                    half, mt = i // 2, i % 2
                    dve.wait_ge(a_tr, 4 * h + i + 1)
                    V.tensor_copy(prob_t[:, mt, half * HALF:(half + 1) * HALF], bank[4 + i][:, :]).then_inc(a_te, 1)
            for kt in range(KT):
                dve.wait_ge(s_hi, kt + 1)
                V.tensor_tensor(act_lo[:, kt, :], r2[:, kt, :], act_hi[:, kt, :].bitcast(F32), ALU.subtract).then_inc(s_lo, 1)
            dve.wait_ge(gain_in, 32)
            for t in range(NT):
                out_evac(1, 0, t, post_gain2)
            post_norm(1, post_gain2)
            norm_lows(1, 16)

            V.memset(up_raw[:, :, 0:FFN_CONV - 1], 0.0)
            V.memset(r2[:, :, :], 0.0).then_inc(o_y, 1)

            def tap(k, col):
                r, off = ((1, 0), (1, 44), (2, 0), (2, 44))[k]
                return consts[:, r, bass.ds(col + off, 1)]

            def conv_step(u, col, i):
                w, k = i // 3, i % 3
                dst = (up_a, up_b)[w]
                c = col + w * FFN_TILES
                if k == 0:
                    dve.wait_ge(f_ev, 4 if isinstance(u, int) and u == 0 else u * 4 + (2 * w + 2))
                    if w == 0 and not (isinstance(u, int) and u == 0):
                        dve.wait_ge(f_l, u)
                    V.tensor_scalar(dst[:, :], up_raw[:, w, FFN_CONV - 1:FFN_CONV - 1 + SEQ], tap(2, c), tap(3, c),
                                    ALU.mult, ALU.add).then_inc(f_cv, 1)
                else:
                    dve.wait_ge(f_cv, u * 7 + i)
                    V.scalar_tensor_tensor(out=dst[:, :], in0=up_raw[:, w, k - 1:k - 1 + SEQ], scalar=tap(k - 1, c),
                                           in1=dst[:, :], op0=ALU.mult, op1=ALU.add).then_inc(f_cv, 1)

            def gate_pair(u):
                dve.wait_ge(f_gl, u + 1)
                dve.wait_ge(f_cv, u * 7 + 6)
                V.tensor_tensor(up_a[:, :], up_a[:, :], up_b[:, :], ALU.mult).then_inc(f_cv, 1)

            def low_pair(u, p):
                dve.wait_ge(f_h, u + 1)
                V.tensor_tensor(f_lo[:, p, :], up_a[:, :], f_hi[:, p, :].bitcast(F32), ALU.subtract).then_inc(f_l, 1)

            def add(step, r, n, t):
                dve.wait_ge(d_mm, step * 16 + (r + 1))
                dve.wait_ge(d_ad, step * 16 + (r + 3))
                s = r2[:, t, n * HALF:(n + 1) * HALF]
                V.tensor_tensor(s, s, bank[4 + r % 4][:, :], ALU.add).then_inc(d_ad, 1)

            def adds_and_pair(step, u):
                for r in range(16):
                    if r % 2 == 0 and r < 12:
                        conv_step(u, u, r // 2)
                    if r == 13:
                        gate_pair(u)
                    add(step, r, r // 8, r % 8)

            for u in range(2):
                for i in range(6):
                    conv_step(u, u, i)
                gate_pair(u)
                low_pair(u, u)
            dve.wait_ge(o_y, 1)
            with dve.Fori(1, FFN_STEPS - 1) as s:
                adds_and_pair(s - 1, s * 2)
                low_pair(s * 2, 0)
                for i in range(6):
                    conv_step(s * 2 + 1, s * 2 + 1, i)
                gate_pair(s * 2 + 1)
                low_pair(s * 2 + 1, 1)
            last = FFN_STEPS - 1
            for i in range(6):
                conv_step(2 * last, 2 * last, i)
            gate_pair(2 * last)
            low_pair(2 * last, 2)
            adds_and_pair(last - 1, 2 * last + 1)
            low_pair(2 * last + 1, 3)

            def last_norm(t):
                dve.wait_ge(o_rt, 16 + t + 1)
                V.scalar_tensor_tensor(out=r2[:, t, :], in0=r2[:, t, :], scalar=stat_s[:, t:t + 1], in1=post_gain3[:, :],
                                       op0=ALU.mult, op1=ALU.mult).then_inc(o_y, 1)
                if t >= POOL_ADDS:
                    dve.wait_ge(o_y, 1 + t + 1)
                    V.tensor_tensor(r1[:, t, :], r1[:, t, :], r2[:, t, :], ALU.add).then_inc(o_x, 1)

            def last_var(t):
                dve.wait_ge(o_sq, 32 + t + 1)
                V.tensor_scalar(stat_v[:, t:t + 1], stat[:, t:t + 1], 1.0 / DM, EPS, ALU.mult, ALU.add).then_inc(o_var, 1)
                dve.wait_ge(o_var, 34 + 2 * t + 1)
                V.reciprocal(stat_r[:, t:t + 1], stat_v[:, t:t + 1]).then_inc(o_var, 1)
            for r, (n, t) in enumerate(LAST_ORDER):
                add(last, r, n, t)
                if n and t == 2:
                    dve.wait_ge(gain_in, 48)
                if n and t >= 2:
                    last_norm(t - 2)
                if n and t:
                    last_var(t - 1)
            last_norm(NT - 2)
            last_var(NT - 1)
            last_norm(NT - 1)


ROW_COUNTS = [120, 88, 88, 56]
GAIN_ROWS = ["norm_pre_mix", "norm_pre_mem", "norm_pre_ffn", "norm_mem_kv", "gm_v_norm"]
ROW_LOADS = 5

_INS = ["x", "mem", "norm_pre_mix", "norm_post_mix", "norm_pre_mem", "norm_mem_kv", "norm_post_mem",
        "norm_pre_ffn", "norm_post_ffn", "w_in", "gm_v_norm", "gm_w_s", "gm_b_s", "ssd_conv_w", "ssd_conv_b",
        "ssd_dt_bias", "ssd_a_log", "ssd_d", "ssd_norm", "w_branch_a", "w_branch_b", "w_out",
        "xa_w_q", "xa_w_kv", "xa_w_o", "ffn_w_up", "ffn_conv_w", "ffn_conv_b", "ffn_w_down"]


def kernel(**inputs):
    import numpy as _np
    import concourse.bacc as _bacc
    from concourse import mybir as _mybir
    from concourse.bass_utils import run_bass_kernel_spmd as _run

    nc = _bacc.Bacc("TRN2", target_bir_lowering=False, num_devices=1)
    arrays, args = {}, {}
    for name in _INS:
        v = _np.ascontiguousarray(inputs[name])
        arrays[f"in_{name}"] = v
        args[name] = nc.dram_tensor(f"in_{name}", v.shape, _mybir.dt.from_np(v.dtype), kind="ExternalInput").ap()
    out = nc.dram_tensor("out_x", (1, SEQ, DM), _mybir.dt.float32, kind="ExternalOutput").ap()
    trunk(nc, args, out)
    r = _run(nc, [arrays], core_ids=[0])
    return r.results[0]["out_x"]
```
